# Optimizing a Trainium2 kernel written in Bass

```python
import math
import jax, jax.numpy as jnp
from jax import lax
import numpy as np

D_MODEL = 1024
BATCH = 1
SEQ = 512
DEPTH = 1

GRID_W = 64
MEM_LEN = 256
HEAD_DIM = 64
N_Q_HEADS = D_MODEL // HEAD_DIM
N_KV_HEADS = 4
GQA_GROUP = N_Q_HEADS // N_KV_HEADS
Q_WIDTH = N_Q_HEADS * HEAD_DIM
KV_WIDTH = N_KV_HEADS * HEAD_DIM
N_FOURIER_GROUPS = 4
FOURIER_GROUP_DIM = 128
FOURIER_WIDTH = N_FOURIER_GROUPS * FOURIER_GROUP_DIM
IN_WIDTH = Q_WIDTH + 2 * KV_WIDTH + FOURIER_WIDTH + 2 * D_MODEL
ROPE_AXIS_DIM = HEAD_DIM // 2
ROPE_THETA = 10000.0
Q_BLOCK = 128
N_CROSS_HEADS = 4
CROSS_HEAD_DIM = 64
CROSS_WIDTH = N_CROSS_HEADS * CROSS_HEAD_DIM
D_FF = 2816
RMS_EPS = 1e-6

kernel_name = "hybrid_fnet_axial_gqa_macaron_encoder"

def rmsnorm(x, g):
    xf = x.astype(jnp.float32)
    y = xf * lax.rsqrt(jnp.mean(xf * xf, axis=-1, keepdims=True) + RMS_EPS)
    return (y * g.astype(jnp.float32)).astype(x.dtype)

def swiglu(x, w_gate, w_up, w_down):
    return (jax.nn.silu(x @ w_gate) * (x @ w_up)) @ w_down

def axial_rope_tables(S, dtype):
    rows = S // GRID_W
    row = jnp.repeat(jnp.arange(rows, dtype=jnp.float32), GRID_W)
    col = jnp.tile(jnp.arange(GRID_W, dtype=jnp.float32), rows)
    inv = 1.0 / (ROPE_THETA ** (jnp.arange(0, ROPE_AXIS_DIM, 2, dtype=jnp.float32) / ROPE_AXIS_DIM))
    ang_r = row[:, None] * inv[None, :]
    ang_c = col[:, None] * inv[None, :]
    return (jnp.cos(ang_r).astype(dtype), jnp.sin(ang_r).astype(dtype),
            jnp.cos(ang_c).astype(dtype), jnp.sin(ang_c).astype(dtype))

def _rotate(x, cos, sin):
    S, F = cos.shape
    shape = (1, S) + (1,) * (x.ndim - 3) + (F,)
    c = cos.reshape(shape)
    s = sin.reshape(shape)
    x1, x2 = x[..., :F], x[..., F:]
    return jnp.concatenate([x1 * c - x2 * s, x2 * c + x1 * s], axis=-1)

def apply_axial_rope(x, tables):
    cr, sr, cc, sc = tables
    xr = _rotate(x[..., :ROPE_AXIS_DIM], cr, sr)
    xc = _rotate(x[..., ROPE_AXIS_DIM:], cc, sc)
    return jnp.concatenate([xr, xc], axis=-1)

def fourier_mixer(f):
    B, S, _ = f.shape
    fg = f.reshape(B, S, N_FOURIER_GROUPS, FOURIER_GROUP_DIM).astype(jnp.float32)
    y = jnp.real(jnp.fft.fft2(fg, axes=(1, 3), norm="ortho"))
    return y.reshape(B, S, FOURIER_WIDTH).astype(f.dtype)

def gqa_axial_attention(q, k, v, q_gain, k_gain, tables):
    B, S, _ = q.shape
    q = rmsnorm(q.reshape(B, S, N_KV_HEADS, GQA_GROUP, HEAD_DIM), q_gain)
    k = rmsnorm(k.reshape(B, S, N_KV_HEADS, HEAD_DIM), k_gain)
    v = v.reshape(B, S, N_KV_HEADS, HEAD_DIM)
    q = apply_axial_rope(q, tables)
    k = apply_axial_rope(k, tables)
    scale = 1.0 / math.sqrt(HEAD_DIM)
    nb = S // Q_BLOCK
    qb = q.reshape(B, nb, Q_BLOCK, N_KV_HEADS, GQA_GROUP, HEAD_DIM).transpose(1, 0, 2, 3, 4, 5)

    def attend(qblk):
        s = jnp.einsum('bqkgd,bskd->bkgqs', qblk, k).astype(jnp.float32) * scale
        p = jax.nn.softmax(s, axis=-1).astype(v.dtype)
        return jnp.einsum('bkgqs,bskd->bqkgd', p, v)

    o = lax.map(attend, qb)
    return o.transpose(1, 0, 2, 3, 4, 5).reshape(B, S, Q_WIDTH)

def memory_cross_attention(h_n, mem_n, w_cq, w_ck, w_cv, w_co):
    B, S, _ = h_n.shape
    M = mem_n.shape[1]
    q = (h_n @ w_cq).reshape(B, S, N_CROSS_HEADS, CROSS_HEAD_DIM)
    k = (mem_n @ w_ck).reshape(B, M, N_CROSS_HEADS, CROSS_HEAD_DIM)
    v = (mem_n @ w_cv).reshape(B, M, N_CROSS_HEADS, CROSS_HEAD_DIM)
    s = jnp.einsum('bshd,bmhd->bhsm', q, k).astype(jnp.float32) * (1.0 / math.sqrt(CROSS_HEAD_DIM))
    p = jax.nn.softmax(s, axis=-1).astype(v.dtype)
    o = jnp.einsum('bhsm,bmhd->bshd', p, v).reshape(B, S, CROSS_WIDTH)
    return o @ w_co

def setup_inputs(seed: int = 0) -> dict:
    key = jax.random.key(seed)
    ks = iter(jax.random.split(key, 32))
    f32 = jnp.float32

    def dense(shape):
        return jax.random.normal(next(ks), (DEPTH,) + shape, f32) * (shape[0] ** -0.5)

    def gain(shape):
        return 1.0 + 0.1 * jax.random.normal(next(ks), shape, f32)

    return {
        "x": jax.random.normal(next(ks), (BATCH, SEQ, D_MODEL), f32),
        "mem": jax.random.normal(next(ks), (BATCH, MEM_LEN, D_MODEL), f32),
        "g_ffn1": gain((DEPTH, D_MODEL)),
        "w1_gate": dense((D_MODEL, D_FF)),
        "w1_up": dense((D_MODEL, D_FF)),
        "w1_down": dense((D_FF, D_MODEL)),
        "g_mix": gain((DEPTH, D_MODEL)),
        "w_in": dense((D_MODEL, IN_WIDTH)),
        "q_gain": gain((DEPTH, HEAD_DIM)),
        "k_gain": gain((DEPTH, HEAD_DIM)),
        "w_fourier_branch": dense((FOURIER_WIDTH, D_MODEL)),
        "w_attn_branch": dense((Q_WIDTH, D_MODEL)),
        "w_out": dense((D_MODEL, D_MODEL)),
        "g_cross": gain((DEPTH, D_MODEL)),
        "g_mem": gain((DEPTH, D_MODEL)),
        "w_cq": dense((D_MODEL, CROSS_WIDTH)),
        "w_ck": dense((D_MODEL, CROSS_WIDTH)),
        "w_cv": dense((D_MODEL, CROSS_WIDTH)),
        "w_co": dense((CROSS_WIDTH, D_MODEL)),
        "g_ffn2": gain((DEPTH, D_MODEL)),
        "w2_gate": dense((D_MODEL, D_FF)),
        "w2_up": dense((D_MODEL, D_FF)),
        "w2_down": dense((D_FF, D_MODEL)),
        "g_final": gain((D_MODEL,)),
    }

def reference(x, mem, g_ffn1, w1_gate, w1_up, w1_down, g_mix, w_in, q_gain, k_gain,
              w_fourier_branch, w_attn_branch, w_out, g_cross, g_mem, w_cq, w_ck, w_cv,
              w_co, g_ffn2, w2_gate, w2_up, w2_down, g_final):
    S = x.shape[1]
    tables = axial_rope_tables(S, x.dtype)
    split_at = [Q_WIDTH, Q_WIDTH + KV_WIDTH, Q_WIDTH + 2 * KV_WIDTH,
                Q_WIDTH + 2 * KV_WIDTH + FOURIER_WIDTH,
                Q_WIDTH + 2 * KV_WIDTH + FOURIER_WIDTH + D_MODEL]
    h = x
    for l in range(DEPTH):
        h = h + 0.5 * swiglu(rmsnorm(h, g_ffn1[l]), w1_gate[l], w1_up[l], w1_down[l])

        n = rmsnorm(h, g_mix[l])
        p = n @ w_in[l]
        q, k, v, f, gate_f, gate_a = jnp.split(p, split_at, axis=-1)
        y_f = fourier_mixer(f) @ w_fourier_branch[l]
        y_a = gqa_axial_attention(q, k, v, q_gain[l], k_gain[l], tables) @ w_attn_branch[l]
        merged = jax.nn.sigmoid(gate_f) * y_f + jax.nn.sigmoid(gate_a) * y_a
        h = h + merged @ w_out[l]

        h = h + memory_cross_attention(rmsnorm(h, g_cross[l]), rmsnorm(mem, g_mem[l]),
                                       w_cq[l], w_ck[l], w_cv[l], w_co[l])

        h = h + 0.5 * swiglu(rmsnorm(h, g_ffn2[l]), w2_gate[l], w2_up[l], w2_down[l])
    return rmsnorm(h, g_final)


_drawn_inputs = setup_inputs


def setup_inputs(seed=0):
    import zlib

    import numpy as np

    out = dict(_drawn_inputs(seed))
    spreads = {}
    factors = {'q_gain': 8.0, 'k_gain': 8.0, 'g_cross': 5.5, 'g_mem': 3.931, 'g_ffn2': 5.153}
    for name, (base, spread) in spreads.items():
        noise = np.random.default_rng([zlib.crc32(name.encode()), seed]).standard_normal(out[name].shape)
        drawn = base * np.exp(spread * noise) if base else spread * noise
        out[name] = __import__('jax').numpy.asarray(drawn.astype(out[name].dtype))
    for name, factor in factors.items():
        out[name] = (out[name] * factor).astype(out[name].dtype)
    return out
```

```python
from contextlib import ExitStack

import numpy as np

import concourse.bass as bass
from concourse import mybir

ACT = mybir.ActivationFunctionType
ALU = mybir.AluOpType
AX = mybir.AxisListType
F32 = mybir.dt.float32
F32R = mybir.dt.float32r

P = 128
TOKENS = 512
D_MODEL = 1024
D_TILES = D_MODEL // P
MEM_LEN = 256
HEAD_DIM = 64
N_HEADS = 16
N_KV = 4
N_CROSS = 4
D_FF = 2816
FF_TILES = D_FF // P
FF_PAIRS = FF_TILES // 2
PAIRS = D_TILES // 2
GROUPS = 4
EPS = 1e-6
SCALE = HEAD_DIM ** -0.5
COLS = 2 * P
CHUNK = D_TILES * COLS
DOWN_SPLIT = (6, 6, 5, 5)
DOWN_FIRST = (0, 6, 12, 17)
BRANCH_K = (4, 8, 8, 8)

C_FFN1 = 0
C_DOWN1 = C_FFN1 + 2 * FF_PAIRS
C_IN = C_DOWN1 + 4 * PAIRS
C_MEM = C_IN + 8
C_DFT = C_MEM + 2
C_BRANCH = C_DFT + 2
C_OUT = C_BRANCH + 4 * PAIRS
C_CROSS = C_OUT + PAIRS
C_FFN2 = C_CROSS + 2
C_DOWN2 = C_FFN2 + 2 * FF_PAIRS
N_CHUNKS = C_DOWN2 + 4 * PAIRS

KIB = 1024


def encoder_block(nc, xT, memT, stream, gains, head_gains, rope, channel_dft, identity, outT):
    with ExitStack() as ctx:
        base = -(-nc.sbuf_base // 32) * 32

        def at(name, shape, kib, dt=F32):
            return nc.alloc_sbuf_tensor_at(name, shape, dt, offset=base + int(kib * KIB))

        def sem(name):
            return ctx.enter_context(nc.semaphore(name))

        def psum(name):
            return ctx.enter_context(nc.psum_tensor(name, [P, 2, TOKENS], F32))

        h = at("h", [P, D_TILES, TOKENS], 0)
        raw = [at(f"raw{b}", [P, CHUNK], 16 + 8 * b) for b in range(2)]
        w_hi = [at(f"w_hi{b}", [P, CHUNK], 32 + 8 * b, F32R) for b in range(2)]
        w_lo = [at(f"w_lo{b}", [P, CHUNK], 48 + 8 * b, F32R) for b in range(2)]
        row_factor = at("row_factor", [P, TOKENS], 64)
        square_sum = at("square_sum", [P, TOKENS], 66)
        SM = 68
        ident = at("ident", [P, P], SM)
        ones = at("ones", [P, P], SM + .5, F32R)
        head_ones = at("head_ones", [P, P], SM + 1, F32R)
        pick_hi = at("pick_hi", [P, P], SM + 1.5, F32R)
        pick_lo = at("pick_lo", [P, P], SM + 2, F32R)
        gain = at("gain", [P, 6, D_TILES], SM + 2.5)
        head_gain = at("head_gain", [P, 8], SM + 2.75)
        ch_raw = at("ch_raw", [P, 2 * P], SM + 3)
        ch_hi = at("ch_hi", [P, 2 * P], SM + 4, F32R)
        ch_lo = at("ch_lo", [P, 2 * P], SM + 5, F32R)
        row_max = at("row_max", [P, 2, 4], SM + 6)
        max_hi = at("max_hi", [P, 2, 4], SM + 6.0625, F32R)
        max_lo = at("max_lo", [P, 2, 4], SM + 6.125, F32R)
        T = SM + 6.25
        total_hi = at("total_hi", [P, TOKENS], T, F32R)
        total_lo = at("total_lo", [P, TOKENS], T + 2, F32R)
        mean_sq = at("mean_sq", [P, TOKENS], T + 4)
        rsq = at("rsq", [P, TOKENS], T + 6)
        newton = at("newton", [P, TOKENS], T + 8)
        squares = [at(f"squares{b}", [P, TOKENS], T + 8 + 2 * b) for b in range(2)]
        gate_t = at("gate_t", [P, 2, TOKENS], T)
        silu_t = at("silu_t", [P, 2, TOKENS], T + 4)
        up_t = at("up_t", [P, 2, TOKENS], T + 8)
        V = T + 12
        x_hi = at("x_hi", [P, D_TILES, TOKENS], V, F32R)
        x_lo = at("x_lo", [P, D_TILES, TOKENS], V + 16, F32R)
        ff_hi = at("ff_hi", [P, FF_TILES, TOKENS], V + 32, F32R)
        ff_lo = at("ff_lo", [P, FF_TILES, TOKENS], V + 76, F32R)
        kq = at("kq", [P, 10, TOKENS], V + 32)
        v_t = at("v_t", [P, 2, TOKENS], V + 52)
        f_t = at("f_t", [P, GROUPS, TOKENS], V + 56)
        f_lo = at("f_lo", [P, GROUPS, TOKENS], V + 56, F32R)
        mem = at("mem", [P, D_TILES, MEM_LEN], V + 64)
        f_hi = at("f_hi", [P, GROUPS, TOKENS], V + 64, F32R)
        mem_sq = at("mem_sq", [P, D_TILES, MEM_LEN], V + 72)
        mem_hi = at("mem_hi", [P, D_TILES, MEM_LEN], V + 72, F32R)
        mem_lo = at("mem_lo", [P, D_TILES, MEM_LEN], V + 80, F32R)
        cross_k = at("cross_k", [P, 2, MEM_LEN], V + 52)
        cross_v = at("cross_v", [P, 2, MEM_LEN], V + 54)
        v_tok = at("v_tok", [P, 4, N_KV * HEAD_DIM], V + 88)
        rope_cos = at("rope_cos", [P, TOKENS], V + 96)
        rope_sin = at("rope_sin", [P, TOKENS], V + 98)
        hsq = at("hsq", [P, 2, TOKENS], V + 100)
        hsq_hi = at("hsq_hi", [P, 2, TOKENS], V + 104, F32R)
        hsq_lo = at("hsq_lo", [P, 2, TOKENS], V + 108, F32R)
        hmean = at("hmean", [P, 2, TOKENS], V + 112)
        hrsq = at("hrsq", [P, 2, TOKENS], V + 116)
        hnewton = at("hnewton", [P, 2, TOKENS], T)
        shuffled = at("shuffled", [P, 2, TOKENS], T + 4)
        rotated = at("rotated", [P, 2, TOKENS], T + 8)
        msum = at("msum", [P, MEM_LEN], T + 4)
        msum_hi = at("msum_hi", [P, MEM_LEN], T + 5, F32R)
        msum_lo = at("msum_lo", [P, MEM_LEN], T + 6, F32R)
        mmean = at("mmean", [P, MEM_LEN], T + 7)
        mrsq = at("mrsq", [P, MEM_LEN], T + 8)
        mnewton = at("mnewton", [P, MEM_LEN], T + 9)
        y_hi = at("y_hi", [P, 4, 2 * TOKENS], V, F32R)
        y_lo = at("y_lo", [P, 4, 2 * TOKENS], V + 16, F32R)
        a_hi = at("a_hi", [P, GROUPS, TOKENS], V + 72, F32R)
        a_lo = at("a_lo", [P, GROUPS, TOKENS], V + 80, F32R)
        p_hi = [at(f"p_hi{b}", [P, 4, TOKENS], V + 8 * b, F32R) for b in range(2)]
        p_lo = [at(f"p_lo{b}", [P, 4, TOKENS], V + 16 + 8 * b, F32R) for b in range(2)]
        p_main = at("p_main", [P, 4, TOKENS], V + 56)
        p_cross = at("p_cross", [P, 4, TOKENS], V + 72)
        diag_hi = at("diag_hi", [P, 4, P], V + 64, F32R)
        diag_lo = at("diag_lo", [P, 4, P], V + 66, F32R)
        q_at = (V + 68, V + 92, V + 116, T)
        q1 = [at(f"q1_{b}", [P, TOKENS], q_at[b], F32R) for b in range(4)]
        q2 = [at(f"q2_{b}", [P, TOKENS], q_at[b] + 2, F32R) for b in range(4)]

        def kv_buffer(tag, kib, keys):
            v_shape = [P, keys // P, 3 * HEAD_DIM]
            v_kib = keys // P * 0.75
            return (at(f"k1_{tag}", [P, keys], kib, F32R), at(f"k2_{tag}", [P, keys], kib + keys / 256, F32R),
                    at(f"v_hi_{tag}", v_shape, kib + keys / 128, F32R),
                    at(f"v_lo_{tag}", v_shape, kib + keys / 128 + v_kib, F32R))

        kv_main = [kv_buffer(f"m{b}", V + 96 + 10 * b, TOKENS) for b in range(2)]
        kv_cross = [kv_buffer(f"c{b}", V + 96 + 5 * b, MEM_LEN) for b in range(N_CROSS)]
        denom = at("denom", [P, TOKENS], T + 4)
        cross_q = at("cross_q", [P, 2, TOKENS], V + 56)
        cross_o = at("cross_o", [P, 2, TOKENS], V + 60)
        co_hi = at("co_hi", [P, 2, TOKENS], V + 80, F32R)
        co_lo = at("co_lo", [P, 2, TOKENS], V + 84, F32R)
        o_hi = at("o_hi", [P, D_TILES, TOKENS], V + 56, F32R)
        o_lo = at("o_lo", [P, D_TILES, TOKENS], V + 88, F32R)
        m_hi = at("m_hi", [P, D_TILES, TOKENS], V + 32, F32R)
        m_lo = at("m_lo", [P, D_TILES, TOKENS], V + 104, F32R)
        gf_t = at("gf_t", [P, 2, TOKENS], T)
        ga_t = at("ga_t", [P, 2, TOKENS], T + 4)
        merged_t = at("merged_t", [P, 2, TOKENS], T + 8)
        final_t = at("final_t", [P, D_TILES, TOKENS], V)

        ps_a, ps_b, ps_c, ps_d = (psum(f"ps_{c}") for c in "abcd")
        stat = ps_d[:, 1, :]

        x_loaded = [sem(f"x_loaded{i}") for i in range(PAIRS)]
        consts_loaded = sem("consts_loaded")
        mix_loaded = sem("mix_loaded")
        stored = sem("stored")
        consts_set = sem("consts_set")
        ch_hi_made, ch_lo_made = sem("ch_hi_made"), sem("ch_lo_made")
        raw_loaded = [sem(f"raw_loaded{b}") for b in range(2)]
        w_hi_made = sem("w_hi_made")
        w_lo_made = sem("w_lo_made")
        chunk_used = sem("chunk_used")

        FREE = 1

        def sems(tag, *steps):
            return {step: sem(f"{tag}_{step}") for step in steps}

        norm_sems = sems("norm", "h_new0", "h_new1", "tile0", "x_hi", "squared", "x_lo", "summed", "total_hi",
                         "total_lo", "stat", "mean", "root", "newton", "factor")
        norm_adds = {"h_new0": PAIRS, "h_new1": PAIRS, "tile0": PAIRS, "x_hi": D_TILES, "squared": D_TILES,
                     "x_lo": D_TILES, "summed": D_TILES + 1, "newton": 4}

        class Norm:
            def __init__(self, earlier, earlier_updates, earlier_tile0):
                self.before = {step: norm_adds.get(step, 1) * earlier for step in norm_sems}
                self.before["h_new0"] = self.before["h_new1"] = PAIRS * earlier_updates + FREE
                self.before["tile0"] = PAIRS * earlier_tile0

            def __getitem__(self, step):
                return norm_sems[step]

            def at(self, step, value):
                return norm_sems[step], value + self.before[step]

        norms = {"ffn1": Norm(0, 0, 0), "mix": Norm(1, 0, 0), "cross": Norm(2, 1, 1), "ffn2": Norm(3, 2, 2),
                 "final": Norm(4, 3, 2)}
        ffns = {tag: sems(tag, "gate_out", "silu", "up_out", "product", "ff_hi", "ff_lo")
                for tag in ("ffn1", "ffn2")}
        pr = sems("proj", "out", "v_turned", "v_tok", "y_full", "y_hi", "f_hi", "f_lo", "a_hi", "a_lo")
        hd = sems("head", "sq", "sq_hi", "sq_lo", "stat", "mean", "root", "recip", "y_sq", "t_mul", "t_aff",
                  "factor", "scaled", "shuffled", "mul", "roped")
        mm = sems("mem", "squared", "sum", "sum_hi", "sum_lo", "stat", "mean", "root", "newton", "factor",
                  "normed", "hi", "lo")
        br = sems("branch", "o_hi", "o_lo", "x_hi", "x_lo", "gf_out", "ga_out", "sig_f", "sig_a", "yf", "ya",
                  "merged", "m_hi", "m_lo")
        cr = sems("cr", "q_out", "co_hi", "co_lo", "co_tile")
        out_ready = sem("out_ready")

        def wide(ap, n=2):
            return ap.unsqueeze(1).to_broadcast([P, n, ap.shape[1]])

        def wait_apart(engine, semaphore, value):
            engine.wait_ge(semaphore, value)
            engine.wait_ge(semaphore, 1)

        def convert_hi(act, b, q, cols=CHUNK, first=False):
            act.wait_ge(raw_loaded[b], 16 * q + 16)
            if not first:
                act.wait_ge(chunk_used, 2 * q + b - 1)
            nc.scalar.activation(w_hi[b][:, 0:cols], raw[b][:, 0:cols], ACT.Copy).then_inc(w_hi_made, 1)

        def convert_lo(dve, b, q, cols=CHUNK):
            dve.wait_ge(w_hi_made, 2 * q + b + 1)
            nc.vector.tensor_tensor(w_lo[b][:, 0:cols], raw[b][:, 0:cols],
                                    w_hi[b][:, 0:cols].bitcast(F32), ALU.subtract).then_inc(w_lo_made, 1)

        def product(out, w, x, start, stop):
            nc.tensor.matmul(out, w[0], x[0], start=start, stop=False)
            nc.tensor.matmul(out, w[0], x[1], start=False, stop=False)
            return nc.tensor.matmul(out, w[1], x[0], start=False, stop=stop)

        def weight(b, k, m, cols=COLS):
            s = slice(k * cols + m * P, k * cols + (m + 1) * P)
            return w_hi[b][:, s], w_lo[b][:, s]

        def part(pair, k, cols=slice(None)):
            return pair[0][:, k, cols], pair[1][:, k, cols]

        x_parts = (x_hi, x_lo)
        pipes = (ps_a, ps_b)

        class Attention:
            def __init__(self, tag, heads, keys, q_tiles, out_tiles, k_tiles, v_rows, buffers, per_kv, p_raw):
                self.heads, self.keys, self.key_tiles = heads, keys, keys // P
                self.q_tiles, self.out_tiles, self.k_tiles, self.v_rows = q_tiles, out_tiles, k_tiles, v_rows
                self.buffers, self.per_kv, self.p_raw = buffers, per_kv, p_raw
                self.s = sems(tag, "consts", "k_hi", "k_all", "v_hi", "v_all", "q_hi", "q_lo", "s_full",
                              "row_max", "max_hi", "max_lo", "diag", "shift", "shift_in", "st_full", "p", "p_hi",
                              "p_lo", "pv", "denom", "o")

            def kv(self, i):
                return self.buffers[i // self.per_kv % len(self.buffers)]

            def half(self, i):
                return slice(HEAD_DIM * (i % 2), HEAD_DIM * (i % 2) + HEAD_DIM)

        main = Attention("main", N_HEADS, TOKENS, kq[:, 2:10, :], kq[:, 2:10, :], kq[:, 0:2, :], v_tok[:, :, :],
                         kv_main, N_HEADS // N_KV, p_main)
        cross = Attention("crossatt", N_CROSS, MEM_LEN, cross_q[:, :, :], cross_o[:, :, :], cross_k[:, :, :],
                          cross_v[:, :, :], kv_cross, 1, p_cross)
        LOW, HIGH = slice(0, HEAD_DIM), slice(HEAD_DIM, P)
        score_banks = [ps_a[:, 0, :], ps_a[:, 1, :]]
        st_banks = [ps_b[:, 0, :], ps_b[:, 1, :], ps_c[:, 0, :], ps_c[:, 1, :]]
        pv_bank, shift_bank = ps_d[:, 0, :], ps_d[:, 1, :]

        def st_bank(at_, i, kt):
            return st_banks[kt if at_.key_tiles == 4 else 2 * (i % 2) + kt]

        block = ctx.enter_context(nc.Block())

        @block.sync
        def _(sp):
            def load(b, q, cols=CHUNK, first=False):
                if not first:
                    sp.wait_ge(w_lo_made, 2 * q + b - 1)
                sp.dma_start(raw[b][:, 0:cols], stream[2 * q + b, :, 0:cols]).then_inc(raw_loaded[b], 16)

            def ffn_stream(c0):
                with sp.Fori(1, FF_PAIRS + 1) as j:
                    for b in range(2):
                        load(b, c0 // 2 + j)
                down = (c0 + 2 * FF_PAIRS) // 2
                for i in (2, 3):
                    load(i % 2, down + 1, DOWN_SPLIT[i] * COLS)
                with sp.Fori(1, PAIRS) as p:
                    for i in range(4):
                        load(i % 2, down + 2 * p + i // 2, DOWN_SPLIT[i] * COLS)

            for b in range(2):
                load(b, 0, first=True)
            ffn_stream(C_FFN1)
            with sp.Fori(C_IN // 2, C_BRANCH // 2) as q:
                for b in range(2):
                    load(b, q)
            with sp.Fori(0, PAIRS) as m:
                for i in range(4):
                    load(i % 2, C_BRANCH // 2 + 2 * m + i // 2, BRANCH_K[i] * COLS)
            with sp.Fori(C_OUT // 2, C_FFN2 // 2 + 1) as q:
                for b in range(2):
                    load(b, q)
            ffn_stream(C_FFN2)
            for p in range(PAIRS):
                sp.wait_ge(out_ready, 2 * p + 2)
                sp.dma_start(outT[:, 2 * p:2 * p + 2, :], final_t[:, 2 * p:2 * p + 2, :]).then_inc(stored, 16)
            sp.wait_ge(stored, 16 * PAIRS)

        @block.gpsimd
        def _(pool):
            def fill_all(semaphore, fills):
                for n, (out, value) in enumerate(fills):
                    if n:
                        pool.wait_ge(semaphore, n)
                    nc.gpsimd.memset(out.bitcast(F32), value).then_inc(semaphore, 1)

            fill_all(consts_set, [(head_ones[:, :], 0.0), (pick_hi[:, :], 0.0), (pick_lo[:, :], 0.0),
                                  (ones[:, :], 1.0), (head_ones[LOW, LOW], 1.0), (head_ones[HIGH, HIGH], 1.0),
                                  (pick_hi[:, 64:96], 1.0), (pick_lo[:, 96:128], 1.0)])

            pool.wait_ge(mix_loaded, 48)
            with pool.Fori(0, 5) as s:
                pool.wait_ge(hd["shuffled"], s + 1)
                nc.gpsimd.tensor_tensor(shuffled[:, :, :], shuffled[:, :, :], wide(rope_sin[:, :]), ALU.mult)\
                    .then_inc(hd["mul"], 1)
                nc.gpsimd.tensor_tensor(rotated[:, :, :], hrsq[:, :, :], wide(rope_cos[:, :]), ALU.mult)\
                    .then_inc(hd["mul"], 1)
                wait_apart(pool, hd["mul"], 2 * s + 2)
                nc.gpsimd.tensor_tensor(kq[:, bass.ds(2 * s, 2), :], shuffled[:, :, :], rotated[:, :, :], ALU.add)\
                    .then_inc(hd["roped"], 1)

            def constants(at_):
                fill_all(at_.s["consts"], [fill for k1, k2, v1, v2 in at_.buffers for fill in (
                    (k2[HIGH, :], 0.0), (k2[64:65, :], 1.0), (k2[96:97, :], 1.0),
                    (v1[:, :, HIGH], 1.0), (v2[:, :, HIGH], 0.0))])

            def low_parts(at_):
                for i in range(at_.heads):
                    for kt in range(at_.key_tiles):
                        pool.wait_ge(at_.s["p_hi"], at_.key_tiles * i + kt + 1)
                        nc.gpsimd.tensor_tensor(p_lo[i % 2][:, kt, :], at_.p_raw[:, kt, :],
                                                p_hi[i % 2][:, kt, :].bitcast(F32), ALU.subtract)\
                            .then_inc(at_.s["p_lo"], 1)

            pool.wait_ge(hd["roped"], 5)
            constants(main)
            low_parts(main)
            pool.wait_ge(chunk_used, C_OUT + PAIRS)
            constants(cross)
            low_parts(cross)

        @block.scalar
        def _(act):
            def copy(out, in_, scale=1.0):
                return nc.scalar.activation(out, in_, ACT.Copy, scale=scale)

            def refresh(n, gain_row, d, m, ready, split=True):
                act.wait_ge(*ready)
                if split:
                    copy(x_hi[:, d, :], h[:, d, :], gain[:, gain_row, d:d + 1]).then_inc(n["x_hi"], 1)
                act.wait_ge(*n.at("summed", d))
                nc.scalar.activation(squares[m][:, :], h[:, d, :], ACT.Square).then_inc(n["squared"], 1)

            def total(n):
                act.wait_ge(*n.at("summed", D_TILES + 1))
                copy(total_hi[:, :], square_sum[:, :]).then_inc(n["total_hi"], 1)

            def root(n):
                act.wait_ge(*n.at("mean", 1))
                nc.scalar.activation(rsq[:, :], mean_sq[:, :], ACT.Sqrt).then_inc(n["root"], 1)

            def feed_forward(tag, c0, j):
                f = ffns[tag]
                convert_hi(act, 0, c0 // 2 + j + 1)
                act.wait_ge(f["gate_out"], j + 1)
                nc.scalar.activation(silu_t[:, :, :], gate_t[:, :, :], ACT.Silu).then_inc(f["silu"], 1)
                convert_hi(act, 1, c0 // 2 + j + 1)
                wait_apart(act, f["product"], j + 1)
                copy(ff_hi[:, bass.ds(2 * j, 2), :], up_t[:, :, :]).then_inc(f["ff_hi"], 1)

            def down(n, gain_row, c0, p, last, end):
                for i in range(3 if not (end and last) else 2):
                    cols = (DOWN_SPLIT[(i + 2) % 4] * COLS) if not (last and i >= 2) else CHUNK
                    convert_hi(act, i % 2, c0 // 2 + 2 * p + i // 2 + 1, cols)
                for m in range(2):
                    refresh(n, gain_row, 2 * p + m, m, n.at(f"h_new{m}", p + 1), split=not end)
                if not (end and last):
                    convert_hi(act, 1, c0 // 2 + 2 * p + 2, CHUNK if last else DOWN_SPLIT[1] * COLS)

            def ffn(tag, nxt, c0, gain_row, end):
                n = norms[tag]
                total(n)
                root(n)
                feed_forward(tag, c0, 0)
                with act.Fori(1, FF_PAIRS) as j:
                    feed_forward(tag, c0, j)
                down0 = c0 + 2 * FF_PAIRS
                for p in range(PAIRS):
                    down(norms[nxt], gain_row, down0, p, p == PAIRS - 1, end)

            act.dma_start(gain[:, :, :], gains).then_inc(consts_loaded, 16)
            act.dma_start(head_gain[:, :], head_gains).then_inc(consts_loaded, 16)
            for p in range(PAIRS):
                act.dma_start(h[:, 2 * p:2 * p + 2, :], xT[:, 2 * p:2 * p + 2, :]).then_inc(x_loaded[p], 16)
            act.dma_start(ident[:, :], identity).then_inc(consts_loaded, 16)
            act.dma_start(ch_raw[:, :], channel_dft).then_inc(consts_loaded, 16)
            act.wait_ge(consts_loaded, 64)
            for d in range(D_TILES):
                refresh(norms["ffn1"], 0, d, d % 2, (x_loaded[d // 2], 16))
            convert_hi(act, 0, 0, first=True)
            convert_hi(act, 1, 0, first=True)
            ffn("ffn1", "mix", C_FFN1, 1, False)

            n = norms["mix"]
            act.wait_ge(chunk_used, C_IN)
            act.dma_start(mem[:, :, :], memT).then_inc(mix_loaded, 16)
            act.dma_start(rope_cos[:, :], rope[0]).then_inc(mix_loaded, 16)
            act.dma_start(rope_sin[:, :], rope[1]).then_inc(mix_loaded, 16)
            total(n)
            root(n)

            def square_heads(s):
                nc.scalar.activation(hsq[:, :, :], kq[:, bass.ds(2 * s, 2), :], ACT.Square).then_inc(hd["sq"], 1)
                act.wait_ge(hd["sq"], s + 1)
                copy(hsq_hi[:, :, :], hsq[:, :, :]).then_inc(hd["sq_hi"], 1)

            def head_root(s):
                act.wait_ge(hd["mean"], s + 1 + FREE)
                act.wait_ge(hd["mul"], 2 * s)
                nc.scalar.activation(hrsq[:, :, :], hmean[:, :, :], ACT.Sqrt).then_inc(hd["root"], 1)
                act.wait_ge(hd["recip"], s + 1)
                nc.scalar.activation(hnewton[:, :, :], hrsq[:, :, :], ACT.Square).then_inc(hd["y_sq"], 1)
                act.wait_ge(hd["t_mul"], s + 1)
                nc.scalar.activation(hnewton[:, :, :], hnewton[:, :, :], ACT.Copy, bias=1.5, scale=-0.5)\
                    .then_inc(hd["t_aff"], 1)

            act.wait_ge(mix_loaded, 48)
            nc.scalar.activation(mem_sq[:, :, :], mem[:, :, :], ACT.Square).then_inc(mm["squared"], 1)
            copy(ch_hi[:, :], ch_raw[:, :]).then_inc(ch_hi_made, 1)
            q0 = C_IN // 2
            convert_hi(act, 0, q0 + 1)
            act.wait_ge(pr["out"], 1)
            square_heads(0)
            convert_hi(act, 1, q0 + 1)
            act.wait_ge(mm["sum"], 1)
            copy(msum_hi[:, :], msum[:, :]).then_inc(mm["sum_hi"], 1)
            convert_hi(act, 0, q0 + 2)
            convert_hi(act, 1, q0 + 2)
            act.wait_ge(mm["mean"], 1)
            nc.scalar.activation(mrsq[:, :], mmean[:, :], ACT.Sqrt).then_inc(mm["root"], 1)
            act.wait_ge(mm["normed"], 1)
            for k in range(D_TILES):
                copy(mem_hi[:, k, :], mem[:, k, :], gain[:, 5, k:k + 1]).then_inc(mm["hi"], 1)
            for t in range(2):
                for b in range(2):
                    s = 2 * t + b
                    convert_hi(act, b, q0 + 3 + t)
                    head_root(s)
                    act.wait_ge(pr["out"], 5 + s)
                    act.wait_ge(hd["stat"], s + 1)
                    square_heads(s + 1)
            act.wait_ge(mm["lo"], D_TILES)
            copy(f_hi[:, :, :], f_t[:, :, :]).then_inc(pr["f_hi"], 1)
            convert_hi(act, 0, q0 + 5)
            head_root(4)
            convert_hi(act, 1, q0 + 5)
            for tt in range(4):
                act.wait_ge(pr["y_full"], tt + 1)
                copy(y_hi[:, tt, :], pipes[tt % 2].rearrange("p a b -> p (a b)")).then_inc(pr["y_hi"], 1)
            convert_hi(act, 0, C_BRANCH // 2, BRANCH_K[0] * COLS)
            convert_hi(act, 1, C_BRANCH // 2)
            for half in range(2):
                copy(a_hi[:, 2 * half:2 * half + 2, :], pipes[half][:, :, :]).then_inc(pr["a_hi"], 1)

            def kv_high(at_, g):
                e = at_.half(g)
                k1, k2, v1, v2 = at_.buffers[g % len(at_.buffers)]
                source = at_.k_tiles[e, g // 2, :]
                if g >= len(at_.buffers):
                    act.wait_ge(at_.s["pv"], at_.per_kv * (g - 1))
                copy(k1[LOW, :], source).then_inc(at_.s["k_hi"], 1)
                copy(k1[HIGH, :], source).then_inc(at_.s["k_hi"], 1)
                copy(k2[LOW, :], source).then_inc(at_.s["k_hi"], 1)
                values = at_.v_rows[:, :, HEAD_DIM * g:HEAD_DIM * (g + 1)]
                copy(v1[:, :, LOW], values).then_inc(at_.s["v_hi"], 1)
                copy(v1[:, :, 2 * HEAD_DIM:], values).then_inc(at_.s["v_hi"], 1)

            def q_high(at_, i):
                source = at_.q_tiles[at_.half(i), i // 2, :]
                if i >= 4:
                    act.wait_ge(at_.s["st_full"], at_.key_tiles * (i - 3))
                copy(q1[i % 4][LOW, :], source).then_inc(at_.s["q_hi"], 1)
                copy(q1[i % 4][HIGH, :], source).then_inc(at_.s["q_hi"], 1)

            def shift_in(at_, i):
                act.wait_ge(at_.s["shift"], i + 1)
                copy(q2[i % 4][HIGH, :], shift_bank[HIGH, :]).then_inc(at_.s["shift_in"], 1)

            def exponentials(at_, i):
                n_kt = at_.key_tiles
                for kt in range(n_kt):
                    act.wait_ge(at_.s["st_full"], n_kt * i + kt + 1)
                    if i >= 1:
                        act.wait_ge(at_.s["p_lo"], n_kt * (i - 1) + kt + 1)
                    nc.scalar.activation(at_.p_raw[:, kt, :], st_bank(at_, i, kt), ACT.Exp, scale=SCALE)\
                        .then_inc(at_.s["p"], 1)

            def attention(at_):
                for g in range(1 if at_ is main else N_CROSS):
                    kv_high(at_, g)
                for i in range(3):
                    q_high(at_, i)
                shift_in(at_, 0)
                for i in range(at_.heads):
                    exponentials(at_, i)
                    if i + 1 < at_.heads:
                        shift_in(at_, i + 1)
                    if i + 3 < at_.heads:
                        q_high(at_, i + 3)
                    if at_ is main and i % 4 == 1 and i // 4 + 1 < N_KV:
                        kv_high(at_, i // 4 + 1)

            act.wait_ge(hd["roped"], 5)
            act.wait_ge(pr["v_tok"], 1)
            attention(main)

            act.wait_ge(main.s["o"], N_HEADS)
            for half in range(2):
                s = slice(4 * half, 4 * half + 4)
                copy(o_hi[:, s, :], main.out_tiles[:, s, :]).then_inc(br["o_hi"], 1)
            for k in range(D_TILES):
                copy(x_hi[:, k, :], h[:, k, :], gain[:, 1, k:k + 1]).then_inc(br["x_hi"], 1)

            def branch(m, last):
                q = C_BRANCH // 2 + 2 * m
                convert_hi(act, 0, q + 1)
                convert_hi(act, 1, q + 1)
                act.wait_ge(br["gf_out"], m + 1 + FREE)
                nc.scalar.activation(gf_t[:, :, :], gf_t[:, :, :], ACT.Sigmoid).then_inc(br["sig_f"], 1)
                convert_hi(act, 0, q + 2, CHUNK if last else BRANCH_K[0] * COLS)
                act.wait_ge(br["ga_out"], m + 1 + FREE)
                nc.scalar.activation(ga_t[:, :, :], ga_t[:, :, :], ACT.Sigmoid).then_inc(br["sig_a"], 1)
                convert_hi(act, 1, q + 2)
                wait_apart(act, br["merged"], m + 1)
                copy(m_hi[:, bass.ds(2 * m, 2), :], merged_t[:, :, :]).then_inc(br["m_hi"], 1)

            with act.Fori(0, PAIRS - 1) as m:
                branch(m, False)
            branch(PAIRS - 1, True)

            n = norms["cross"]
            for t in range(2):
                for b in range(2):
                    for m in range(2):
                        refresh(n, 2, 2 * (2 * t + b) + m, m, n.at(f"h_new{m}", 2 * t + b + 1))
                    convert_hi(act, b, C_OUT // 2 + t + 1)

            total(n)
            root(n)
            convert_hi(act, 0, C_CROSS // 2 + 1)
            act.wait_ge(cr["q_out"], 1)
            attention(cross)
            act.wait_ge(cross.s["o"], N_CROSS)
            copy(co_hi[:, :, :], cross_o[:, :, :]).then_inc(cr["co_hi"], 1)
            n = norms["ffn2"]
            for p in range(PAIRS):
                for m in range(2):
                    refresh(n, 3, 2 * p + m, m, n.at(f"h_new{m}", p + 1))
            convert_hi(act, 1, C_CROSS // 2 + 1)
            ffn("ffn2", "final", C_FFN2, 4, True)
            total(norms["final"])
            root(norms["final"])

        @block.vector
        def _(dve):
            def tt(out, a, b, op):
                return nc.vector.tensor_tensor(out, a, b, op)

            def minus(out, a, hi):
                return tt(out, a, hi.bitcast(F32), ALU.subtract)

            def clear(n):
                nc.vector.memset(square_sum[:, :], 0.0).then_inc(n["summed"], 1)

            def refresh(n, gain_row, d, m, split=True):
                if split:
                    dve.wait_ge(*n.at("x_hi", d + 1))
                    nc.vector.scalar_tensor_tensor(x_lo[:, d, :], h[:, d, :], gain[:, gain_row, bass.ds(d, 1)],
                                                   x_hi[:, d, :].bitcast(F32), ALU.mult, ALU.subtract)\
                        .then_inc(n["x_lo"], 1)
                dve.wait_ge(*n.at("squared", d + 1))
                dve.wait_ge(*n.at("summed", d + 1))
                tt(square_sum[:, :], square_sum[:, :], squares[m][:, :], ALU.add).then_inc(n["summed"], 1)

            def residual(n, d, m, bank, factor):
                nc.vector.scalar_tensor_tensor(h[:, d, :], bank, factor, h[:, d, :], ALU.mult, ALU.add)\
                    .then_inc(n[f"h_new{m}"], 1)

            def inverse_root(y, mean, t, out, root, newton, factor, before=0):
                dve.wait_ge(root, before + 1)
                nc.vector.reciprocal(y, y).then_inc(newton, 1)
                dve.wait_ge(newton, 4 * before + 1)
                tt(t, y, y, ALU.mult).then_inc(newton, 1)
                dve.wait_ge(newton, 4 * before + 2)
                tt(t, t, mean, ALU.mult).then_inc(newton, 1)
                dve.wait_ge(newton, 4 * before + 3)
                nc.vector.tensor_scalar(t, t, -0.5, 1.5, ALU.mult, ALU.add).then_inc(newton, 1)
                dve.wait_ge(newton, 4 * before + 4)
                tt(out, y, t, ALU.mult).then_inc(factor, 1)
                dve.wait_ge(factor, before + 1)

            def total(n):
                dve.wait_ge(*n.at("total_hi", 1))
                minus(total_lo[:, :], square_sum[:, :], total_hi[:, :]).then_inc(n["total_lo"], 1)

            def factor(n):
                dve.wait_ge(*n.at("stat", 1))
                nc.vector.tensor_scalar(mean_sq[:, :], stat, 1.0 / D_MODEL, EPS, ALU.mult, ALU.add)\
                    .then_inc(n["mean"], 1)
                inverse_root(rsq[:, :], mean_sq[:, :], newton[:, :], row_factor[:, :], n["root"], n["newton"],
                             n["factor"], n.before["root"])

            rf = wide(row_factor[:, :])

            def feed_forward(tag, c0, j):
                f = ffns[tag]
                dve.wait_ge(chunk_used, c0 + 2 * j + 1)
                tt(gate_t[:, :, :], ps_a[:, :, :], rf, ALU.mult).then_inc(f["gate_out"], 1)
                convert_lo(dve, 0, c0 // 2 + j + 1)
                dve.wait_ge(chunk_used, c0 + 2 * j + 2)
                dve.wait_ge(f["ff_lo"], j)
                tt(up_t[:, :, :], ps_b[:, :, :], rf, ALU.mult).then_inc(f["up_out"], 1)
                dve.wait_ge(f["silu"], j + 1)
                dve.wait_ge(f["up_out"], j + 1)
                tt(up_t[:, :, :], up_t[:, :, :], silu_t[:, :, :], ALU.mult).then_inc(f["product"], 1)
                convert_lo(dve, 1, c0 // 2 + j + 1)
                dve.wait_ge(f["ff_hi"], j + 1)
                two = bass.ds(2 * j, 2)
                minus(ff_lo[:, two, :], up_t[:, :, :], ff_hi[:, two, :]).then_inc(f["ff_lo"], 1)

            def down(n, gain_row, c0, p, last, end):
                for i in range(3 if not (end and last) else 2):
                    cols = (DOWN_SPLIT[(i + 2) % 4] * COLS) if not (last and i >= 2) else CHUNK
                    convert_lo(dve, i % 2, c0 // 2 + 2 * p + i // 2 + 1, cols)
                dve.wait_ge(*n.at("tile0", p + 1))
                residual(n, 2 * p, 0, ps_c[:, 0, :], 0.5)
                dve.wait_ge(chunk_used, c0 + 4 * p + 4)
                residual(n, 2 * p + 1, 1, ps_c[:, 1, :], 0.5)
                for m in range(2):
                    refresh(n, gain_row, 2 * p + m, m, split=not end)
                if not (end and last):
                    convert_lo(dve, 1, c0 // 2 + 2 * p + 2, CHUNK if last else DOWN_SPLIT[1] * COLS)

            def ffn(tag, nxt, c0, gain_row, end):
                total(norms[tag])
                factor(norms[tag])
                feed_forward(tag, c0, 0)
                with dve.Fori(1, FF_PAIRS) as j:
                    feed_forward(tag, c0, j)
                n = norms[nxt]
                clear(n)
                down0 = c0 + 2 * FF_PAIRS
                with dve.Fori(0, PAIRS - 1) as p:
                    down(n, gain_row, down0, p, False, end)
                down(n, gain_row, down0, PAIRS - 1, True, end)

            clear(norms["ffn1"])
            dve.wait_ge(consts_loaded, 64)
            for d in range(D_TILES):
                refresh(norms["ffn1"], 0, d, d % 2)
            convert_lo(dve, 0, 0)
            convert_lo(dve, 1, 0)
            ffn("ffn1", "mix", C_FFN1, 1, False)

            q0 = C_IN // 2
            n = norms["mix"]
            total(n)
            factor(n)

            def project_out(u, b, out):
                dve.wait_ge(chunk_used, C_IN + u + 1)
                tt(out, pipes[b][:, :, :], rf, ALU.mult).then_inc(pr["out"], 1)

            def square_low(s):
                dve.wait_ge(hd["sq_hi"], s + 1)
                minus(hsq_lo[:, :, :], hsq[:, :, :], hsq_hi[:, :, :]).then_inc(hd["sq_lo"], 1)

            def norm_heads(s):
                dve.wait_ge(hd["stat"], s + 1)
                nc.vector.tensor_scalar(hmean[:, :, :], ps_c[:, :, :], 1.0 / HEAD_DIM, EPS, ALU.mult, ALU.add)\
                    .then_inc(hd["mean"], 1)
                dve.wait_ge(hd["root"], s + 1)
                nc.vector.reciprocal(hrsq[:, :, :], hrsq[:, :, :]).then_inc(hd["recip"], 1)
                dve.wait_ge(hd["y_sq"], s + 1)
                tt(hnewton[:, :, :], hnewton[:, :, :], hmean[:, :, :], ALU.mult).then_inc(hd["t_mul"], 1)
                dve.wait_ge(hd["t_aff"], s + 1)
                tt(hrsq[:, :, :], hrsq[:, :, :], hnewton[:, :, :], ALU.mult).then_inc(hd["factor"], 1)
                dve.wait_ge(hd["factor"], s + 1)
                nc.vector.scalar_tensor_tensor(hrsq[:, :, :], kq[:, bass.ds(2 * s, 2), :], head_gain[:, bass.ds(s, 1)], hrsq[:, :, :],
                                               ALU.mult, ALU.mult).then_inc(hd["scaled"], 1)
                dve.wait_ge(hd["roped"], s)
                dve.wait_ge(hd["scaled"], s + 1)
                nc.vector.stream_shuffle(shuffled[:, :, :], hrsq[:, :, :], [(i + 16) % 32 for i in range(32)])\
                    .then_inc(hd["shuffled"], 1)

            project_out(0, 0, kq[:, 0:2, :])
            convert_lo(dve, 0, q0 + 1)
            square_low(0)
            project_out(1, 1, v_t[:, :, :])
            convert_lo(dve, 1, q0 + 1)
            dve.wait_ge(mm["squared"], 1)
            nc.vector.tensor_reduce(msum[:, :], mem_sq[:, :, :].rearrange("p k t -> p t k"), AX.X, ALU.add)\
                .then_inc(mm["sum"], 1)
            dve.wait_ge(ch_hi_made, 1)
            minus(ch_lo[:, :], ch_raw[:, :], ch_hi[:, :]).then_inc(ch_lo_made, 1)
            project_out(2, 0, f_t[:, 0:2, :])
            convert_lo(dve, 0, q0 + 2)
            dve.wait_ge(mm["sum_hi"], 1)
            minus(msum_lo[:, :], msum[:, :], msum_hi[:, :]).then_inc(mm["sum_lo"], 1)
            dve.wait_ge(pr["v_turned"], 1)
            nc.vector.tensor_copy(v_tok[:, :, :].rearrange("p a b -> p (a b)"),
                                  ps_d[:, :, :].rearrange("p a b -> p (a b)")).then_inc(pr["v_tok"], 1)
            project_out(3, 1, f_t[:, 2:4, :])
            convert_lo(dve, 1, q0 + 2)
            dve.wait_ge(mm["stat"], 1)
            nc.vector.tensor_scalar(mmean[:, :], stat[:, 0:MEM_LEN], 1.0 / D_MODEL, EPS, ALU.mult, ALU.add)\
                .then_inc(mm["mean"], 1)
            inverse_root(mrsq[:, :], mmean[:, :], mnewton[:, :], mrsq[:, :], mm["root"], mm["newton"], mm["factor"])
            tt(mem[:, :, :], mem[:, :, :], wide(mrsq[:, :], D_TILES), ALU.mult).then_inc(mm["normed"], 1)
            for k in range(D_TILES):
                dve.wait_ge(mm["hi"], k + 1)
                nc.vector.scalar_tensor_tensor(mem_lo[:, k, :], mem[:, k, :], gain[:, 5, k:k + 1],
                                               mem_hi[:, k, :].bitcast(F32), ALU.mult, ALU.subtract)\
                    .then_inc(mm["lo"], 1)
            for t in range(2):
                for b in range(2):
                    s = 2 * t + b
                    project_out(4 + s, b, kq[:, bass.ds(2 * s + 2, 2), :])
                    convert_lo(dve, b, q0 + 3 + t)
                    norm_heads(s)
                    square_low(s + 1)
            dve.wait_ge(pr["f_hi"], 1)
            minus(f_lo[:, :, :], f_t[:, :, :], f_hi[:, :, :]).then_inc(pr["f_lo"], 1)
            dve.wait_ge(chunk_used, C_MEM + 1)
            nc.vector.tensor_copy(cross_k[:, :, :], ps_a[:, :, 0:MEM_LEN]).then_inc(pr["out"], 1)
            convert_lo(dve, 0, q0 + 5)
            norm_heads(4)
            dve.wait_ge(chunk_used, C_MEM + 2)
            nc.vector.tensor_copy(cross_v[:, :, :], ps_b[:, :, 0:MEM_LEN]).then_inc(pr["out"], 1)
            convert_lo(dve, 1, q0 + 5)
            for tt_ in range(4):
                dve.wait_ge(pr["y_hi"], tt_ + 1)
                minus(y_lo[:, tt_, :], pipes[tt_ % 2].rearrange("p a b -> p (a b)"), y_hi[:, tt_, :])\
                    .then_inc(pr["out"], 1)
            convert_lo(dve, 0, C_BRANCH // 2, BRANCH_K[0] * COLS)
            convert_lo(dve, 1, C_BRANCH // 2)
            for half in range(2):
                dve.wait_ge(pr["a_hi"], half + 1)
                s = slice(2 * half, 2 * half + 2)
                minus(a_lo[:, s, :], pipes[half][:, :, :], a_hi[:, s, :]).then_inc(pr["a_lo"], 1)

            def kv_low(at_, g):
                e = at_.half(g)
                k1, k2, v1, v2 = at_.buffers[g % len(at_.buffers)]
                dve.wait_ge(at_.s["k_hi"], 3 * (g + 1))
                minus(k1[HIGH, :], at_.k_tiles[e, g // 2, :], k1[e, :]).then_inc(at_.s["k_all"], 1)
                dve.wait_ge(at_.s["v_hi"], 2 * (g + 1))
                values = at_.v_rows[:, :, HEAD_DIM * g:HEAD_DIM * (g + 1)]
                minus(v2[:, :, LOW], values, v1[:, :, LOW]).then_inc(at_.s["v_all"], 1)
                minus(v2[:, :, 2 * HEAD_DIM:], values, v1[:, :, LOW]).then_inc(at_.s["v_all"], 1)

            def q_low(at_, i):
                e = at_.half(i)
                dve.wait_ge(at_.s["q_hi"], 2 * (i + 1))
                minus(q2[i % 4][LOW, :], at_.q_tiles[e, i // 2, :], q1[i % 4][e, :]).then_inc(at_.s["q_lo"], 1)

            def shifts(at_, i):
                b = i % 2
                for qt in range(4):
                    dve.wait_ge(at_.s["s_full"], 4 * i + qt + 1)
                    nc.vector.tensor_reduce(row_max[:, b, qt:qt + 1], score_banks[qt % 2][:, 0:at_.keys],
                                            AX.X, ALU.max).then_inc(at_.s["row_max"], 1)
                dve.wait_ge(at_.s["row_max"], 4 * i + 4)
                nc.vector.tensor_scalar(max_hi[:, b, :], row_max[:, b, :], -1.0, None, ALU.mult)\
                    .then_inc(at_.s["max_hi"], 1)
                dve.wait_ge(at_.s["max_hi"], i + 1)
                nc.vector.scalar_tensor_tensor(max_lo[:, b, :], row_max[:, b, :], -1.0,
                                               max_hi[:, b, :].bitcast(F32), ALU.mult, ALU.subtract)\
                    .then_inc(at_.s["max_lo"], 1)
                dve.wait_ge(at_.s["max_lo"], i + 1)
                if i >= 1:
                    dve.wait_ge(at_.s["shift"], i)
                for diag, values in ((diag_hi, max_hi), (diag_lo, max_lo)):
                    tt(diag[:, :, :], wide(ident[:, :], 4),
                       values[:, b, :].bitcast(F32).unsqueeze(2).to_broadcast([P, 4, P]), ALU.mult)\
                        .then_inc(at_.s["diag"], 1)

            def probabilities(at_, i):
                n_kt = at_.key_tiles
                if i >= 2:
                    dve.wait_ge(at_.s["pv"], i - 1)
                for kt in range(n_kt):
                    dve.wait_ge(at_.s["p"], n_kt * i + kt + 1)
                    nc.vector.tensor_copy(p_hi[i % 2][:, kt, :], at_.p_raw[:, kt, :]).then_inc(at_.s["p_hi"], 1)

            def normalize(at_, i):
                e, other = at_.half(i), at_.half(i + 1)
                dve.wait_ge(at_.s["pv"], i + 1)
                nc.vector.reciprocal(denom[e, :], pv_bank[other, :]).then_inc(at_.s["denom"], 1)
                dve.wait_ge(at_.s["denom"], i + 1)
                tt(at_.out_tiles[e, i // 2, :], pv_bank[e, :], denom[e, :], ALU.mult).then_inc(at_.s["o"], 1)

            def attention(at_):
                for g in range(1 if at_ is main else N_CROSS):
                    kv_low(at_, g)
                for i in range(3):
                    q_low(at_, i)
                shifts(at_, 0)
                shifts(at_, 1)
                for i in range(at_.heads):
                    if i >= 2:
                        normalize(at_, i - 2)
                    probabilities(at_, i)
                    if i + 2 < at_.heads:
                        shifts(at_, i + 2)
                    if i + 3 < at_.heads:
                        q_low(at_, i + 3)
                    if at_ is main and i % 4 == 1 and i // 4 + 1 < N_KV:
                        kv_low(at_, i // 4 + 1)
                normalize(at_, at_.heads - 2)
                normalize(at_, at_.heads - 1)

            attention(main)

            for half in range(2):
                s = slice(4 * half, 4 * half + 4)
                dve.wait_ge(br["o_hi"], half + 1)
                minus(o_lo[:, s, :], main.out_tiles[:, s, :], o_hi[:, s, :]).then_inc(br["o_lo"], 1)
            for k in range(D_TILES):
                dve.wait_ge(br["x_hi"], k + 1)
                nc.vector.scalar_tensor_tensor(x_lo[:, k, :], h[:, k, :], gain[:, 1, k:k + 1],
                                               x_hi[:, k, :].bitcast(F32), ALU.mult, ALU.subtract)\
                    .then_inc(br["x_lo"], 1)

            def branch(m, last):
                q = C_BRANCH // 2 + 2 * m
                convert_lo(dve, 0, q + 1)
                convert_lo(dve, 1, q + 1)
                dve.wait_ge(chunk_used, 2 * q + 3)
                tt(gf_t[:, :, :], ps_a[:, :, :], rf, ALU.mult).then_inc(br["gf_out"], 1)
                convert_lo(dve, 0, q + 2, CHUNK if last else BRANCH_K[0] * COLS)
                dve.wait_ge(br["sig_f"], m + 1)
                tt(gf_t[:, :, :], ps_d[:, :, :], gf_t[:, :, :], ALU.mult).then_inc(br["yf"], 1)
                dve.wait_ge(chunk_used, 2 * q + 4)
                tt(ga_t[:, :, :], ps_b[:, :, :], rf, ALU.mult).then_inc(br["ga_out"], 1)
                convert_lo(dve, 1, q + 2)
                dve.wait_ge(br["sig_a"], m + 1)
                tt(ga_t[:, :, :], ps_c[:, :, :], ga_t[:, :, :], ALU.mult).then_inc(br["ya"], 1)
                dve.wait_ge(br["yf"], m + 1 + FREE)
                dve.wait_ge(br["ya"], m + 1 + FREE)
                tt(merged_t[:, :, :], gf_t[:, :, :], ga_t[:, :, :], ALU.add).then_inc(br["merged"], 1)
                dve.wait_ge(br["m_hi"], m + 1)
                two = bass.ds(2 * m, 2)
                minus(m_lo[:, two, :], merged_t[:, :, :], m_hi[:, two, :]).then_inc(br["m_lo"], 1)

            with dve.Fori(0, PAIRS - 1) as m:
                branch(m, False)
            branch(PAIRS - 1, True)

            n = norms["cross"]
            clear(n)
            with dve.Fori(0, 2) as t:
                for b in range(2):
                    p = 2 * t + b
                    dve.wait_ge(*n.at("tile0", p + 1))
                    residual(n, 2 * p, 0, ps_c[:, 0, :], 1.0)
                    dve.wait_ge(chunk_used, C_OUT + p + 1)
                    residual(n, 2 * p + 1, 1, ps_c[:, 1, :], 1.0)
                    for m in range(2):
                        refresh(n, 2, 2 * p + m, m)
                    convert_lo(dve, b, C_OUT // 2 + t + 1)

            total(n)
            factor(n)
            dve.wait_ge(chunk_used, C_CROSS + 1)
            tt(cross_q[:, :, :], ps_a[:, :, :], rf, ALU.mult).then_inc(cr["q_out"], 1)
            convert_lo(dve, 0, C_CROSS // 2 + 1)
            dve.wait_ge(cr["q_out"], 1)
            attention(cross)
            dve.wait_ge(cr["co_hi"], 1)
            minus(co_lo[:, :, :], cross_o[:, :, :], co_hi[:, :, :]).then_inc(cr["co_lo"], 1)
            n = norms["ffn2"]
            clear(n)
            with dve.Fori(0, PAIRS) as p:
                for m in range(2):
                    dve.wait_ge(cr["co_tile"], 2 * p + m + 1)
                    residual(n, 2 * p + m, m, ps_c[:, m, :], 1.0)
                    refresh(n, 3, 2 * p + m, m)
            convert_lo(dve, 1, C_CROSS // 2 + 1)
            ffn("ffn2", "final", C_FFN2, 4, True)
            n = norms["final"]
            total(n)
            factor(n)
            for d in range(D_TILES):
                nc.vector.scalar_tensor_tensor(final_t[:, d, :], h[:, d, :], gain[:, 4, d:d + 1],
                                               row_factor[:, :], ALU.mult, ALU.mult).then_inc(out_ready, 1)

        @block.tensor
        def _(pe):
            def sum_rows(n):
                pe.wait_ge(*n.at("total_lo", 1))
                nc.tensor.matmul(stat, ones[:, :], total_hi[:, :], start=True, stop=False)
                nc.tensor.matmul(stat, ones[:, :], total_lo[:, :], start=False, stop=True).then_inc(n["stat"], 1)

            def project(b, out, chunk, n=None):
                pe.wait_ge(w_lo_made, chunk + 1)
                for m in range(2):
                    for k in range(D_TILES):
                        if n is not None and m == 0:
                            pe.wait_ge(*n.at("x_lo", k + 1))
                        last = product(out[:, m, :], weight(b, k, m), part(x_parts, k), k == 0, k == D_TILES - 1)
                    if n is not None and m == 0:
                        sum_rows(n)
                last.then_inc(chunk_used, 1)

            def ffn(tag, nxt, c0):
                f, n = ffns[tag], norms[nxt]
                project(0, ps_a, c0, norms[tag])
                project(1, ps_b, c0 + 1)
                with pe.Fori(1, FF_PAIRS) as j:
                    pe.wait_ge(f["gate_out"], j)
                    project(0, ps_a, c0 + 2 * j)
                    pe.wait_ge(f["up_out"], j)
                    project(1, ps_b, c0 + 2 * j + 1)
                down0 = c0 + 2 * FF_PAIRS
                with pe.Fori(0, PAIRS) as p:
                    for i in range(4):
                        pe.wait_ge(w_lo_made, down0 + 4 * p + i + 1)
                        pe.wait_ge(f["ff_lo"], FF_PAIRS - (i < 3))
                        for m in range(2):
                            if i == 0:
                                pe.wait_ge(*n.at(f"h_new{m}", p))
                            for k in range(DOWN_SPLIT[i]):
                                kt = DOWN_FIRST[i] + k
                                last = product(ps_c[:, m, :], weight(i % 2, k, m), part((ff_hi, ff_lo), kt),
                                               kt == 0, kt == FF_TILES - 1)
                            if i == 3 and m == 0:
                                last.then_inc(n["tile0"], 1)
                        last.then_inc(chunk_used, 1)

            for reader in (norm_sems["h_new0"], norm_sems["h_new1"], hd["mean"], br["yf"], br["ya"], br["gf_out"],
                           br["ga_out"]):
                pe.sem_inc(reader, FREE)
            pe.wait_ge(consts_set, 8)
            ffn("ffn1", "mix", C_FFN1)

            def head_sums(s):
                pe.wait_ge(hd["sq_lo"], s + 1)
                pe.wait_ge(hd["mean"], s + FREE)
                for m in range(2):
                    nc.tensor.matmul(ps_c[:, m, :], head_ones[:, :], hsq_hi[:, m, :], start=True, stop=False)
                    last = nc.tensor.matmul(ps_c[:, m, :], head_ones[:, :], hsq_lo[:, m, :], start=False, stop=True)
                last.then_inc(hd["stat"], 1)

            project(0, ps_a, C_IN, norms["mix"])
            project(1, ps_b, C_IN + 1)
            pe.wait_ge(pr["out"], 1)
            project(0, ps_a, C_IN + 2)
            pe.wait_ge(consts_loaded, 64)
            pe.wait_ge(pr["out"], 2)
            for kt in range(4):
                for m in range(2):
                    last = nc.tensor.transpose(ps_d[:, kt // 2, (kt % 2) * COLS + m * P:(kt % 2) * COLS + (m + 1) * P],
                                               v_t[:, m, kt * P:(kt + 1) * P], ident[:, :])
            last.then_inc(pr["v_turned"], 1)
            project(1, ps_b, C_IN + 3)
            pe.wait_ge(mm["sum_lo"], 1)
            pe.wait_ge(pr["v_tok"], 1)
            nc.tensor.matmul(stat[:, 0:MEM_LEN], ones[:, :], msum_hi[:, :], start=True, stop=False)
            nc.tensor.matmul(stat[:, 0:MEM_LEN], ones[:, :], msum_lo[:, :], start=False, stop=True)\
                .then_inc(mm["stat"], 1)
            with pe.Fori(0, 2) as t:
                for b in range(2):
                    s = 2 * t + b
                    pe.wait_ge(pr["out"], 3 + s)
                    project(b, pipes[b], C_IN + 4 + s)
                    head_sums(s)
            pe.wait_ge(mm["lo"], D_TILES)
            pe.wait_ge(pr["out"], 7)
            pe.wait_ge(w_lo_made, C_MEM + 1)
            for m in range(2):
                for k in range(D_TILES):
                    last = product(ps_a[:, m, 0:MEM_LEN], weight(0, k, m), part((mem_hi, mem_lo), k),
                                   k == 0, k == D_TILES - 1)
            last.then_inc(chunk_used, 1)
            head_sums(4)
            pe.wait_ge(pr["out"], 8)
            pe.wait_ge(w_lo_made, C_MEM + 2)
            for mt in range(2):
                for k in range(D_TILES):
                    s = slice(k * COLS, (k + 1) * COLS)
                    last = product(ps_b[:, mt, 0:COLS], part((mem_hi, mem_lo), k, slice(mt * P, (mt + 1) * P)),
                                   (w_hi[1][:, s], w_lo[1][:, s]), k == 0, k == D_TILES - 1)
            last.then_inc(chunk_used, 1)

            pe.wait_ge(ch_lo_made, 1)
            pe.wait_ge(pr["f_lo"], 1)
            for tt_ in range(4):
                pe.wait_ge(pr["out"], 9 + tt_)
                for g in range(GROUPS):
                    last = product(pipes[tt_ % 2][:, g // 2, (g % 2) * COLS:(g % 2 + 1) * COLS],
                                   part((f_hi, f_lo), g, slice(tt_ * P, (tt_ + 1) * P)), (ch_hi[:, :], ch_lo[:, :]),
                                   True, True)
                last.then_inc(pr["y_full"], 1)
            pe.wait_ge(pr["out"], 14)
            for i in range(2):
                pe.wait_ge(w_lo_made, C_DFT + i + 1)
                for g in range(GROUPS):
                    for tt_ in range(4):
                        s = slice(tt_ * TOKENS, (tt_ + 1) * TOKENS)
                        last = product(pipes[g // 2][:, g % 2, :],
                                       part((y_hi, y_lo), tt_, slice(g * COLS + i * P, g * COLS + (i + 1) * P)),
                                       (w_hi[i][:, s], w_lo[i][:, s]), i == 0 and tt_ == 0, i == 1 and tt_ == 3)
                last.then_inc(chunk_used, 1)

            def scores(at_, i, qt):
                k1, k2, v1, v2 = at_.kv(i)
                if qt == 0:
                    pe.wait_ge(at_.s["k_all"], i // at_.per_kv + 1)
                    pe.wait_ge(at_.s["q_lo"], i + 1)
                if 4 * i + qt >= 2:
                    pe.wait_ge(at_.s["row_max"], 4 * i + qt - 1)
                s, bank = slice(qt * P, (qt + 1) * P), score_banks[qt % 2][:, 0:at_.keys]
                nc.tensor.matmul(bank, q1[i % 4][:, s], k1[:, :], start=True, stop=False)
                nc.tensor.matmul(bank, q2[i % 4][LOW, s], k2[LOW, :], start=False, stop=True)\
                    .then_inc(at_.s["s_full"], 1)

            def shift(at_, i):
                pe.wait_ge(at_.s["diag"], 2 * i + 2)
                if i >= 1:
                    pe.wait_ge(at_.s["shift_in"], i)
                nc.tensor.matmul(shift_bank, pick_hi[:, :], diag_hi[:, :, :], start=True, stop=False)
                nc.tensor.matmul(shift_bank, pick_lo[:, :], diag_lo[:, :, :], start=False, stop=True)\
                    .then_inc(at_.s["shift"], 1)

            def turned_scores(at_, i):
                k1, k2, v1, v2 = at_.kv(i)
                pe.wait_ge(at_.s["shift_in"], i + 1)
                for kt in range(at_.key_tiles):
                    uses = at_.key_tiles * i + kt - 4
                    if uses >= 0:
                        pe.wait_ge(at_.s["p"], uses + 1)
                    s = slice(kt * P, (kt + 1) * P)
                    nc.tensor.matmul(st_bank(at_, i, kt), k1[:, s], q1[i % 4][:, :], start=True, stop=False)
                    nc.tensor.matmul(st_bank(at_, i, kt), k2[:, s], q2[i % 4][:, :], start=False, stop=True)\
                        .then_inc(at_.s["st_full"], 1)

            def values(at_, i, tiles):
                k1, k2, v1, v2 = at_.kv(i)
                e = slice(HEAD_DIM * (i % 2), HEAD_DIM * (i % 2) + P)
                if tiles[0] == 0:
                    pe.wait_ge(at_.s["v_all"], 2 * (i // at_.per_kv) + 2)
                    if i >= 1:
                        pe.wait_ge(at_.s["o"], i)
                for kt in tiles:
                    pe.wait_ge(at_.s["p_lo"], at_.key_tiles * i + kt + 1)
                    last = product(pv_bank, (v1[:, kt, e], v2[:, kt, e]), part((p_hi[i % 2], p_lo[i % 2]), kt),
                                   kt == 0, kt == at_.key_tiles - 1)
                if tiles[-1] == at_.key_tiles - 1:
                    last.then_inc(at_.s["pv"], 1)

            def attention(at_):
                half = at_.key_tiles // 2
                pe.wait_ge(at_.s["consts"], 5 * len(at_.buffers))
                for qt in range(4):
                    scores(at_, 0, qt)
                shift(at_, 0)
                for qt in range(4):
                    scores(at_, 1, qt)
                for i in range(at_.heads):
                    turned_scores(at_, i)
                    if i + 1 < at_.heads:
                        shift(at_, i + 1)
                    for part_ in range(2):
                        if i + 2 < at_.heads:
                            scores(at_, i + 2, 2 * part_)
                            scores(at_, i + 2, 2 * part_ + 1)
                        if i >= 1:
                            values(at_, i - 1, range(part_ * half, (part_ + 1) * half))
                values(at_, at_.heads - 1, range(at_.key_tiles))

            pe.wait_ge(pr["a_lo"], 2)
            attention(main)

            def branch(m, last_turn):
                c = C_BRANCH + 4 * m
                pe.wait_ge(w_lo_made, c + 1)
                pe.wait_ge(br["yf"], m + FREE)
                for t in range(2):
                    for k in range(GROUPS):
                        last = product(ps_d[:, t, :], weight(0, k, t), part((a_hi, a_lo), k), k == 0, k == GROUPS - 1)
                last.then_inc(chunk_used, 1)
                pe.wait_ge(w_lo_made, c + 2)
                pe.wait_ge(br["ya"], m + FREE)
                for t in range(2):
                    for k in range(D_TILES):
                        pe.wait_ge(br["o_lo"], k // 4 + 1)
                        last = product(ps_c[:, t, :], weight(1, k, t), part((o_hi, o_lo), k), k == 0, k == D_TILES - 1)
                last.then_inc(chunk_used, 1)
                pe.wait_ge(br["x_lo"], D_TILES)
                pe.wait_ge(br["gf_out"], m + FREE)
                project(0, ps_a, c + 2)
                pe.wait_ge(br["ga_out"], m + FREE)
                project(1, ps_b, c + 3)

            pe.wait_ge(main.s["o"], N_HEADS)
            with pe.Fori(0, PAIRS) as m:
                branch(m, False)

            n = norms["cross"]
            pe.wait_ge(br["ya"], PAIRS + FREE)
            with pe.Fori(0, 2) as t:
                for b in range(2):
                    p = 2 * t + b
                    pe.wait_ge(w_lo_made, C_OUT + p + 1)
                    for m in range(2):
                        pe.wait_ge(*n.at(f"h_new{m}", p))
                        for k in range(D_TILES):
                            if m == 0 and k in (0, D_TILES - 2):
                                pe.wait_ge(br["m_lo"], PAIRS - (k == 0))
                            last = product(ps_c[:, m, :], weight(b, k, m), part((m_hi, m_lo), k),
                                           k == 0, k == D_TILES - 1)
                        last.then_inc(chunk_used if m else n["tile0"], 1)

            project(0, ps_a, C_CROSS, n)
            attention(cross)
            n = norms["ffn2"]
            pe.wait_ge(w_lo_made, C_CROSS + 2)
            pe.wait_ge(cr["co_lo"], 1)
            for d in range(D_TILES):
                if d >= 2:
                    pe.wait_ge(*n.at(f"h_new{d % 2}", d // 2))
                for k in range(2):
                    last = product(ps_c[:, d % 2, :], weight(1, k, d, D_MODEL), part((co_hi, co_lo), k), k == 0, k == 1)
                last.then_inc(cr["co_tile"], 1)
            pe.drain().then_inc(chunk_used, 1)
            ffn("ffn2", "final", C_FFN2)
            sum_rows(norms["final"])


def column_chunks(w):
    K, N = w.shape
    return w.reshape(K // P, P, N // COLS, COLS).transpose(2, 1, 0, 3).reshape(N // COLS, P, K // P * COLS)


def down_chunks(w):
    return [c[:, f * COLS:(f + k) * COLS] for c in column_chunks(w) for f, k in zip(DOWN_FIRST, DOWN_SPLIT)]


def weight_stream(a):
    def gate_up(gate, up):
        return [c for pair in zip(column_chunks(gate), column_chunks(up)) for c in pair]

    q_w, kv_w, f_w = N_HEADS * HEAD_DIM, N_KV * HEAD_DIM, GROUPS * P
    w_in = a["w_in"][0]
    edges = np.cumsum([0, q_w, kv_w, kv_w, f_w, D_MODEL, D_MODEL])
    q, k, v, f, gate_f, gate_a = (column_chunks(w_in[:, s:e]) for s, e in zip(edges[:-1], edges[1:]))
    t = np.arange(TOKENS)
    angle = 2 * np.pi * (np.outer(t, t) % TOKENS) / TOKENS
    dft = [np.cos(angle), -np.sin(angle)]
    dft = [m.astype(np.float32).reshape(4, P, TOKENS).transpose(1, 0, 2).reshape(P, CHUNK) for m in dft]
    branches = zip(column_chunks(a["w_fourier_branch"][0]), column_chunks(a["w_attn_branch"][0]), gate_f, gate_a)
    w_co = a["w_co"][0].reshape(2, P, D_MODEL).transpose(1, 0, 2).reshape(P, CHUNK)
    chunks = [*gate_up(a["w1_gate"][0], a["w1_up"][0]), *down_chunks(a["w1_down"][0]),
              *k, *v, *f, *q, *column_chunks(a["w_ck"][0]), *column_chunks(a["w_cv"][0]), *dft,
              *(c for four in branches for c in four), *column_chunks(a["w_out"][0]),
              *column_chunks(a["w_cq"][0]), w_co,
              *gate_up(a["w2_gate"][0], a["w2_up"][0]), *down_chunks(a["w2_down"][0])]
    out = np.zeros((N_CHUNKS, P, CHUNK), np.float32)
    assert len(chunks) == N_CHUNKS
    for n, c in enumerate(chunks):
        out[n, :, :c.shape[1]] = c
    return out


def feature_tiles(x):
    return np.ascontiguousarray(x.reshape(x.shape[0], -1, P).transpose(2, 1, 0))


def rope_tables():
    f32 = np.float32
    t = np.arange(TOKENS)
    inv = f32(1.0) / (f32(10000.0) ** (np.arange(0, 32, 2, dtype=f32) / f32(32)))
    d = np.arange(P) % HEAD_DIM
    position = np.where((d < 32)[:, None], (t // 64)[None, :], (t % 64)[None, :]).astype(f32)
    angle = position * inv[d % 16][:, None]
    sign = np.where(d % 32 < 16, -1.0, 1.0)[:, None]
    return np.stack([np.cos(angle), sign * np.sin(angle)]).astype(f32)


def kernel(**inputs):
    import concourse.bacc as _bacc
    from concourse.bass_utils import run_bass_kernel_spmd as _run

    a = {name: np.asarray(value) for name, value in inputs.items()}
    gains = np.stack([a["g_ffn1"][0], a["g_mix"][0], a["g_cross"][0], a["g_ffn2"][0], a["g_final"], a["g_mem"][0]])
    heads = np.stack([a["k_gain"][0]] + [a["q_gain"][0]] * 7, axis=1)
    c = np.arange(P)
    angle = 2 * np.pi * (np.outer(c, c) % P) / P
    channel = np.concatenate([np.cos(angle), np.sin(angle)], axis=1) / np.sqrt(TOKENS * P)
    arrays = {
        "xT": feature_tiles(a["x"][0]),
        "memT": feature_tiles(a["mem"][0]),
        "stream": weight_stream(a),
        "gains": np.ascontiguousarray(gains.reshape(6, D_TILES, P).transpose(2, 0, 1)),
        "head_gains": np.ascontiguousarray(np.concatenate([heads, heads])),
        "rope": rope_tables(),
        "channel_dft": channel.astype(np.float32),
        "identity": np.eye(P, dtype=np.float32),
    }
    nc = _bacc.Bacc("TRN2", target_bir_lowering=False, num_devices=1)
    args = [nc.dram_tensor(name, x.shape, F32, kind="ExternalInput").ap() for name, x in arrays.items()]
    out = nc.dram_tensor("outT", (P, D_TILES, TOKENS), F32, kind="ExternalOutput").ap()
    encoder_block(nc, *args, out)
    r = _run(nc, [arrays], core_ids=[0])
    outT = r.results[0]["outT"]
    return outT.transpose(2, 1, 0).reshape(1, TOKENS, D_MODEL)
```

```python
from contextlib import ExitStack

import numpy as np

import concourse.bass as bass
from concourse import mybir

ACT = mybir.ActivationFunctionType
ALU = mybir.AluOpType
AX = mybir.AxisListType
F32 = mybir.dt.float32
F32R = mybir.dt.float32r

P = 128
TOKENS = 512
D_MODEL = 1024
D_TILES = D_MODEL // P
MEM_LEN = 256
HEAD_DIM = 64
N_HEADS = 16
N_KV = 4
N_CROSS = 4
D_FF = 2816
FF_TILES = D_FF // P
FF_PAIRS = FF_TILES // 2
PAIRS = D_TILES // 2
GROUPS = 4
EPS = 1e-6
SCALE = HEAD_DIM ** -0.5
COLS = 2 * P
CHUNK = D_TILES * COLS
DOWN_SPLIT = (6, 6, 5, 5)
DOWN_FIRST = (0, 6, 12, 17)
BRANCH_K = (4, 8, 8, 8)

C_FFN1 = 0
C_DOWN1 = C_FFN1 + 2 * FF_PAIRS
C_IN = C_DOWN1 + 4 * PAIRS
C_DFT = C_IN + 8
C_BRANCH = C_DFT + 2
C_OUT = C_BRANCH + 4 * PAIRS
C_CK = C_OUT + PAIRS
C_CQ, C_CV, C_CO = C_CK + 1, C_CK + 2, C_CK + 3
C_FFN2 = C_CO + 1
C_DOWN2 = C_FFN2 + 2 * FF_PAIRS
N_CHUNKS = C_DOWN2 + 4 * PAIRS

KIB = 1024


def encoder_block(nc, xT, memT, stream, gains, head_gains, rope, channel_dft, identity, outT):
    with ExitStack() as ctx:
        base = -(-nc.sbuf_base // 32) * 32

        def at(name, shape, kib, dt=F32):
            return nc.alloc_sbuf_tensor_at(name, shape, dt, offset=base + int(kib * KIB))

        def sem(name):
            return ctx.enter_context(nc.semaphore(name))

        def psum(name):
            return ctx.enter_context(nc.psum_tensor(name, [P, 2, TOKENS], F32))

        h = at("h", [P, D_TILES, TOKENS], 0)
        raw = [at(f"raw{b}", [P, CHUNK], 16 + 8 * b) for b in range(2)]
        w_hi = [at(f"w_hi{b}", [P, CHUNK], 32 + 8 * b, F32R) for b in range(2)]
        w_lo = [at(f"w_lo{b}", [P, CHUNK], 48 + 8 * b, F32R) for b in range(2)]
        row_factor = at("row_factor", [P, TOKENS], 64)
        square_sum = at("square_sum", [P, TOKENS], 66)
        SM = 68
        ident = at("ident", [P, P], SM)
        ones = at("ones", [P, P], SM + .5)
        head_ones = at("head_ones", [P, P], SM + 1, F32R)
        pick = at("pick", [P, P], SM + 1.5, F32R)
        gain = at("gain", [P, 6, D_TILES], SM + 2.5)
        head_gain = at("head_gain", [P, 8], SM + 2.75)
        ch_raw = at("ch_raw", [P, 2 * P], SM + 3)
        ch_hi = at("ch_hi", [P, 2 * P], SM + 4, F32R)
        ch_lo = at("ch_lo", [P, 2 * P], SM + 5, F32R)
        row_max = at("row_max", [P, 2, 4], SM + 6)
        T = SM + 6.25
        newton = at("newton", [P, TOKENS], T + 2)
        neg_half = at("neg_half", [P, TOKENS], T + 4)
        rsq = at("rsq", [P, TOKENS], T + 6)
        squares = [at(f"squares{b}", [P, TOKENS], T + 8 + 2 * b) for b in range(2)]
        gate_t = at("gate_t", [P, 2, TOKENS], T)
        silu_t = at("silu_t", [P, 2, TOKENS], T + 4)
        up_t = at("up_t", [P, 2, TOKENS], T + 8)
        V = T + 12
        x_hi = at("x_hi", [P, D_TILES, TOKENS], V, F32R)
        x_lo = at("x_lo", [P, D_TILES, TOKENS], V + 16, F32R)
        ff_hi = at("ff_hi", [P, FF_TILES, TOKENS], V + 32, F32R)
        ff_lo = at("ff_lo", [P, FF_TILES, TOKENS], V + 76, F32R)
        kq = at("kq", [P, 10, TOKENS], V + 32)
        v_t = at("v_t", [P, 2, TOKENS], V + 52)
        f_t = at("f_t", [P, GROUPS, TOKENS], V + 56)
        f_lo = at("f_lo", [P, GROUPS, TOKENS], V + 56, F32R)
        f_hi = at("f_hi", [P, GROUPS, TOKENS], V + 64, F32R)
        v_tok = at("v_tok", [P, 4, N_KV * HEAD_DIM], V + 88)
        rope_cos = at("rope_cos", [P, TOKENS], V + 96)
        rope_sin = at("rope_sin", [P, TOKENS], V + 98)
        hsq = at("hsq", [P, 2, TOKENS], V + 100)
        hsq_hi = at("hsq_hi", [P, 2, TOKENS], V + 104, F32R)
        hsq_lo = at("hsq_lo", [P, 2, TOKENS], V + 108, F32R)
        hneg_half = at("hneg_half", [P, 2, TOKENS], V + 112)
        hrsq = at("hrsq", [P, 2, TOKENS], V + 116)
        hnewton = at("hnewton", [P, 2, TOKENS], T)
        shuffled = at("shuffled", [P, 2, TOKENS], T + 4)
        rotated = at("rotated", [P, 2, TOKENS], T + 8)
        normed = at("normed", [P, 2, TOKENS], V + 92)
        mem = at("mem", [P, D_TILES, MEM_LEN], V + 72)
        mem_sq = at("mem_sq", [P, D_TILES, MEM_LEN], V + 80)
        mem_hi = at("mem_hi", [P, D_TILES, MEM_LEN], V + 56, F32R)
        mem_lo = at("mem_lo", [P, D_TILES, MEM_LEN], V + 64, F32R)
        msum = at("msum", [P, MEM_LEN], V + 48)
        mneg_half = at("mneg_half", [P, MEM_LEN], V + 49)
        mrsq = at("mrsq", [P, MEM_LEN], V + 50)
        mnewton = at("mnewton", [P, MEM_LEN], V + 51)
        cross_k = at("cross_k", [P, 2, MEM_LEN], V + 88)
        cross_v = at("cross_v", [P, 2, MEM_LEN], V + 90)
        y_hi = at("y_hi", [P, 4, 2 * TOKENS], V, F32R)
        y_lo = at("y_lo", [P, 4, 2 * TOKENS], V + 16, F32R)
        a_hi = at("a_hi", [P, GROUPS, TOKENS], V + 72, F32R)
        a_lo = at("a_lo", [P, GROUPS, TOKENS], V + 80, F32R)
        p_hi = [at(f"p_hi{b}", [P, 4, TOKENS], V + 8 * b, F32R) for b in range(2)]
        p_lo = [at(f"p_lo{b}", [P, 4, TOKENS], V + 16 + 8 * b, F32R) for b in range(2)]
        p_main = at("p_main", [P, 4, TOKENS], V + 56)
        p_cross = at("p_cross", [P, 2, TOKENS], V + 72)
        diag = at("diag", [P, 4, P], T + 6, F32R)
        q_at = (V + 52, V + 92, V + 116, T)
        q1 = [at(f"q1_{b}", [P, TOKENS], q_at[b], F32R) for b in range(4)]
        q2 = [at(f"q2_{b}", [P, TOKENS], q_at[b] + 2, F32R) for b in range(4)]

        def kv_buffer(tag, kib, keys):
            v_shape = [P, keys // P, 3 * HEAD_DIM]
            v_kib = keys // P * 0.75
            return (at(f"k1_{tag}", [P, keys], kib, F32R), at(f"k2_{tag}", [P, keys], kib + keys / 256, F32R),
                    at(f"v_hi_{tag}", v_shape, kib + keys / 128, F32R),
                    at(f"v_lo_{tag}", v_shape, kib + keys / 128 + v_kib, F32R))

        kv_main = [kv_buffer(f"m{b}", V + 96 + 10 * b, TOKENS) for b in range(2)]
        kv_cross = [kv_buffer(f"c{b}", V + 96 + 5 * b, MEM_LEN) for b in range(N_CROSS)]
        denom = at("denom", [P, TOKENS], T + 4)
        cross_q = at("cross_q", [P, 2, TOKENS], V + 32)
        cross_o = at("cross_o", [P, 2, TOKENS], V + 36)
        co_hi = at("co_hi", [P, 2, TOKENS], V + 80, F32R)
        co_lo = at("co_lo", [P, 2, TOKENS], V + 84, F32R)
        o_hi = at("o_hi", [P, D_TILES, TOKENS], V + 56, F32R)
        o_lo = at("o_lo", [P, D_TILES, TOKENS], V + 88, F32R)
        m_hi = at("m_hi", [P, D_TILES, TOKENS], V + 32, F32R)
        m_lo = at("m_lo", [P, D_TILES, TOKENS], V + 104, F32R)
        gf_t = at("gf_t", [P, 2, TOKENS], T)
        ga_t = at("ga_t", [P, 2, TOKENS], T + 4)
        merged_t = at("merged_t", [P, 2, TOKENS], T + 8)
        final_t = at("final_t", [P, D_TILES, TOKENS], V)

        ps_a, ps_b, ps_c, ps_d = (psum(f"ps_{c}") for c in "abcd")
        stat = ps_d[:, 1, :]

        x_loaded = [sem(f"x_loaded{i}") for i in range(PAIRS)]
        gains_loaded = sem("gains_loaded")
        consts_loaded = sem("consts_loaded")
        rope_loaded = sem("rope_loaded")
        mem_loaded = sem("mem_loaded")
        first_half = {step: sem(f"first_half_{step}") for step in ("loaded", "hi", "lo")}
        stored = sem("stored")
        consts_set = sem("consts_set")
        ch_hi_made, ch_lo_made = sem("ch_hi_made"), sem("ch_lo_made")
        raw_loaded = [sem(f"raw_loaded{b}") for b in range(2)]
        w_hi_made = sem("w_hi_made")
        w_lo_made = sem("w_lo_made")
        chunk_used = sem("chunk_used")

        FREE = 1

        def sems(tag, *steps):
            return {step: sem(f"{tag}_{step}") for step in steps}

        norm_sems = sems("norm", "h_new0", "h_new1", "tile0", "x_hi", "squared", "x_lo", "summed", "stat",
                         "neg_half", "root", "newton", "factor")
        norm_adds = {"h_new0": PAIRS, "h_new1": PAIRS, "tile0": PAIRS, "x_hi": D_TILES, "squared": D_TILES,
                     "x_lo": D_TILES, "summed": D_TILES + 1, "newton": 2}

        class Norm:
            def __init__(self, earlier, earlier_updates, earlier_tile0):
                self.before = {step: norm_adds.get(step, 1) * earlier for step in norm_sems}
                self.before["h_new0"] = self.before["h_new1"] = PAIRS * earlier_updates + FREE
                self.before["tile0"] = PAIRS * earlier_tile0

            def __getitem__(self, step):
                return norm_sems[step]

            def at(self, step, value):
                return norm_sems[step], value + self.before[step]

        norms = {"ffn1": Norm(0, 0, 0), "mix": Norm(1, 0, 0), "cross": Norm(2, 1, 1), "ffn2": Norm(3, 2, 2),
                 "final": Norm(4, 3, 2)}
        ffns = {tag: sems(tag, "gate_out", "silu", "up_out", "product", "ff_hi", "ff_lo")
                for tag in ("ffn1", "ffn2")}
        pr = sems("proj", "out", "v_turned", "v_tok", "y_full", "y_hi", "f_hi", "f_lo", "a_full",
                  "a_hi", "a_lo")
        hd = sems("head", "sq", "sq_hi", "sq_lo", "stat", "neg_half", "root", "y_sq", "t_mul", "factor",
                  "scaled", "shuffled", "mul", "roped")
        mm = sems("mem", "squared", "sum", "stat", "neg_half", "root", "newton", "factor", "normed", "hi", "lo")
        br = sems("branch", "o_hi", "o_lo", "x_hi", "x_lo", "gf_out", "ga_out", "sig_f", "sig_a", "yf", "ya",
                  "merged", "m_hi", "m_lo")
        cr = sems("cr", "k_out", "q_out", "v_out", "co_hi", "co_lo", "co_tile")
        out_ready = sem("out_ready")

        def wide(ap, n=2):
            return ap.unsqueeze(1).to_broadcast([P, n, ap.shape[1]])

        def wait_apart(engine, semaphore, value):
            engine.wait_ge(semaphore, value)
            engine.wait_ge(semaphore, 1)

        def convert_hi(act, b, q, cols=CHUNK, first=False):
            act.wait_ge(raw_loaded[b], 16 * q + 16)
            if not first:
                act.wait_ge(chunk_used, 2 * q + b - 1)
            nc.scalar.activation(w_hi[b][:, 0:cols], raw[b][:, 0:cols], ACT.Copy).then_inc(w_hi_made, 1)

        def convert_lo(dve, b, q, cols=CHUNK):
            dve.wait_ge(w_hi_made, 2 * q + b + 1)
            nc.vector.tensor_tensor(w_lo[b][:, 0:cols], raw[b][:, 0:cols],
                                    w_hi[b][:, 0:cols].bitcast(F32), ALU.subtract).then_inc(w_lo_made, 1)

        def product(out, w, x, start, stop):
            nc.tensor.matmul(out, w[0], x[0], start=start, stop=False)
            nc.tensor.matmul(out, w[0], x[1], start=False, stop=False)
            return nc.tensor.matmul(out, w[1], x[0], start=False, stop=stop)

        def weight(b, k, m, cols=COLS):
            s = slice(k * cols + m * P, k * cols + (m + 1) * P)
            return w_hi[b][:, s], w_lo[b][:, s]

        def part(pair, k, cols=slice(None)):
            return pair[0][:, k, cols], pair[1][:, k, cols]

        x_parts = (x_hi, x_lo)
        pipes = (ps_a, ps_b)
        y_pipes = (ps_b, ps_c, ps_a, ps_d)
        co_banks = [ps[:, m, :] for ps in (ps_a, ps_b, ps_c, ps_d) for m in range(2)]

        class Attention:
            def __init__(self, tag, heads, keys, q_tiles, out_tiles, k_tiles, v_rows, buffers, per_kv, p_raw):
                self.heads, self.keys, self.pairs = heads, keys, keys // (2 * P)
                self.q_tiles, self.out_tiles, self.k_tiles, self.v_rows = q_tiles, out_tiles, k_tiles, v_rows
                self.buffers, self.per_kv, self.p_raw = buffers, per_kv, p_raw
                self.s = sems(tag, "consts", "k_hi", "k_all", "v_hi", "v_all", "q_hi", "q_lo", "s_full",
                              "row_max", "diag", "shift", "shift_in", "st_full", "p", "p_hi0", "p_hi1", "p_lo", "pv",
                              "log_denom", "inv_denom", "o")

            def kv(self, i):
                return self.buffers[i // self.per_kv % len(self.buffers)]

            def half(self, i):
                return slice(HEAD_DIM * (i % 2), HEAD_DIM * (i % 2) + HEAD_DIM)

        main = Attention("main", N_HEADS, TOKENS, kq[:, 2:10, :], kq[:, 2:10, :], kq[:, 0:2, :], v_tok[:, :, :],
                         kv_main, N_HEADS // N_KV, p_main)
        cross = Attention("crossatt", N_CROSS, MEM_LEN, cross_q[:, :, :], cross_o[:, :, :], cross_k[:, :, :],
                          cross_v[:, :, :], kv_cross, 1, p_cross)
        LOW, HIGH = slice(0, HEAD_DIM), slice(HEAD_DIM, P)
        pv_bank, shift_bank = ps_d[:, 0, :], ps_d[:, 1, :]

        def st_pair(at_, i, j):
            return (ps_b, ps_c)[j if at_.pairs == 2 else i % 2]

        block = ctx.enter_context(nc.Block())

        @block.sync
        def _(sp):
            def load(b, q, cols=CHUNK, first=False):
                if not first:
                    sp.wait_ge(w_lo_made, 2 * q + b - 1)
                sp.dma_start(raw[b][:, 0:cols], stream[2 * q + b, :, 0:cols]).then_inc(raw_loaded[b], 16)

            def ffn_stream(c0):
                with sp.Fori(1, FF_PAIRS + 1) as j:
                    for b in range(2):
                        load(b, c0 // 2 + j)
                down = (c0 + 2 * FF_PAIRS) // 2
                for i in (2, 3):
                    load(i % 2, down + 1, DOWN_SPLIT[i] * COLS)
                with sp.Fori(1, PAIRS) as p:
                    for i in range(4):
                        load(i % 2, down + 2 * p + i // 2, DOWN_SPLIT[i] * COLS)

            half = CHUNK // 2
            for p in range(PAIRS):
                sp.dma_start(h[:, 2 * p:2 * p + 2, :], xT[:, 2 * p:2 * p + 2, :]).then_inc(x_loaded[p], 16)
                if p == 0:
                    sp.dma_start(raw[0][:, 0:half], stream[0, :, 0:half]).then_inc(first_half["loaded"], 16)
                if p == 1:
                    sp.dma_start(raw[0][:, half:], stream[0, :, half:]).then_inc(raw_loaded[0], 16)
            load(1, 0, first=True)
            ffn_stream(C_FFN1)
            with sp.Fori(C_IN // 2, C_BRANCH // 2) as q:
                for b in range(2):
                    load(b, q)
            with sp.Fori(0, PAIRS) as m:
                for i in range(4):
                    load(i % 2, C_BRANCH // 2 + 2 * m + i // 2, BRANCH_K[i] * COLS)
            sp.wait_ge(chunk_used, C_BRANCH + 4 * (PAIRS - 1) + 1)
            sp.dma_start(mem[:, :, :], memT).then_inc(mem_loaded, 16)
            with sp.Fori(C_OUT // 2, C_FFN2 // 2 + 1) as q:
                for b in range(2):
                    load(b, q)
            ffn_stream(C_FFN2)
            for p in range(PAIRS):
                sp.wait_ge(out_ready, 2 * p + 2)
                sp.dma_start(outT[:, 2 * p:2 * p + 2, :], final_t[:, 2 * p:2 * p + 2, :]).then_inc(stored, 16)
            sp.wait_ge(stored, 16 * PAIRS)

        @block.gpsimd
        def _(pool):
            def fill_all(semaphore, fills):
                for n, (out, value) in enumerate(fills):
                    if n:
                        pool.wait_ge(semaphore, n)
                    nc.gpsimd.memset(out.bitcast(F32), value).then_inc(semaphore, 1)

            fill_all(consts_set, [(head_ones[:, :], 0.0), (pick[:, :], 0.0),
                                  (ones[:, :], 1.0), (head_ones[LOW, LOW], 1.0), (head_ones[HIGH, HIGH], 1.0),
                                  (pick[:, 64:96], 1.0)])

            pool.wait_ge(rope_loaded, 32)
            with pool.Fori(0, 5) as s:
                pool.wait_ge(hd["shuffled"], s + 1)
                nc.gpsimd.tensor_tensor(shuffled[:, :, :], shuffled[:, :, :], wide(rope_sin[:, :]), ALU.mult)\
                    .then_inc(hd["mul"], 1)
                nc.gpsimd.tensor_tensor(rotated[:, :, :], normed[:, :, :], wide(rope_cos[:, :]), ALU.mult)\
                    .then_inc(hd["mul"], 1)
                wait_apart(pool, hd["mul"], 2 * s + 2)
                nc.gpsimd.tensor_tensor(kq[:, bass.ds(2 * s, 2), :], shuffled[:, :, :], rotated[:, :, :], ALU.add)\
                    .then_inc(hd["roped"], 1)

            def constants(at_):
                fill_all(at_.s["consts"], [fill for k1, k2, v1, v2 in at_.buffers for fill in (
                    (k2[HIGH, :], 0.0), (k2[64:65, :], 1.0),
                    (v1[:, :, HIGH], 1.0), (v2[:, :, HIGH], 0.0))])

            def minus(out, a, hi):
                return nc.gpsimd.tensor_tensor(out, a, hi.bitcast(F32), ALU.subtract)

            def low_parts(at_):
                for i in range(at_.heads):
                    for j in range(at_.pairs):
                        two = slice(2 * j, 2 * j + 2)
                        pool.wait_ge(at_.s[f"p_hi{j}"], i + 1)
                        minus(p_lo[i % 2][:, two, :], at_.p_raw[:, two, :], p_hi[i % 2][:, two, :])\
                            .then_inc(at_.s["p_lo"], 1)
                    if at_ is main and i % 4 == 1 and i // 4 + 1 < N_KV:
                        g = i // 4 + 1
                        k1, k2, v1, v2 = at_.buffers[g % 2]
                        pool.wait_ge(at_.s["p_lo"], 2 * i + 2)
                        pool.wait_ge(at_.s["k_hi"], 3 * (g + 1))
                        minus(k1[HIGH, :], at_.k_tiles[at_.half(g), g // 2, :], k1[at_.half(g), :])\
                            .then_inc(at_.s["k_all"], 1)
                        pool.wait_ge(at_.s["k_all"], g + 1)
                        pool.wait_ge(at_.s["v_hi"], 2 * (g + 1))
                        values = at_.v_rows[:, :, HEAD_DIM * g:HEAD_DIM * (g + 1)]
                        minus(v2[:, :, LOW], values, v1[:, :, LOW]).then_inc(at_.s["v_all"], 1)
                        minus(v2[:, :, 2 * HEAD_DIM:], values, v1[:, :, LOW]).then_inc(at_.s["v_all"], 1)
                        pool.wait_ge(at_.s["v_all"], 2 * g + 2)

            pool.wait_ge(hd["roped"], 5)
            constants(main)
            low_parts(main)
            pool.wait_ge(chunk_used, C_OUT + PAIRS)
            constants(cross)
            low_parts(cross)
            n = norms["ffn2"]
            for d in range(D_TILES):
                pool.wait_ge(*n.at("squared", d + 1))
                pool.wait_ge(*n.at("summed", d + 1))
                nc.gpsimd.tensor_tensor(square_sum[:, :], square_sum[:, :], squares[d % 2][:, :], ALU.add)\
                    .then_inc(n["summed"], 1)

        @block.scalar
        def _(act):
            def copy(out, in_, scale=1.0):
                return nc.scalar.activation(out, in_, ACT.Copy, scale=scale)

            def high(n, gain_row, d, ready):
                act.wait_ge(*ready)
                copy(x_hi[:, d, :], h[:, d, :], gain[:, gain_row, d:d + 1]).then_inc(n["x_hi"], 1)

            def square(n, d, m, ready):
                act.wait_ge(*ready)
                act.wait_ge(*n.at("summed", d))
                nc.scalar.activation(squares[m][:, :], h[:, d, :], ACT.Square).then_inc(n["squared"], 1)

            def refresh(n, gain_row, d, m, ready, split=True):
                if split:
                    high(n, gain_row, d, ready)
                square(n, d, m, ready)

            def inverse_root(out, neg_half_mean):
                return nc.scalar.activation(out, neg_half_mean, ACT.Abs_reciprocal_sqrt, scale=-2.0)

            def root(n, then=None):
                act.preload_act_table(ACT.Abs_reciprocal_sqrt)
                act.wait_ge(*n.at("neg_half", 1))
                inverse_root(rsq[:, :], neg_half[:, :]).then_inc(n["root"], 1)
                if then is not None:
                    act.preload_act_table(then)

            def feed_forward(tag, c0, j):
                f = ffns[tag]
                convert_hi(act, 0, c0 // 2 + j + 1)
                act.wait_ge(f["gate_out"], j + 1)
                nc.scalar.activation(silu_t[:, :, :], gate_t[:, :, :], ACT.Silu).then_inc(f["silu"], 1)
                convert_hi(act, 1, c0 // 2 + j + 1)
                wait_apart(act, f["product"], j + 1)
                copy(ff_hi[:, bass.ds(2 * j, 2), :], up_t[:, :, :]).then_inc(f["ff_hi"], 1)

            def down(n, gain_row, c0, p, last, end):
                for i in range(3 if not (end and last) else 2):
                    cols = (DOWN_SPLIT[(i + 2) % 4] * COLS) if not (last and i >= 2) else CHUNK
                    convert_hi(act, i % 2, c0 // 2 + 2 * p + i // 2 + 1, cols)
                for m in range(2):
                    refresh(n, gain_row, 2 * p + m, m, n.at(f"h_new{m}", p + 1), split=not end)
                if not (end and last):
                    convert_hi(act, 1, c0 // 2 + 2 * p + 2, CHUNK if last else DOWN_SPLIT[1] * COLS)

            def ffn(tag, nxt, c0, gain_row, end):
                root(norms[tag], ACT.Silu)
                feed_forward(tag, c0, 0)
                with act.Fori(1, FF_PAIRS) as j:
                    feed_forward(tag, c0, j)
                down0 = c0 + 2 * FF_PAIRS
                for p in range(PAIRS):
                    down(norms[nxt], gain_row, down0, p, p == PAIRS - 1, end)

            act.dma_start(gain[:, :, :], gains).then_inc(gains_loaded, 16)
            act.dma_start(head_gain[:, :], head_gains).then_inc(consts_loaded, 16)
            act.dma_start(ident[:, :], identity).then_inc(consts_loaded, 16)
            act.dma_start(ch_raw[:, :], channel_dft).then_inc(consts_loaded, 16)
            n = norms["ffn1"]
            act.wait_ge(gains_loaded, 16)
            for d in range(D_TILES):
                if d == 2:
                    act.wait_ge(first_half["loaded"], 16)
                    copy(w_hi[0][:, 0:CHUNK // 2], raw[0][:, 0:CHUNK // 2]).then_inc(first_half["hi"], 1)
                if d == 4:
                    act.wait_ge(raw_loaded[0], 16)
                    copy(w_hi[0][:, CHUNK // 2:], raw[0][:, CHUNK // 2:]).then_inc(w_hi_made, 1)
                high(n, 0, d, (x_loaded[d // 2], 16))
            for d in range(D_TILES):
                square(n, d, d % 2, (x_loaded[d // 2], 16))
                if d == 3:
                    convert_hi(act, 1, 0, first=True)
            ffn("ffn1", "mix", C_FFN1, 1, False)

            act.wait_ge(chunk_used, C_IN)
            act.dma_start(rope_cos[:, :], rope[0]).then_inc(rope_loaded, 16)
            act.dma_start(rope_sin[:, :], rope[1]).then_inc(rope_loaded, 16)
            root(norms["mix"])

            def square_heads(s):
                act.wait_ge(pr["out"], s + 1 if s == 0 else s + 2)
                if s >= 1:
                    act.wait_ge(hd["stat"], s)
                nc.scalar.activation(hsq[:, :, :], kq[:, 2 * s:2 * s + 2, :], ACT.Square).then_inc(hd["sq"], 1)
                act.wait_ge(hd["sq"], s + 1)
                copy(hsq_hi[:, :, :], hsq[:, :, :]).then_inc(hd["sq_hi"], 1)

            def head_root(s):
                act.wait_ge(hd["neg_half"], s + 1 + FREE)
                if s >= 1:
                    act.wait_ge(hd["scaled"], s)
                inverse_root(hrsq[:, :, :], hneg_half[:, :, :]).then_inc(hd["root"], 1)
                act.wait_ge(hd["root"], s + 1)
                nc.scalar.activation(hnewton[:, :, :], hrsq[:, :, :], ACT.Square).then_inc(hd["y_sq"], 1)

            q0 = C_IN // 2
            act.wait_ge(consts_loaded, 48)
            copy(ch_hi[:, :], ch_raw[:, :]).then_inc(ch_hi_made, 1)
            convert_hi(act, 0, q0 + 1)
            square_heads(0)
            convert_hi(act, 1, q0 + 1)
            for u in range(2, 6):
                convert_hi(act, u % 2, q0 + u // 2 + 1)
                square_heads(u - 1)
                head_root(u - 2)
            convert_hi(act, 0, q0 + 4)
            act.wait_ge(pr["out"], 7)
            copy(f_hi[:, 0:2, :], f_t[:, 0:2, :]).then_inc(pr["f_hi"], 1)
            head_root(4)
            act.wait_ge(pr["out"], 8)
            copy(f_hi[:, 2:4, :], f_t[:, 2:4, :]).then_inc(pr["f_hi"], 1)

            def k_high(at_, g):
                k1, k2, v1, v2 = at_.buffers[g % len(at_.buffers)]
                source = at_.k_tiles[at_.half(g), g // 2, :]
                if g >= len(at_.buffers):
                    act.wait_ge(at_.s["pv"], at_.per_kv * (g - 1))
                copy(k1[LOW, :], source).then_inc(at_.s["k_hi"], 1)
                copy(k1[HIGH, :], source).then_inc(at_.s["k_hi"], 1)
                copy(k2[LOW, :], source).then_inc(at_.s["k_hi"], 1)

            def v_high(at_, g):
                k1, k2, v1, v2 = at_.buffers[g % len(at_.buffers)]
                values = at_.v_rows[:, :, HEAD_DIM * g:HEAD_DIM * (g + 1)]
                copy(v1[:, :, LOW], values).then_inc(at_.s["v_hi"], 1)
                copy(v1[:, :, 2 * HEAD_DIM:], values).then_inc(at_.s["v_hi"], 1)

            def q_high(at_, i):
                source = at_.q_tiles[at_.half(i), i // 2, :]
                if i >= 4:
                    act.wait_ge(at_.s["st_full"], at_.pairs * (i - 3))
                copy(q1[i % 4][LOW, :], source).then_inc(at_.s["q_hi"], 1)
                copy(q1[i % 4][HIGH, :], source).then_inc(at_.s["q_hi"], 1)

            def shift_in(at_, i):
                act.wait_ge(at_.s["shift"], i + 1)
                copy(q2[i % 4][HIGH, :], shift_bank[HIGH, :]).then_inc(at_.s["shift_in"], 1)

            def exponentials(at_, i):
                for j in range(at_.pairs):
                    act.wait_ge(at_.s["st_full"], at_.pairs * i + j + 1)
                    if i >= 1:
                        act.wait_ge(at_.s["p_lo"], at_.pairs * (i - 1) + j + 1)
                    two = slice(2 * j, 2 * j + 2)
                    nc.scalar.activation(at_.p_raw[:, two, :], st_pair(at_, i, j)[:, :, :], ACT.Exp, scale=SCALE)\
                        .then_inc(at_.s["p"], 1)
                if at_.pairs == 2:
                    if i >= 2:
                        act.wait_ge(at_.s["pv"], i - 1)
                    act.wait_ge(at_.s["p"], 2 * i + 2)
                    copy(p_hi[i % 2][:, 2:4, :], at_.p_raw[:, 2:4, :]).then_inc(at_.s["p_hi1"], 1)

            def invert(at_, i):
                e = at_.half(i)
                act.wait_ge(at_.s["pv"], i + 1)
                nc.scalar.activation(denom[e, :], pv_bank[at_.half(i + 1), :], ACT.Ln).then_inc(at_.s["log_denom"], 1)
                act.wait_ge(at_.s["log_denom"], i + 1)
                nc.scalar.activation(denom[e, :], denom[e, :], ACT.Exp, scale=-1.0).then_inc(at_.s["inv_denom"], 1)

            def attention(at_, before_last):
                for i in range(at_.heads):
                    if i >= 2:
                        invert(at_, i - 2)
                    exponentials(at_, i)
                    if i + 1 < at_.heads:
                        shift_in(at_, i + 1)
                    if i + 3 < at_.heads:
                        q_high(at_, i + 3)
                    if at_ is main and i % 4 == 1 and i // 4 + 1 < N_KV:
                        k_high(at_, i // 4 + 1)
                        v_high(at_, i // 4 + 1)
                    if at_ is main and i == 1:
                        convert_hi(act, 1, C_BRANCH // 2)
                invert(at_, at_.heads - 2)
                before_last()
                invert(at_, at_.heads - 1)

            act.preload_act_table_set("natural_log_exp_and_others")
            for tt in range(4):
                act.wait_ge(pr["y_full"], tt + 1)
                copy(y_hi[:, tt, :], y_pipes[tt].rearrange("p a b -> p (a b)")).then_inc(pr["y_hi"], 1)
            convert_hi(act, 1, q0 + 4)
            act.wait_ge(hd["roped"], 5)
            k_high(main, 0)
            for i in range(3):
                q_high(main, i)
            act.wait_ge(pr["v_tok"], 1)
            v_high(main, 0)
            convert_hi(act, 0, C_BRANCH // 2, BRANCH_K[0] * COLS)
            shift_in(main, 0)
            for half in range(2):
                act.wait_ge(pr["a_full"], half + 1)
                copy(a_hi[:, 2 * half:2 * half + 2, :], y_pipes[half][:, :, :]).then_inc(pr["a_hi"], 1)
            def split_x(tiles):
                act.wait_ge(main.s["pv"], N_HEADS - (tiles[0] == 0))
                for k in tiles:
                    copy(x_hi[:, k, :], h[:, k, :], gain[:, 1, k:k + 1]).then_inc(br["x_hi"], 1)

            attention(main, lambda: split_x(range(4)))

            split_x(range(4, D_TILES))
            act.preload_act_table(ACT.Sigmoid)
            act.wait_ge(main.s["o"], N_HEADS)
            for half in range(2):
                s = slice(4 * half, 4 * half + 4)
                copy(o_hi[:, s, :], main.out_tiles[:, s, :]).then_inc(br["o_hi"], 1)

            def branch(m, last):
                q = C_BRANCH // 2 + 2 * m
                convert_hi(act, 0, q + 1)
                act.wait_ge(br["gf_out"], m + 1 + FREE)
                nc.scalar.activation(gf_t[:, :, :], gf_t[:, :, :], ACT.Sigmoid).then_inc(br["sig_f"], 1)
                convert_hi(act, 1, q + 1)
                act.wait_ge(br["ga_out"], m + 1 + FREE)
                nc.scalar.activation(ga_t[:, :, :], ga_t[:, :, :], ACT.Sigmoid).then_inc(br["sig_a"], 1)
                convert_hi(act, 0, q + 2, CHUNK if last else BRANCH_K[0] * COLS)
                if last:
                    act.wait_ge(mem_loaded, 16)
                    nc.scalar.activation(mem_sq[:, :, :], mem[:, :, :], ACT.Square).then_inc(mm["squared"], 1)
                else:
                    convert_hi(act, 1, q + 2)
                wait_apart(act, br["merged"], m + 1)
                copy(m_hi[:, bass.ds(2 * m, 2), :], merged_t[:, :, :]).then_inc(br["m_hi"], 1)
                if last:
                    convert_hi(act, 1, q + 2)

            with act.Fori(0, PAIRS - 1) as m:
                branch(m, False)
            branch(PAIRS - 1, True)

            n = norms["cross"]
            for p in range(PAIRS):
                for m in range(2):
                    high(n, 2, 2 * p + m, n.at(f"h_new{m}", p + 1))
                convert_hi(act, p % 2, C_OUT // 2 + p // 2 + 1)
                for m in range(2):
                    square(n, 2 * p + m, m, n.at(f"h_new{m}", p + 1))
                if p == 0:
                    act.wait_ge(mm["neg_half"], 1)
                    inverse_root(mrsq[:, :], mneg_half[:, :]).then_inc(mm["root"], 1)
                else:
                    act.wait_ge(mm["normed"], 1)
                    for k in range(*((0, 4), (4, 8), (8, 8))[p - 1]):
                        copy(mem_hi[:, k, :], mem[:, k, :], gain[:, 5, k:k + 1]).then_inc(mm["hi"], 1)

            root(n)
            act.preload_act_table_set("natural_log_exp_and_others")
            convert_hi(act, 0, C_CK // 2 + 1)
            act.wait_ge(cr["k_out"], 1)
            for g in range(N_CROSS):
                k_high(cross, g)
            act.wait_ge(cr["q_out"], 1)
            for i in range(3):
                q_high(cross, i)
            shift_in(cross, 0)
            act.wait_ge(cr["v_out"], 1)
            for g in range(N_CROSS):
                v_high(cross, g)
            convert_hi(act, 1, C_CK // 2 + 1)
            convert_hi(act, 0, C_CK // 2 + 2)

            def co_high(k):
                act.wait_ge(cross.s["o"], 2 * k + 2)
                copy(co_hi[:, k, :], cross_o[:, k, :]).then_inc(cr["co_hi"], 1)

            attention(cross, lambda: co_high(0))
            co_high(1)
            n = norms["ffn2"]
            for p in range(PAIRS):
                for m in range(2):
                    refresh(n, 3, 2 * p + m, m, n.at(f"h_new{m}", p + 1))
            convert_hi(act, 1, C_CK // 2 + 2)
            ffn("ffn2", "final", C_FFN2, 4, True)
            root(norms["final"])

        @block.vector
        def _(dve):
            def tt(out, a, b, op):
                return nc.vector.tensor_tensor(out, a, b, op)

            def minus(out, a, hi):
                return tt(out, a, hi.bitcast(F32), ALU.subtract)

            def clear(n):
                nc.vector.memset(square_sum[:, :], 0.0).then_inc(n["summed"], 1)

            def low(n, gain_row, d):
                dve.wait_ge(*n.at("x_hi", d + 1))
                nc.vector.scalar_tensor_tensor(x_lo[:, d, :], h[:, d, :], gain[:, gain_row, bass.ds(d, 1)],
                                               x_hi[:, d, :].bitcast(F32), ALU.mult, ALU.subtract)\
                    .then_inc(n["x_lo"], 1)

            def add_squares(n, d, m):
                dve.wait_ge(*n.at("squared", d + 1))
                dve.wait_ge(*n.at("summed", d + 1))
                tt(square_sum[:, :], square_sum[:, :], squares[m][:, :], ALU.add).then_inc(n["summed"], 1)

            def refresh(n, gain_row, d, m, split=True):
                if split:
                    low(n, gain_row, d)
                add_squares(n, d, m)

            def residual(n, d, m, bank, factor):
                nc.vector.scalar_tensor_tensor(h[:, d, :], bank, factor, h[:, d, :], ALU.mult, ALU.add)\
                    .then_inc(n[f"h_new{m}"], 1)

            def half_mean(out, sums, count):
                return nc.vector.tensor_scalar(out, sums, -0.5 / count, -0.5 * EPS, ALU.mult, ALU.add)

            def refine(out, y, half, t, root, newton, factor, before=0):
                dve.wait_ge(root, before + 1)
                tt(t, y, y, ALU.mult).then_inc(newton, 1)
                dve.wait_ge(newton, 2 * before + 1)
                tt(t, t, half, ALU.mult).then_inc(newton, 1)
                dve.wait_ge(newton, 2 * before + 2)
                nc.vector.scalar_tensor_tensor(out, t, 1.5, y, ALU.add, ALU.mult).then_inc(factor, 1)
                dve.wait_ge(factor, before + 1)

            def factor(n):
                dve.wait_ge(*n.at("stat", 1))
                half_mean(neg_half[:, :], stat, D_MODEL).then_inc(n["neg_half"], 1)
                dve.wait_ge(*n.at("neg_half", 1))
                refine(row_factor[:, :], rsq[:, :], neg_half[:, :], newton[:, :], n["root"], n["newton"],
                       n["factor"], n.before["root"])

            rf = wide(row_factor[:, :])

            def feed_forward(tag, c0, j):
                f = ffns[tag]
                dve.wait_ge(chunk_used, c0 + 2 * j + 1)
                tt(gate_t[:, :, :], ps_a[:, :, :], rf, ALU.mult).then_inc(f["gate_out"], 1)
                convert_lo(dve, 0, c0 // 2 + j + 1)
                dve.wait_ge(chunk_used, c0 + 2 * j + 2)
                dve.wait_ge(f["ff_lo"], j)
                tt(up_t[:, :, :], ps_b[:, :, :], rf, ALU.mult).then_inc(f["up_out"], 1)
                dve.wait_ge(f["silu"], j + 1)
                dve.wait_ge(f["up_out"], j + 1)
                tt(up_t[:, :, :], up_t[:, :, :], silu_t[:, :, :], ALU.mult).then_inc(f["product"], 1)
                convert_lo(dve, 1, c0 // 2 + j + 1)
                dve.wait_ge(f["ff_hi"], j + 1)
                two = bass.ds(2 * j, 2)
                minus(ff_lo[:, two, :], up_t[:, :, :], ff_hi[:, two, :]).then_inc(f["ff_lo"], 1)

            def down(n, gain_row, c0, p, last, end):
                for i in range(3 if not (end and last) else 2):
                    cols = (DOWN_SPLIT[(i + 2) % 4] * COLS) if not (last and i >= 2) else CHUNK
                    convert_lo(dve, i % 2, c0 // 2 + 2 * p + i // 2 + 1, cols)
                dve.wait_ge(*n.at("tile0", p + 1))
                residual(n, 2 * p, 0, ps_c[:, 0, :], 0.5)
                dve.wait_ge(chunk_used, c0 + 4 * p + 4)
                residual(n, 2 * p + 1, 1, ps_c[:, 1, :], 0.5)
                for m in range(2):
                    refresh(n, gain_row, 2 * p + m, m, split=not end)
                if not (end and last):
                    convert_lo(dve, 1, c0 // 2 + 2 * p + 2, CHUNK if last else DOWN_SPLIT[1] * COLS)

            def ffn(tag, nxt, c0, gain_row, end):
                factor(norms[tag])
                feed_forward(tag, c0, 0)
                with dve.Fori(1, FF_PAIRS) as j:
                    feed_forward(tag, c0, j)
                n = norms[nxt]
                clear(n)
                down0 = c0 + 2 * FF_PAIRS
                with dve.Fori(0, PAIRS - 1) as p:
                    down(n, gain_row, down0, p, False, end)
                down(n, gain_row, down0, PAIRS - 1, True, end)

            n = norms["ffn1"]
            clear(n)
            dve.wait_ge(gains_loaded, 16)
            half = CHUNK // 2
            for d in range(D_TILES):
                if d == 2:
                    dve.wait_ge(first_half["hi"], 1)
                    minus(w_lo[0][:, 0:half], raw[0][:, 0:half], w_hi[0][:, 0:half]).then_inc(first_half["lo"], 1)
                if d == 4:
                    dve.wait_ge(w_hi_made, 1)
                    minus(w_lo[0][:, half:], raw[0][:, half:], w_hi[0][:, half:]).then_inc(w_lo_made, 1)
                low(n, 0, d)
            for d in range(D_TILES):
                add_squares(n, d, d % 2)
                if d == 3:
                    convert_lo(dve, 1, 0)
            ffn("ffn1", "mix", C_FFN1, 1, False)

            q0 = C_IN // 2
            dve.wait_ge(consts_loaded, 48)
            factor(norms["mix"])

            def project_out(u, b, out):
                dve.wait_ge(chunk_used, C_IN + u + 1)
                tt(out, pipes[b][:, :, :], rf, ALU.mult).then_inc(pr["out"], 1)

            def square_low(s):
                dve.wait_ge(hd["sq_hi"], s + 1)
                minus(hsq_lo[:, :, :], hsq[:, :, :], hsq_hi[:, :, :]).then_inc(hd["sq_lo"], 1)

            def f_low(half):
                s = slice(2 * half, 2 * half + 2)
                dve.wait_ge(pr["f_hi"], half + 1)
                minus(f_lo[:, s, :], f_t[:, s, :], f_hi[:, s, :]).then_inc(pr["f_lo"], 1)

            def norm_heads(s):
                dve.wait_ge(hd["stat"], s + 1)
                half_mean(hneg_half[:, :, :], ps_c[:, :, :], HEAD_DIM).then_inc(hd["neg_half"], 1)
                dve.wait_ge(hd["neg_half"], s + 1 + FREE)
                if s == 4:
                    f_low(0)
                    project_out(7, 1, f_t[:, 2:4, :])
                dve.wait_ge(hd["y_sq"], s + 1)
                tt(hnewton[:, :, :], hnewton[:, :, :], hneg_half[:, :, :], ALU.mult).then_inc(hd["t_mul"], 1)
                if s == 4:
                    f_low(1)
                dve.wait_ge(hd["t_mul"], s + 1)
                nc.vector.scalar_tensor_tensor(hrsq[:, :, :], hnewton[:, :, :], 1.5, hrsq[:, :, :],
                                               ALU.add, ALU.mult).then_inc(hd["factor"], 1)
                dve.wait_ge(hd["factor"], s + 1)
                if s >= 1:
                    dve.wait_ge(hd["mul"], 2 * s)
                nc.vector.scalar_tensor_tensor(normed[:, :, :], kq[:, 2 * s:2 * s + 2, :], head_gain[:, s:s + 1],
                                               hrsq[:, :, :], ALU.mult, ALU.mult).then_inc(hd["scaled"], 1)
                if s >= 1:
                    dve.wait_ge(hd["roped"], s)
                dve.wait_ge(hd["scaled"], s + 1)
                nc.vector.stream_shuffle(shuffled[:, :, :], normed[:, :, :], [(i + 16) % 32 for i in range(32)])\
                    .then_inc(hd["shuffled"], 1)

            project_out(0, 0, kq[:, 0:2, :])
            convert_lo(dve, 0, q0 + 1)
            square_low(0)
            dve.wait_ge(ch_hi_made, 1)
            minus(ch_lo[:, :], ch_raw[:, :], ch_hi[:, :]).then_inc(ch_lo_made, 1)
            project_out(1, 1, v_t[:, :, :])
            convert_lo(dve, 1, q0 + 1)
            for u in range(2, 6):
                project_out(u, u % 2, kq[:, 2 * u - 2:2 * u, :])
                convert_lo(dve, u % 2, q0 + u // 2 + 1)
                square_low(u - 1)
                if u == 2:
                    dve.wait_ge(pr["v_turned"], 1)
                    nc.vector.tensor_copy(v_tok[:, :, :].rearrange("p a b -> p (a b)"),
                                          ps_d[:, :, :].rearrange("p a b -> p (a b)")).then_inc(pr["v_tok"], 1)
                norm_heads(u - 2)
            project_out(6, 0, f_t[:, 0:2, :])
            convert_lo(dve, 0, q0 + 4)
            norm_heads(4)

            def k_low(at_, g):
                k1, k2, v1, v2 = at_.buffers[g % len(at_.buffers)]
                e = at_.half(g)
                dve.wait_ge(at_.s["k_hi"], 3 * (g + 1))
                minus(k1[HIGH, :], at_.k_tiles[e, g // 2, :], k1[e, :]).then_inc(at_.s["k_all"], 1)

            def v_low(at_, g):
                k1, k2, v1, v2 = at_.buffers[g % len(at_.buffers)]
                dve.wait_ge(at_.s["v_hi"], 2 * (g + 1))
                values = at_.v_rows[:, :, HEAD_DIM * g:HEAD_DIM * (g + 1)]
                minus(v2[:, :, LOW], values, v1[:, :, LOW]).then_inc(at_.s["v_all"], 1)
                minus(v2[:, :, 2 * HEAD_DIM:], values, v1[:, :, LOW]).then_inc(at_.s["v_all"], 1)

            def q_low(at_, i):
                e = at_.half(i)
                dve.wait_ge(at_.s["q_hi"], 2 * (i + 1))
                minus(q2[i % 4][LOW, :], at_.q_tiles[e, i // 2, :], q1[i % 4][e, :]).then_inc(at_.s["q_lo"], 1)

            def row_maxima(at_, i, j):
                dve.wait_ge(at_.s["s_full"], 2 * i + j + 1)
                nc.vector.tensor_reduce(row_max[:, i % 2, 2 * j:2 * j + 2], ps_a[:, :, 0:at_.keys], AX.X, ALU.max)\
                    .then_inc(at_.s["row_max"], 1)

            def diagonal(at_, i):
                dve.wait_ge(at_.s["row_max"], 2 * i + 2)
                if i >= 1:
                    dve.wait_ge(at_.s["shift"], i)
                nc.vector.scalar_tensor_tensor(diag[:, :, :], wide(ident[:, :], 4), -1.0,
                                               row_max[:, i % 2, :].unsqueeze(2).to_broadcast([P, 4, P]),
                                               ALU.mult, ALU.mult).then_inc(at_.s["diag"], 1)

            def probabilities(at_, i):
                if i >= 2:
                    dve.wait_ge(at_.s["pv"], i - 1)
                dve.wait_ge(at_.s["p"], at_.pairs * i + 1)
                nc.vector.tensor_copy(p_hi[i % 2][:, 0:2, :], at_.p_raw[:, 0:2, :]).then_inc(at_.s["p_hi0"], 1)

            def normalize(at_, i):
                e = at_.half(i)
                dve.wait_ge(at_.s["inv_denom"], i + 1)
                tt(at_.out_tiles[e, i // 2, :], pv_bank[e, :], denom[e, :], ALU.mult).then_inc(at_.s["o"], 1)

            def attention(at_, before_last):
                for i in range(at_.heads):
                    later = i + 2 < at_.heads
                    if i >= 2:
                        normalize(at_, i - 2)
                    probabilities(at_, i)
                    if later:
                        row_maxima(at_, i + 2, 0)
                    if i + 3 < at_.heads:
                        q_low(at_, i + 3)
                    if later:
                        row_maxima(at_, i + 2, 1)
                        diagonal(at_, i + 2)
                    if at_ is main and i == 1:
                        convert_lo(dve, 1, C_BRANCH // 2)
                normalize(at_, at_.heads - 2)
                before_last()
                normalize(at_, at_.heads - 1)

            for tt_ in range(4):
                dve.wait_ge(pr["y_hi"], tt_ + 1)
                minus(y_lo[:, tt_, :], y_pipes[tt_].rearrange("p a b -> p (a b)"), y_hi[:, tt_, :])\
                    .then_inc(pr["out"], 1)
            convert_lo(dve, 1, q0 + 4)
            k_low(main, 0)
            q_low(main, 0)
            row_maxima(main, 0, 0)
            row_maxima(main, 0, 1)
            diagonal(main, 0)
            q_low(main, 1)
            row_maxima(main, 1, 0)
            q_low(main, 2)
            row_maxima(main, 1, 1)
            diagonal(main, 1)
            v_low(main, 0)
            convert_lo(dve, 0, C_BRANCH // 2, BRANCH_K[0] * COLS)
            for half in range(2):
                dve.wait_ge(pr["a_hi"], half + 1)
                s = slice(2 * half, 2 * half + 2)
                minus(a_lo[:, s, :], y_pipes[half][:, :, :], a_hi[:, s, :]).then_inc(pr["a_lo"], 1)
            def split_x(tiles):
                for k in tiles:
                    dve.wait_ge(br["x_hi"], k + 1)
                    nc.vector.scalar_tensor_tensor(x_lo[:, k, :], h[:, k, :], gain[:, 1, k:k + 1],
                                                   x_hi[:, k, :].bitcast(F32), ALU.mult, ALU.subtract)\
                        .then_inc(br["x_lo"], 1)

            attention(main, lambda: split_x(range(4)))

            split_x(range(4, D_TILES))
            for half in range(2):
                s = slice(4 * half, 4 * half + 4)
                dve.wait_ge(br["o_hi"], half + 1)
                minus(o_lo[:, s, :], main.out_tiles[:, s, :], o_hi[:, s, :]).then_inc(br["o_lo"], 1)

            def branch(m, last):
                q = C_BRANCH // 2 + 2 * m
                convert_lo(dve, 0, q + 1)
                dve.wait_ge(chunk_used, 2 * q + 2)
                tt(gf_t[:, :, :], ps_b[:, :, :], rf, ALU.mult).then_inc(br["gf_out"], 1)
                convert_lo(dve, 1, q + 1)
                dve.wait_ge(br["sig_f"], m + 1)
                tt(gf_t[:, :, :], ps_a[:, :, :], gf_t[:, :, :], ALU.mult).then_inc(br["yf"], 1)
                dve.wait_ge(chunk_used, 2 * q + 3)
                tt(ga_t[:, :, :], ps_d[:, :, :], rf, ALU.mult).then_inc(br["ga_out"], 1)
                convert_lo(dve, 0, q + 2, CHUNK if last else BRANCH_K[0] * COLS)
                if not last:
                    convert_lo(dve, 1, q + 2)
                dve.wait_ge(br["sig_a"], m + 1)
                dve.wait_ge(chunk_used, 2 * q + 4)
                tt(ga_t[:, :, :], ps_c[:, :, :], ga_t[:, :, :], ALU.mult).then_inc(br["ya"], 1)
                dve.wait_ge(br["yf"], m + 1 + FREE)
                dve.wait_ge(br["ya"], m + 1 + FREE)
                tt(merged_t[:, :, :], gf_t[:, :, :], ga_t[:, :, :], ALU.add).then_inc(br["merged"], 1)
                dve.wait_ge(br["m_hi"], m + 1)
                two = bass.ds(2 * m, 2)
                minus(m_lo[:, two, :], merged_t[:, :, :], m_hi[:, two, :]).then_inc(br["m_lo"], 1)
                if last:
                    convert_lo(dve, 1, q + 2)

            with dve.Fori(0, PAIRS - 1) as m:
                branch(m, False)
            branch(PAIRS - 1, True)

            dve.wait_ge(mm["squared"], 1)
            nc.vector.tensor_reduce(msum[:, :], mem_sq[:, :, :].rearrange("p k t -> p t k"), AX.X, ALU.add)\
                .then_inc(mm["sum"], 1)
            n = norms["cross"]
            clear(n)
            for p in range(PAIRS):
                dve.wait_ge(*n.at("tile0", p + 1))
                residual(n, 2 * p, 0, ps_d[:, 0, :], 1.0)
                dve.wait_ge(chunk_used, C_OUT + p + 1)
                residual(n, 2 * p + 1, 1, ps_d[:, 1, :], 1.0)
                for m in range(2):
                    low(n, 2, 2 * p + m)
                convert_lo(dve, p % 2, C_OUT // 2 + p // 2 + 1)
                for m in range(2):
                    add_squares(n, 2 * p + m, m)
                if p == 0:
                    dve.wait_ge(mm["stat"], 1)
                    half_mean(mneg_half[:, :], ps_a[:, 0, 0:MEM_LEN], D_MODEL).then_inc(mm["neg_half"], 1)
                    dve.wait_ge(mm["neg_half"], 1)
                    refine(mrsq[:, :], mrsq[:, :], mneg_half[:, :], mnewton[:, :], mm["root"], mm["newton"],
                           mm["factor"])
                    tt(mem[:, :, :], mem[:, :, :], wide(mrsq[:, :], D_TILES), ALU.mult).then_inc(mm["normed"], 1)
                else:
                    for k in range(*((0, 4), (4, 8), (8, 8))[p - 1]):
                        dve.wait_ge(mm["hi"], k + 1)
                        nc.vector.scalar_tensor_tensor(mem_lo[:, k, :], mem[:, k, :], gain[:, 5, k:k + 1],
                                                       mem_hi[:, k, :].bitcast(F32), ALU.mult, ALU.subtract)\
                            .then_inc(mm["lo"], 1)

            factor(n)
            dve.wait_ge(chunk_used, C_CK + 1)
            nc.vector.tensor_copy(cross_k[:, :, :], ps_a[:, :, 0:MEM_LEN]).then_inc(cr["k_out"], 1)
            convert_lo(dve, 0, C_CK // 2 + 1)
            for g in range(N_CROSS):
                k_low(cross, g)
            dve.wait_ge(chunk_used, C_CQ + 1)
            tt(cross_q[:, :, :], ps_b[:, :, :], rf, ALU.mult).then_inc(cr["q_out"], 1)
            for i in range(3):
                q_low(cross, i)
            row_maxima(cross, 0, 0)
            row_maxima(cross, 0, 1)
            diagonal(cross, 0)
            row_maxima(cross, 1, 0)
            row_maxima(cross, 1, 1)
            diagonal(cross, 1)
            dve.wait_ge(chunk_used, C_CV + 1)
            nc.vector.tensor_copy(cross_v[:, :, :], ps_c[:, :, 0:MEM_LEN]).then_inc(cr["v_out"], 1)
            for g in range(N_CROSS):
                v_low(cross, g)
            convert_lo(dve, 1, C_CK // 2 + 1)
            convert_lo(dve, 0, C_CK // 2 + 2)

            def co_low(k):
                dve.wait_ge(cr["co_hi"], k + 1)
                minus(co_lo[:, k, :], cross_o[:, k, :], co_hi[:, k, :]).then_inc(cr["co_lo"], 1)

            attention(cross, lambda: co_low(0))
            co_low(1)
            n = norms["ffn2"]
            clear(n)
            for d in range(D_TILES):
                dve.wait_ge(cr["co_tile"], d + 1)
                residual(n, d, d % 2, co_banks[d], 1.0)
                low(n, 3, d)
            convert_lo(dve, 1, C_CK // 2 + 2)
            ffn("ffn2", "final", C_FFN2, 4, True)
            n = norms["final"]
            factor(n)
            for d in range(D_TILES):
                nc.vector.scalar_tensor_tensor(final_t[:, d, :], h[:, d, :], gain[:, 4, d:d + 1],
                                               row_factor[:, :], ALU.mult, ALU.mult).then_inc(out_ready, 1)

        @block.tensor
        def _(pe):
            def sum_rows(n):
                pe.wait_ge(*n.at("summed", D_TILES + 1))
                nc.tensor.matmul(stat, ones[:, :], square_sum[:, :], start=True, stop=True).then_inc(n["stat"], 1)

            def project(b, out, chunk):
                pe.wait_ge(w_lo_made, chunk + 1)
                for m in range(2):
                    for k in range(D_TILES):
                        last = product(out[:, m, :], weight(b, k, m), part(x_parts, k), k == 0, k == D_TILES - 1)
                last.then_inc(chunk_used, 1)

            def project_new(b, out, chunk, n, halves=False):
                pe.wait_ge(*((first_half["lo"], 1) if halves else (w_lo_made, chunk + 1)))
                for k in range(D_TILES):
                    pe.wait_ge(*n.at("x_lo", k + 1))
                    if halves and k == D_TILES // 2:
                        pe.wait_ge(w_lo_made, chunk + 1)
                    for m in range(2):
                        last = product(out[:, m, :], weight(b, k, m), part(x_parts, k), k == 0, k == D_TILES - 1)
                last.then_inc(chunk_used, 1)

            def ffn(tag, nxt, c0):
                f, n = ffns[tag], norms[nxt]
                project_new(0, ps_a, c0, norms[tag], halves=c0 == 0)
                sum_rows(norms[tag])
                project(1, ps_b, c0 + 1)
                with pe.Fori(1, FF_PAIRS) as j:
                    pe.wait_ge(f["gate_out"], j)
                    project(0, ps_a, c0 + 2 * j)
                    pe.wait_ge(f["up_out"], j)
                    project(1, ps_b, c0 + 2 * j + 1)
                down0 = c0 + 2 * FF_PAIRS
                with pe.Fori(0, PAIRS) as p:
                    for i in range(4):
                        pe.wait_ge(w_lo_made, down0 + 4 * p + i + 1)
                        pe.wait_ge(f["ff_lo"], FF_PAIRS - (i < 3))
                        for m in range(2):
                            if i == 0:
                                pe.wait_ge(*n.at(f"h_new{m}", p))
                            for k in range(DOWN_SPLIT[i]):
                                kt = DOWN_FIRST[i] + k
                                last = product(ps_c[:, m, :], weight(i % 2, k, m), part((ff_hi, ff_lo), kt),
                                               kt == 0, kt == FF_TILES - 1)
                            if i == 3 and m == 0:
                                last.then_inc(n["tile0"], 1)
                        last.then_inc(chunk_used, 1)

            for reader in (norm_sems["h_new0"], norm_sems["h_new1"], hd["neg_half"], br["yf"], br["ya"], br["gf_out"],
                           br["ga_out"]):
                pe.sem_inc(reader, FREE)
            pe.wait_ge(consts_set, 6)
            ffn("ffn1", "mix", C_FFN1)

            def head_sums(s):
                pe.wait_ge(hd["sq_lo"], s + 1)
                pe.wait_ge(hd["neg_half"], s + FREE)
                for m in range(2):
                    nc.tensor.matmul(ps_c[:, m, :], head_ones[:, :], hsq_hi[:, m, :], start=True, stop=False)
                    last = nc.tensor.matmul(ps_c[:, m, :], head_ones[:, :], hsq_lo[:, m, :], start=False, stop=True)
                last.then_inc(hd["stat"], 1)

            project_new(0, ps_a, C_IN, norms["mix"])
            sum_rows(norms["mix"])
            project(1, ps_b, C_IN + 1)
            pe.wait_ge(pr["out"], 1)
            project(0, ps_a, C_IN + 2)
            pe.wait_ge(consts_loaded, 48)
            pe.wait_ge(pr["out"], 2)
            for kt in range(4):
                for m in range(2):
                    last = nc.tensor.transpose(ps_d[:, kt // 2, (kt % 2) * COLS + m * P:(kt % 2) * COLS + (m + 1) * P],
                                               v_t[:, m, kt * P:(kt + 1) * P], ident[:, :])
            last.then_inc(pr["v_turned"], 1)
            head_sums(0)
            with pe.Fori(0, 2) as t:
                for b in (1, 0):
                    s = 2 * t + 2 - b
                    pe.wait_ge(pr["out"], s + 1)
                    project(b, pipes[b], C_IN + 2 + s)
                    head_sums(s)
            pe.wait_ge(pr["out"], 6)
            project(1, ps_b, C_IN + 7)

            def scores(at_, i, j):
                k1, k2, v1, v2 = at_.kv(i)
                if j == 0:
                    pe.wait_ge(at_.s["k_all"], i // at_.per_kv + 1)
                    pe.wait_ge(at_.s["q_hi"], 2 * (i + 1))
                if 2 * i + j >= 1:
                    pe.wait_ge(at_.s["row_max"], 2 * i + j)
                for t in range(2):
                    s = slice((2 * j + t) * P, (2 * j + t + 1) * P)
                    last = nc.tensor.matmul(ps_a[:, t, 0:at_.keys], q1[i % 4][:, s], k1[:, :], start=True, stop=True)
                last.then_inc(at_.s["s_full"], 1)

            def shift(at_, i):
                pe.wait_ge(at_.s["diag"], i + 1)
                if i >= 1:
                    pe.wait_ge(at_.s["shift_in"], i)
                nc.tensor.matmul(shift_bank, pick[:, :], diag[:, :, :], start=True, stop=True)\
                    .then_inc(at_.s["shift"], 1)

            def turned_scores(at_, i):
                k1, k2, v1, v2 = at_.kv(i)
                pe.wait_ge(at_.s["shift_in"], i + 1)
                pe.wait_ge(at_.s["q_lo"], i + 1)
                for j in range(at_.pairs):
                    if at_ is main and i == 0:
                        pe.wait_ge(pr["a_lo"], j + 1)
                    if at_.pairs * i + j >= 2:
                        pe.wait_ge(at_.s["p"], at_.pairs * i + j - 1)
                    for t in range(2):
                        s = slice((2 * j + t) * P, (2 * j + t + 1) * P)
                        bank = st_pair(at_, i, j)[:, t, :]
                        nc.tensor.matmul(bank, k1[:, s], q1[i % 4][:, :], start=True, stop=False)
                        last = nc.tensor.matmul(bank, k2[:, s], q2[i % 4][:, :], start=False, stop=True)
                    last.then_inc(at_.s["st_full"], 1)

            def values(at_, i, j):
                k1, k2, v1, v2 = at_.kv(i)
                e = slice(HEAD_DIM * (i % 2), HEAD_DIM * (i % 2) + P)
                if j == 0:
                    pe.wait_ge(at_.s["v_all"], 2 * (i // at_.per_kv) + 2)
                    if i >= 1:
                        pe.wait_ge(at_.s["o"], i)
                pe.wait_ge(at_.s["p_lo"], at_.pairs * i + j + 1)
                for kt in (2 * j, 2 * j + 1):
                    last = product(pv_bank, (v1[:, kt, e], v2[:, kt, e]), part((p_hi[i % 2], p_lo[i % 2]), kt),
                                   kt == 0, kt == 2 * at_.pairs - 1)
                if j == at_.pairs - 1:
                    last.then_inc(at_.s["pv"], 1)

            def attention(at_, before_last):
                pe.wait_ge(at_.s["consts"], 4 * len(at_.buffers))
                for i in range(at_.heads):
                    turned_scores(at_, i)
                    if i + 1 < at_.heads:
                        shift(at_, i + 1)
                    for j in range(2):
                        if i + 2 < at_.heads:
                            scores(at_, i + 2, j)
                        if i >= 1 and j < at_.pairs:
                            values(at_, i - 1, j)
                before_last()
                for j in range(at_.pairs):
                    values(at_, at_.heads - 1, j)

            pe.wait_ge(ch_lo_made, 1)
            pe.wait_ge(pr["f_lo"], 2)
            pe.wait_ge(hd["neg_half"], 5 + FREE)
            for tt_ in range(4):
                for g in range(GROUPS):
                    last = product(y_pipes[tt_][:, g // 2, (g % 2) * COLS:(g % 2 + 1) * COLS],
                                   part((f_hi, f_lo), g, slice(tt_ * P, (tt_ + 1) * P)), (ch_hi[:, :], ch_lo[:, :]),
                                   True, True)
                last.then_inc(pr["y_full"], 1)
            between = {(0, 1): lambda: scores(main, 0, 0),
                       (0, 2): lambda: scores(main, 0, 1),
                       (0, 3): lambda: shift(main, 0),
                       (1, 0): lambda: scores(main, 1, 0),
                       (1, 1): lambda: scores(main, 1, 1)}
            for i in range(2):
                pe.wait_ge(w_lo_made, C_DFT + i + 1)
                for g in range(GROUPS):
                    for tt_ in range(4):
                        if i == 0:
                            pe.wait_ge(pr["out"], 9 + tt_ if g % 2 == 0 or g // 2 == 0 else 12)
                        s = slice(tt_ * TOKENS, (tt_ + 1) * TOKENS)
                        last = product(y_pipes[g // 2][:, g % 2, :],
                                       part((y_hi, y_lo), tt_, slice(g * COLS + i * P, g * COLS + (i + 1) * P)),
                                       (w_hi[i][:, s], w_lo[i][:, s]), i == 0 and tt_ == 0, i == 1 and tt_ == 3)
                    if g == GROUPS - 1 and i == 0:
                        last.then_inc(chunk_used, 1)
                    if i == 1 and g % 2 == 1:
                        last.then_inc(pr["a_full"], 1)
                    if (i, g) in between:
                        between[i, g]()
            pe.drain().then_inc(chunk_used, 1)

            def first_fourier_branch():
                pe.wait_ge(main.s["row_max"], 2 * N_HEADS)
                fourier_branch(C_BRANCH)

            def fourier_branch(c):
                pe.wait_ge(w_lo_made, c + 1)
                for t in range(2):
                    for k in range(GROUPS):
                        last = product(ps_a[:, t, :], weight(0, k, t), part((a_hi, a_lo), k), k == 0, k == GROUPS - 1)
                last.then_inc(chunk_used, 1)

            attention(main, first_fourier_branch)

            def branch(m, last_turn):
                c = C_BRANCH + 4 * m
                pe.wait_ge(w_lo_made, c + 2)
                pe.wait_ge(br["gf_out"], m + FREE)
                for t in range(2):
                    for k in range(D_TILES):
                        pe.wait_ge(br["x_lo"], k + 1)
                        last = product(ps_b[:, t, :], weight(1, k, t), part(x_parts, k), k == 0, k == D_TILES - 1)
                last.then_inc(chunk_used, 1)
                pe.wait_ge(br["ga_out"], m + FREE)
                project(0, ps_d, c + 2)
                pe.wait_ge(w_lo_made, c + 4)
                pe.wait_ge(br["ya"], m + FREE)
                for t in range(2):
                    for k in range(D_TILES):
                        pe.wait_ge(br["o_lo"], k // 4 + 1)
                        last = product(ps_c[:, t, :], weight(1, k, t), part((o_hi, o_lo), k), k == 0, k == D_TILES - 1)
                last.then_inc(chunk_used, 1)
                if not last_turn:
                    pe.wait_ge(br["yf"], m + 1 + FREE)
                    fourier_branch(c + 4)

            pe.wait_ge(main.s["p"], 2 * N_HEADS)
            with pe.Fori(0, PAIRS - 1) as m:
                branch(m, False)
            branch(PAIRS - 1, True)

            n = norms["cross"]
            pe.wait_ge(br["ga_out"], PAIRS + FREE)

            def out_pair(p, b):
                pe.wait_ge(w_lo_made, C_OUT + p + 1)
                for ks in (range(D_TILES - 2), range(D_TILES - 2, D_TILES)):
                    for m in range(2):
                        if ks[0] == 0:
                            pe.wait_ge(*n.at(f"h_new{m}", p))
                        if m == 0:
                            pe.wait_ge(br["m_lo"], PAIRS - (ks[0] == 0))
                        for k in ks:
                            last = product(ps_d[:, m, :], weight(b, k, m), part((m_hi, m_lo), k),
                                           k == 0, k == D_TILES - 1)
                        if m == 0 and ks[0] > 0:
                            last.then_inc(n["tile0"], 1)
                last.then_inc(chunk_used, 1)

            out_pair(0, 0)
            pe.wait_ge(mm["sum"], 1)
            pe.wait_ge(br["yf"], PAIRS + FREE)
            nc.tensor.matmul(ps_a[:, 0, 0:MEM_LEN], ones[:, :], msum[:, :], start=True, stop=True)\
                .then_inc(mm["stat"], 1)
            for p in range(1, PAIRS):
                out_pair(p, p % 2)

            pe.wait_ge(mm["lo"], D_TILES)
            pe.wait_ge(w_lo_made, C_CK + 1)
            pe.wait_ge(mm["factor"], 1)
            for m in range(2):
                for k in range(D_TILES):
                    last = product(ps_a[:, m, 0:MEM_LEN], weight(0, k, m), part((mem_hi, mem_lo), k),
                                   k == 0, k == D_TILES - 1)
            last.then_inc(chunk_used, 1)
            sum_rows(n)
            pe.wait_ge(br["gf_out"], PAIRS + FREE)
            project_new(1, ps_b, C_CQ, n)
            pe.wait_ge(w_lo_made, C_CV + 1)
            pe.wait_ge(br["ya"], PAIRS + FREE)

            def memory_values(mt):
                for k in range(D_TILES):
                    s = slice(k * COLS, (k + 1) * COLS)
                    last = product(ps_c[:, mt, 0:COLS], part((mem_hi, mem_lo), k, slice(mt * P, (mt + 1) * P)),
                                   (w_hi[0][:, s], w_lo[0][:, s]), k == 0, k == D_TILES - 1)
                return last

            memory_values(0)
            pe.wait_ge(cr["k_out"], 1)
            scores(cross, 0, 0)
            scores(cross, 0, 1)
            memory_values(1).then_inc(chunk_used, 1)
            shift(cross, 0)
            scores(cross, 1, 0)
            scores(cross, 1, 1)
            pe.wait_ge(cr["q_out"], 1)
            pe.wait_ge(cr["v_out"], 1)
            n = norms["ffn2"]

            def co(k, tiles):
                pe.wait_ge(cr["co_lo"], k + 1)
                for d in tiles:
                    last = product(co_banks[d], weight(1, k, d, D_MODEL), part((co_hi, co_lo), k), k == 0, k == 1)
                    if k == 1:
                        last.then_inc(cr["co_tile"], 1)

            def co_early():
                pe.wait_ge(w_lo_made, C_CO + 1)
                pe.wait_ge(cross.s["row_max"], 2 * N_CROSS)
                pe.wait_ge(cross.s["p"], N_CROSS - 1)
                co(0, range(4))

            attention(cross, co_early)
            pe.wait_ge(cross.s["p"], N_CROSS)
            co(0, range(4, 6))
            pe.wait_ge(cross.s["o"], N_CROSS)
            co(0, range(6, D_TILES))
            co(1, range(D_TILES))
            pe.drain().then_inc(chunk_used, 1)
            pe.wait_ge(*n.at("h_new1", 1))
            ffn("ffn2", "final", C_FFN2)
            sum_rows(norms["final"])


def column_chunks(w):
    K, N = w.shape
    return w.reshape(K // P, P, N // COLS, COLS).transpose(2, 1, 0, 3).reshape(N // COLS, P, K // P * COLS)


def down_chunks(w):
    return [c[:, f * COLS:(f + k) * COLS] for c in column_chunks(w) for f, k in zip(DOWN_FIRST, DOWN_SPLIT)]


def weight_stream(a):
    def gate_up(gate, up):
        return [c for pair in zip(column_chunks(gate), column_chunks(up)) for c in pair]

    q_w, kv_w, f_w = N_HEADS * HEAD_DIM, N_KV * HEAD_DIM, GROUPS * P
    w_in = a["w_in"][0]
    edges = np.cumsum([0, q_w, kv_w, kv_w, f_w, D_MODEL, D_MODEL])
    q, k, v, f, gate_f, gate_a = (column_chunks(w_in[:, s:e]) for s, e in zip(edges[:-1], edges[1:]))
    t = np.arange(TOKENS)
    angle = 2 * np.pi * (np.outer(t, t) % TOKENS) / TOKENS
    dft = [np.cos(angle), -np.sin(angle)]
    dft = [m.astype(np.float32).reshape(4, P, TOKENS).transpose(1, 0, 2).reshape(P, CHUNK) for m in dft]
    branches = zip(column_chunks(a["w_fourier_branch"][0]), gate_f, gate_a, column_chunks(a["w_attn_branch"][0]))
    w_co = a["w_co"][0].reshape(2, P, D_MODEL).transpose(1, 0, 2).reshape(P, CHUNK)
    chunks = [*gate_up(a["w1_gate"][0], a["w1_up"][0]), *down_chunks(a["w1_down"][0]),
              *k, *v, *q, *f, *dft,
              *(c for four in branches for c in four), *column_chunks(a["w_out"][0]),
              *column_chunks(a["w_ck"][0]), *column_chunks(a["w_cq"][0]), *column_chunks(a["w_cv"][0]), w_co,
              *gate_up(a["w2_gate"][0], a["w2_up"][0]), *down_chunks(a["w2_down"][0])]
    out = np.zeros((N_CHUNKS, P, CHUNK), np.float32)
    assert len(chunks) == N_CHUNKS
    for n, c in enumerate(chunks):
        out[n, :, :c.shape[1]] = c
    return out


def feature_tiles(x):
    return np.ascontiguousarray(x.reshape(x.shape[0], -1, P).transpose(2, 1, 0))


def rope_tables():
    f32 = np.float32
    t = np.arange(TOKENS)
    inv = f32(1.0) / (f32(10000.0) ** (np.arange(0, 32, 2, dtype=f32) / f32(32)))
    d = np.arange(P) % HEAD_DIM
    position = np.where((d < 32)[:, None], (t // 64)[None, :], (t % 64)[None, :]).astype(f32)
    angle = position * inv[d % 16][:, None]
    sign = np.where(d % 32 < 16, -1.0, 1.0)[:, None]
    return np.stack([np.cos(angle), sign * np.sin(angle)]).astype(f32)


def kernel(**inputs):
    import concourse.bacc as _bacc
    from concourse.bass_utils import run_bass_kernel_spmd as _run

    a = {name: np.asarray(value) for name, value in inputs.items()}
    gains = np.stack([a["g_ffn1"][0], a["g_mix"][0], a["g_cross"][0], a["g_ffn2"][0], a["g_final"], a["g_mem"][0]])
    heads = np.stack([a["k_gain"][0]] + [a["q_gain"][0]] * 7, axis=1)
    c = np.arange(P)
    angle = 2 * np.pi * (np.outer(c, c) % P) / P
    channel = np.concatenate([np.cos(angle), np.sin(angle)], axis=1) / np.sqrt(TOKENS * P)
    arrays = {
        "xT": feature_tiles(a["x"][0]),
        "memT": feature_tiles(a["mem"][0]),
        "stream": weight_stream(a),
        "gains": np.ascontiguousarray(gains.reshape(6, D_TILES, P).transpose(2, 0, 1)),
        "head_gains": np.ascontiguousarray(np.concatenate([heads, heads])),
        "rope": rope_tables(),
        "channel_dft": channel.astype(np.float32),
        "identity": np.eye(P, dtype=np.float32),
    }
    nc = _bacc.Bacc("TRN2", target_bir_lowering=False, num_devices=1)
    args = [nc.dram_tensor(name, x.shape, F32, kind="ExternalInput").ap() for name, x in arrays.items()]
    out = nc.dram_tensor("outT", (P, D_TILES, TOKENS), F32, kind="ExternalOutput").ap()
    encoder_block(nc, *args, out)
    r = _run(nc, [arrays], core_ids=[0])
    outT = r.results[0]["outT"]
    return outT.transpose(2, 1, 0).reshape(1, TOKENS, D_MODEL)
```

```python
import functools
from contextlib import ExitStack

import numpy as np

import concourse.bass as bass
from concourse import mybir

ACT = mybir.ActivationFunctionType
ALU = mybir.AluOpType
AX = mybir.AxisListType
F32 = mybir.dt.float32
F32R = mybir.dt.float32r

P = 128
TOKENS = 512
D_MODEL = 1024
D_TILES = D_MODEL // P
MEM_LEN = 256
HEAD_DIM = 64
N_HEADS = 16
N_KV = 4
N_CROSS = 4
D_FF = 2816
FF_TILES = D_FF // P
FF_PAIRS = FF_TILES // 2
PAIRS = D_TILES // 2
GROUPS = 4
EPS = 1e-6
SCALE = HEAD_DIM ** -0.5
COLS = 2 * P
DVE_TILES = 5
CHUNK = D_TILES * COLS
DOWN_SPLIT = (6, 6, 5, 5)
DOWN_FIRST = (0, 6, 12, 17)
BRANCH_K = (4, 8, 8, 8)

C_FFN1 = 0
C_DOWN1 = C_FFN1 + 2 * FF_PAIRS
C_IN = C_DOWN1 + 4 * PAIRS
C_DFT = C_IN + 8
C_BRANCH = C_DFT + 2
C_OUT = C_BRANCH + 4 * PAIRS
C_CK = C_OUT + PAIRS
C_CQ, C_CV, C_CO = C_CK + 1, C_CK + 2, C_CK + 3
C_FFN2 = C_CO + 1
C_DOWN2 = C_FFN2 + 2 * FF_PAIRS
N_CHUNKS = C_DOWN2 + 4 * PAIRS

KIB = 1024


def encoder_block(nc, xT, memT, stream, gains, head_gains, rope, channel_dft, identity, outT):
    with ExitStack() as ctx:
        base = -(-nc.sbuf_base // 32) * 32

        def at(name, shape, kib, dt=F32):
            return nc.alloc_sbuf_tensor_at(name, shape, dt, offset=base + int(kib * KIB))

        def sem(name):
            return ctx.enter_context(nc.semaphore(name))

        def psum(name):
            return ctx.enter_context(nc.psum_tensor(name, [P, 2, TOKENS], F32))

        h = at("h", [P, D_TILES, TOKENS], 0)
        raw = [at(f"raw{b}", [P, CHUNK], 16 + 8 * b) for b in range(2)]
        w_hi = [at(f"w_hi{b}", [P, CHUNK], 32 + 8 * b, F32R) for b in range(2)]
        w_lo = [at(f"w_lo{b}", [P, CHUNK], 48 + 8 * b, F32R) for b in range(2)]
        row_factor = at("row_factor", [P, TOKENS], 64)
        square_sum = at("square_sum", [P, TOKENS], 66)
        SM = 68
        ident = at("ident", [P, P], SM)
        ones = at("ones", [P, P], SM + .5)
        head_ones = at("head_ones", [P, P], SM + 1, F32R)
        pick = at("pick", [P, P], SM + 1.5, F32R)
        gain = at("gain", [P, 6, D_TILES], SM + 2.5)
        head_gain = at("head_gain", [P, 8], SM + 2.75)
        ch_raw = at("ch_raw", [P, 2 * P], SM + 3)
        ch_hi = at("ch_hi", [P, 2 * P], SM + 4, F32R)
        ch_lo = at("ch_lo", [P, 2 * P], SM + 5, F32R)
        row_max = at("row_max", [P, 2, 4], SM + 6)
        T = SM + 6.25
        newton = at("newton", [P, TOKENS], T + 2)
        neg_half = at("neg_half", [P, TOKENS], T + 4)
        rsq = at("rsq", [P, TOKENS], T + 6)
        squares = [at(f"squares{b}", [P, TOKENS], T + 8 + 2 * b) for b in range(2)]
        gate_t = at("gate_t", [P, 2, TOKENS], T)
        silu_t = at("silu_t", [P, 2, TOKENS], T + 4)
        up_t = at("up_t", [P, 2, TOKENS], T + 8)
        V = T + 12
        x_hi = at("x_hi", [P, D_TILES, TOKENS], V, F32R)
        x_lo = at("x_lo", [P, D_TILES, TOKENS], V + 16, F32R)
        ff_hi = at("ff_hi", [P, FF_TILES, TOKENS], V + 32, F32R)
        ff_lo = at("ff_lo", [P, FF_TILES, TOKENS], V + 76, F32R)
        kq = at("kq", [P, 10, TOKENS], V + 32)
        v_t = at("v_t", [P, 2, TOKENS], V + 52)
        f_t = at("f_t", [P, GROUPS, TOKENS], V + 56)
        f_lo = at("f_lo", [P, GROUPS, TOKENS], V + 56, F32R)
        f_hi = at("f_hi", [P, GROUPS, TOKENS], V + 64, F32R)
        v_tok = at("v_tok", [P, 4, N_KV * HEAD_DIM], V + 82)
        rope_cos = at("rope_cos", [P, TOKENS], V + 96)
        rope_sin = at("rope_sin", [P, TOKENS], V + 98)
        hsq = at("hsq", [P, 2, TOKENS], V + 100)
        hsq_hi = at("hsq_hi", [P, 2, TOKENS], V + 104, F32R)
        hsq_lo = at("hsq_lo", [P, 2, TOKENS], V + 108, F32R)
        hneg_half = at("hneg_half", [P, 2, TOKENS], V + 112)
        hrsq = at("hrsq", [P, 2, TOKENS], V + 116)
        hnewton = at("hnewton", [P, 2, TOKENS], T)
        shuffled = at("shuffled", [P, 2, TOKENS], T + 4)
        rotated = at("rotated", [P, 2, TOKENS], T + 8)
        normed = at("normed", [P, 2, TOKENS], V + 86)
        mem = at("mem", [P, D_TILES, MEM_LEN], V + 96)
        mem_sq = at("mem_sq", [P, D_TILES, MEM_LEN], V + 64)
        mem_hi = at("mem_hi", [P, D_TILES, MEM_LEN], V + 72, F32R)
        mem_lo = at("mem_lo", [P, D_TILES, MEM_LEN], V + 80, F32R)
        msum = at("msum", [P, MEM_LEN], V + 92)
        mneg_half = at("mneg_half", [P, MEM_LEN], V + 93)
        mrsq = at("mrsq", [P, MEM_LEN], V + 94)
        mnewton = at("mnewton", [P, MEM_LEN], V + 95)
        cross_k = at("cross_k", [P, 2, MEM_LEN], V + 60)
        cross_v = at("cross_v", [P, 2, MEM_LEN], V + 62)
        y_hi = at("y_hi", [P, 4, 2 * TOKENS], V, F32R)
        y_lo = at("y_lo", [P, 4, 2 * TOKENS], V + 16, F32R)
        a_hi = at("a_hi", [P, GROUPS, TOKENS], V + 96, F32R)
        a_lo = at("a_lo", [P, GROUPS, TOKENS], V + 64, F32R)
        p_hi = [at(f"p_hi{b}", [P, 4, TOKENS], V + 8 * b, F32R) for b in range(2)]
        p_lo = [at(f"p_lo{b}", [P, 4, TOKENS], V + 16 + 8 * b, F32R) for b in range(2)]
        p_main = at("p_main", [P, 4, TOKENS], V + 56)
        p_cross = at("p_cross", [P, 2, TOKENS], V + 72)
        diag = at("diag", [P, 4, P], V + 94, F32R)
        q_at = (V + 52, V + 90, V + 116, T)
        q1 = [at(f"q1_{b}", [P, TOKENS], q_at[b], F32R) for b in range(4)]
        q2 = [at(f"q2_{b}", [P, TOKENS], q_at[b] + 2, F32R) for b in range(4)]

        def kv_buffer(tag, kib, keys):
            v_shape = [P, keys // P, 3 * HEAD_DIM]
            v_kib = keys // P * 0.75
            return (at(f"k1_{tag}", [P, keys], kib, F32R), at(f"k2_{tag}", [P, keys], kib + keys / 256, F32R),
                    at(f"v_hi_{tag}", v_shape, kib + keys / 128, F32R),
                    at(f"v_lo_{tag}", v_shape, kib + keys / 128 + v_kib, F32R))

        kv_main = [kv_buffer(f"m{b}", V + 72 + 32 * b, TOKENS) for b in range(2)]
        kv_cross = [kv_buffer(f"c{b}", V + 96 + 5 * b, MEM_LEN) for b in range(N_CROSS)]
        denom = at("denom", [P, TOKENS], T + 4)
        cross_q = at("cross_q", [P, 2, TOKENS], V + 32)
        cross_o = at("cross_o", [P, 2, TOKENS], V + 36)
        co_hi = at("co_hi", [P, 2, TOKENS], V + 80, F32R)
        co_lo = at("co_lo", [P, 2, TOKENS], V + 84, F32R)
        o_hi = at("o_hi", [P, D_TILES, TOKENS], V + 72, F32R)
        o_lo = at("o_lo", [P, D_TILES, TOKENS], V + 104, F32R)
        m_hi = at("m_hi", [P, D_TILES, TOKENS], V + 32, F32R)
        m_lo = at("m_lo", [P, D_TILES, TOKENS], V + 48, F32R)
        gf_t = at("gf_t", [P, 2, TOKENS], T)
        ga_t = at("ga_t", [P, 2, TOKENS], T + 4)
        merged_t = at("merged_t", [P, 2, TOKENS], T + 8)
        final_t = at("final_t", [P, D_TILES, TOKENS], V)

        ps_a, ps_b, ps_c, ps_d = (psum(f"ps_{c}") for c in "abcd")
        stat = ps_d[:, 1, :]

        x_loaded = [sem(f"x_loaded{i}") for i in range(PAIRS)]
        gains_loaded = sem("gains_loaded")
        consts_loaded = sem("consts_loaded")
        rope_loaded = sem("rope_loaded")
        mem_loaded = sem("mem_loaded")
        first_half = {step: sem(f"first_half_{step}") for step in ("loaded", "hi", "lo")}
        stored = sem("stored")
        consts_set = sem("consts_set")
        ch_hi_made, ch_lo_made = sem("ch_hi_made"), sem("ch_lo_made")
        raw_loaded = [sem(f"raw_loaded{b}") for b in range(2)]
        w_hi_made = sem("w_hi_made")
        w_lo_made = sem("w_lo_made")
        chunk_used = sem("chunk_used")

        FREE = 1

        def sems(tag, *steps):
            return {step: sem(f"{tag}_{step}") for step in steps}

        norm_sems = sems("norm", "h_new0", "h_new1", "tile0", "x_hi", "squared", "x_lo", "summed", "stat",
                         "neg_half", "root", "newton", "factor")
        norm_adds = {"h_new0": PAIRS, "h_new1": PAIRS, "tile0": PAIRS, "x_hi": D_TILES, "squared": D_TILES,
                     "x_lo": D_TILES, "summed": D_TILES + 1, "newton": 2}

        class Norm:
            def __init__(self, earlier, earlier_updates, earlier_tile0):
                self.before = {step: norm_adds.get(step, 1) * earlier for step in norm_sems}
                self.before["h_new0"] = self.before["h_new1"] = PAIRS * earlier_updates + FREE
                self.before["tile0"] = PAIRS * earlier_tile0

            def __getitem__(self, step):
                return norm_sems[step]

            def at(self, step, value):
                return norm_sems[step], value + self.before[step]

        norms = {"ffn1": Norm(0, 0, 0), "mix": Norm(1, 0, 0), "cross": Norm(2, 1, 1), "ffn2": Norm(3, 2, 2),
                 "final": Norm(4, 3, 2)}
        ffns = {tag: sems(tag, "gate_out", "silu", "up_out", "product", "ff_hi", "ff_lo")
                for tag in ("ffn1", "ffn2")}
        pr = sems("proj", "out", "v_turned", "v_tok", "y_full", "y_hi", "f_hi", "f_lo", "a_full",
                  "a_hi", "a_lo")
        hd = sems("head", "sq", "sq_hi", "sq_lo", "stat", "neg_half", "root", "y_sq", "t_mul", "factor",
                  "scaled", "shuffled", "mul", "roped")
        mm = sems("mem", "squared", "sum", "stat", "neg_half", "root", "newton", "factor", "normed", "hi", "lo")
        br = sems("branch", "o_hi", "o_lo", "x_hi", "x_lo", "gf_out", "ga_out", "sig_f", "sig_a", "yf", "ya",
                  "merged", "m_hi", "m_lo")
        cr = sems("cr", "k_out", "q_out", "v_out", "co_hi", "co_lo", "co_tile")
        out_ready, gained, pool_out = sem("out_ready"), sem("gained"), sem("pool_out")

        def wide(ap, n=2):
            return ap.unsqueeze(1).to_broadcast([P, n, ap.shape[1]])

        def wait_apart(engine, semaphore, value):
            engine.wait_ge(semaphore, value)
            engine.wait_ge(semaphore, 1)

        def convert_hi(act, b, q, cols=CHUNK, first=False):
            act.wait_ge(raw_loaded[b], 16 * q + 16)
            if not first:
                act.wait_ge(chunk_used, 2 * q + b - 1)
            nc.scalar.activation(w_hi[b][:, 0:cols], raw[b][:, 0:cols], ACT.Copy).then_inc(w_hi_made, 1)

        def convert_lo(dve, b, q, cols=CHUNK):
            dve.wait_ge(w_hi_made, 2 * q + b + 1)
            nc.vector.tensor_tensor(w_lo[b][:, 0:cols], raw[b][:, 0:cols],
                                    w_hi[b][:, 0:cols].bitcast(F32), ALU.subtract).then_inc(w_lo_made, 1)

        def product(out, w, x, start, stop):
            nc.tensor.matmul(out, w[0], x[0], start=start, stop=False)
            nc.tensor.matmul(out, w[0], x[1], start=False, stop=False)
            return nc.tensor.matmul(out, w[1], x[0], start=False, stop=stop)

        def weight(b, k, m, cols=COLS):
            s = slice(k * cols + m * P, k * cols + (m + 1) * P)
            return w_hi[b][:, s], w_lo[b][:, s]

        def part(pair, k, cols=slice(None)):
            return pair[0][:, k, cols], pair[1][:, k, cols]

        x_parts = (x_hi, x_lo)
        pipes = (ps_a, ps_b)
        y_pipes = (ps_c, ps_d, ps_a, ps_b)
        dft_pipes = (ps_c, ps_b)
        out_pipes = (ps_d, ps_b)
        co_banks = [ps[:, m, :] for ps in (ps_a, ps_b, ps_c, ps_d) for m in range(2)]

        class Attention:
            def __init__(self, tag, heads, keys, q_tiles, out_tiles, k_tiles, v_rows, buffers, per_kv, p_raw):
                self.heads, self.keys, self.pairs = heads, keys, keys // (2 * P)
                self.steps = 2 * keys // TOKENS
                self.q_tiles, self.out_tiles, self.k_tiles, self.v_rows = q_tiles, out_tiles, k_tiles, v_rows
                self.buffers, self.per_kv, self.p_raw = buffers, per_kv, p_raw
                self.s = sems(tag, "consts", "k_hi", "k_all", "v_hi", "v_all", "q_hi", "q_hi2", "q_lo", "s_full",
                              "row_max", "diag", "shift", "shift_in", "st_full", "p", "p_hi0", "p_hi1",
                              "p_lo", "p_lo0", "pv", "log_denom", "inv_denom", "o")

            def kv(self, i):
                return self.buffers[i // self.per_kv % len(self.buffers)]

            def half(self, i):
                return slice(HEAD_DIM * (i % 2), HEAD_DIM * (i % 2) + HEAD_DIM)

        main = Attention("main", N_HEADS, TOKENS, kq[:, 2:10, :], kq[:, 2:10, :], kq[:, 0:2, :], v_tok[:, :, :],
                         kv_main, N_HEADS // N_KV, p_main)
        cross = Attention("crossatt", N_CROSS, MEM_LEN, cross_q[:, :, :], cross_o[:, :, :], cross_k[:, :, :],
                          cross_v[:, :, :], kv_cross, 1, p_cross)
        LOW, HIGH = slice(0, HEAD_DIM), slice(HEAD_DIM, P)
        pv_bank, shift_bank = ps_d[:, 0, :], ps_d[:, 1, :]

        def score_tiles(at_, j):
            n = 2 * TOKENS // at_.keys
            return range(n * j, n * j + n), ps_a.rearrange("p a (c k) -> p (a c) k", k=at_.keys)

        def st_pair(at_, i, j):
            return dft_pipes[j if at_.pairs == 2 else 1 - i % 2]

        block = ctx.enter_context(nc.Block())

        @block.sync
        def _(sp):
            def load(b, q, cols=CHUNK, first=False):
                if not first:
                    sp.wait_ge(w_lo_made, 2 * q + b - 1)
                sp.dma_start(raw[b][:, 0:cols], stream[2 * q + b, :, 0:cols]).then_inc(raw_loaded[b], 16)

            def ffn_stream(c0):
                with sp.Fori(1, FF_PAIRS + 1) as j:
                    for b in range(2):
                        load(b, c0 // 2 + j)
                down = (c0 + 2 * FF_PAIRS) // 2
                for i in (2, 3):
                    load(i % 2, down + 1, DOWN_SPLIT[i] * COLS)
                with sp.Fori(1, PAIRS) as p:
                    for i in range(4):
                        load(i % 2, down + 2 * p + i // 2, DOWN_SPLIT[i] * COLS)

            half = CHUNK // 2
            sp.dma_start(raw[0][:, 0:half], stream[0, :, 0:half]).then_inc(first_half["loaded"], 16)
            for p in range(PAIRS):
                sp.dma_start(h[:, 2 * p:2 * p + 2, :], xT[:, 2 * p:2 * p + 2, :]).then_inc(x_loaded[p], 16)
                if p == 1:
                    sp.dma_start(raw[0][:, half:], stream[0, :, half:]).then_inc(raw_loaded[0], 16)
            load(1, 0, first=True)
            ffn_stream(C_FFN1)
            with sp.Fori(C_IN // 2, C_BRANCH // 2) as q:
                for b in range(2):
                    load(b, q)
            with sp.Fori(0, PAIRS) as m:
                for i in range(4):
                    load(i % 2, C_BRANCH // 2 + 2 * m + i // 2, BRANCH_K[i] * COLS)
            sp.wait_ge(chunk_used, C_BRANCH + 4 * (PAIRS - 1) + 1)
            sp.dma_start(mem[:, :, :], memT).then_inc(mem_loaded, 16)
            with sp.Fori(C_OUT // 2, C_FFN2 // 2 + 1) as q:
                for b in range(2):
                    load(b, q)
            ffn_stream(C_FFN2)
            for d in (0, 5, 1, 2, 6, 3, 4, 7):
                if d < DVE_TILES:
                    sp.wait_ge(out_ready, d + 1)
                else:
                    sp.wait_ge(pool_out, d - DVE_TILES + 1)
                sp.dma_start(outT[:, d, :], final_t[:, d, :]).then_inc(stored, 16)
            sp.wait_ge(stored, 16 * D_TILES)

        @block.gpsimd
        def _(pool):
            def fill_all(semaphore, fills, before=0):
                for n, (out, value) in enumerate(fills):
                    if before + n:
                        pool.wait_ge(semaphore, before + n)
                    nc.gpsimd.memset(out.bitcast(F32), value).then_inc(semaphore, 1)

            fill_all(consts_set, [(head_ones[:, :], 0.0), (pick[:, :], 0.0),
                                  (ones[:, :], 1.0), (head_ones[LOW, LOW], 1.0), (head_ones[HIGH, HIGH], 1.0),
                                  (pick[:, 64:96], 1.0)])

            def constants(at_, buffers, before=0):
                fill_all(at_.s["consts"], [fill for k1, k2, v1, v2 in buffers for fill in (
                    (k2[HIGH, :], 0.0), (k2[64:65, :], 1.0),
                    (v1[:, :, HIGH], 1.0), (v2[:, :, HIGH], 0.0))], before)

            pool.wait_ge(rope_loaded, 32)
            constants(main, kv_main[:1])
            with pool.Fori(0, 5) as s:
                pool.wait_ge(hd["shuffled"], s + 1)
                nc.gpsimd.tensor_tensor(shuffled[:, :, :], shuffled[:, :, :], wide(rope_sin[:, :]), ALU.mult)\
                    .then_inc(hd["mul"], 1)
                nc.gpsimd.tensor_tensor(rotated[:, :, :], normed[:, :, :], wide(rope_cos[:, :]), ALU.mult)\
                    .then_inc(hd["mul"], 1)
                wait_apart(pool, hd["mul"], 2 * s + 2)
                nc.gpsimd.tensor_tensor(kq[:, bass.ds(2 * s, 2), :], shuffled[:, :, :], rotated[:, :, :], ALU.add)\
                    .then_inc(hd["roped"], 1)

            def minus(out, a, hi):
                return nc.gpsimd.tensor_tensor(out, a, hi.bitcast(F32), ALU.subtract)

            def v_low(at_, g):
                k1, k2, v1, v2 = at_.buffers[g % len(at_.buffers)]
                pool.wait_ge(at_.s["v_hi"], 2 * (g + 1))
                values = at_.v_rows[:, :, HEAD_DIM * g:HEAD_DIM * (g + 1)]
                minus(v2[:, :, LOW], values, v1[:, :, LOW]).then_inc(at_.s["v_all"], 1)
                minus(v2[:, :, 2 * HEAD_DIM:], values, v1[:, :, LOW]).then_inc(at_.s["v_all"], 1)

            def low_parts(at_):
                for i in range(at_.heads):
                    for j in range(at_.pairs):
                        two = slice(2 * j, 2 * j + 2) if at_ is main else slice(1, 2)
                        pool.wait_ge(at_.s[f"p_hi{j}"], i + 1)
                        minus(p_lo[i % 2][:, two, :], at_.p_raw[:, two, :], p_hi[i % 2][:, two, :])\
                            .then_inc(at_.s["p_lo"], 1)
                    g = i // 4 + 1
                    if at_ is main and g < N_KV and i % 4 in (0, 2):
                        k1, k2, v1, v2 = at_.buffers[g % 2]
                        pool.wait_ge(at_.s["p_lo"], 2 * i + 2)
                        if i % 4 == 0:
                            pool.wait_ge(at_.s["k_hi"], 3 * (g + 1))
                            minus(k1[HIGH, :], at_.k_tiles[at_.half(g), g // 2, :], k1[at_.half(g), :])\
                                .then_inc(at_.s["k_all"], 1)
                            pool.wait_ge(at_.s["k_all"], g + 1)
                        else:
                            v_low(at_, g)

            pool.wait_ge(hd["roped"], 5)
            constants(main, kv_main[1:], 4)
            low_parts(main)
            pool.wait_ge(chunk_used, C_OUT + PAIRS)
            pool.wait_ge(mm["lo"], D_TILES)
            constants(cross, kv_cross)
            pool.wait_ge(cross.s["consts"], 4 * N_CROSS)
            for g in range(N_CROSS):
                v_low(cross, g)
            low_parts(cross)
            n = norms["ffn2"]
            for d in range(D_TILES):
                pool.wait_ge(*n.at("squared", d + 1))
                pool.wait_ge(*n.at("summed", d + 1))
                nc.gpsimd.tensor_tensor(square_sum[:, :], square_sum[:, :], squares[d % 2][:, :], ALU.add)\
                    .then_inc(n["summed"], 1)

            pool.wait_ge(*norms["final"].at("factor", 1))
            pool.wait_ge(gained, D_TILES - DVE_TILES)
            for d in range(DVE_TILES, D_TILES):
                nc.gpsimd.tensor_tensor(final_t[:, d, :], final_t[:, d, :], row_factor[:, :], ALU.mult)\
                    .then_inc(pool_out, 1)

        @block.scalar
        def _(act):
            def copy(out, in_, scale=1.0):
                return nc.scalar.activation(out, in_, ACT.Copy, scale=scale)

            def high(n, gain_row, d, ready):
                act.wait_ge(*ready)
                copy(x_hi[:, d, :], h[:, d, :], gain[:, gain_row, d:d + 1]).then_inc(n["x_hi"], 1)

            def square(n, d, m, ready):
                act.wait_ge(*ready)
                act.wait_ge(*n.at("summed", d))
                nc.scalar.activation(squares[m][:, :], h[:, d, :], ACT.Square).then_inc(n["squared"], 1)

            def refresh(n, gain_row, d, m, ready, split=True):
                if split:
                    high(n, gain_row, d, ready)
                square(n, d, m, ready)

            def inverse_root(out, neg_half_mean):
                return nc.scalar.activation(out, neg_half_mean, ACT.Abs_reciprocal_sqrt, scale=-2.0)

            def root(n, then=None):
                act.preload_act_table(ACT.Abs_reciprocal_sqrt)
                act.wait_ge(*n.at("neg_half", 1))
                inverse_root(rsq[:, :], neg_half[:, :]).then_inc(n["root"], 1)
                if then is not None:
                    act.preload_act_table(then)

            def feed_forward(tag, c0, j):
                f = ffns[tag]
                convert_hi(act, 0, c0 // 2 + j + 1)
                act.wait_ge(f["gate_out"], j + 1)
                nc.scalar.activation(silu_t[:, :, :], gate_t[:, :, :], ACT.Silu).then_inc(f["silu"], 1)
                convert_hi(act, 1, c0 // 2 + j + 1)
                wait_apart(act, f["product"], j + 1)
                copy(ff_hi[:, bass.ds(2 * j, 2), :], up_t[:, :, :]).then_inc(f["ff_hi"], 1)

            def down(n, gain_row, c0, p, last, end):
                for i in range(3 if not (end and last) else 2):
                    cols = (DOWN_SPLIT[(i + 2) % 4] * COLS) if not (last and i >= 2) else CHUNK
                    convert_hi(act, i % 2, c0 // 2 + 2 * p + i // 2 + 1, cols)
                for m in range(2):
                    refresh(n, gain_row, 2 * p + m, m, n.at(f"h_new{m}", p + 1), split=not end)
                if not (end and last):
                    convert_hi(act, 1, c0 // 2 + 2 * p + 2, CHUNK if last else DOWN_SPLIT[1] * COLS)

            def ffn(tag, nxt, c0, gain_row, end):
                root(norms[tag], ACT.Silu)
                feed_forward(tag, c0, 0)
                with act.Fori(1, FF_PAIRS) as j:
                    feed_forward(tag, c0, j)
                down0 = c0 + 2 * FF_PAIRS
                for p in range(PAIRS):
                    if end and p == PAIRS - 1:
                        act.preload_act_table(ACT.Abs_reciprocal_sqrt)
                    down(norms[nxt], gain_row, down0, p, p == PAIRS - 1, end)

            act.dma_start(gain[:, :, :], gains).then_inc(gains_loaded, 16)
            act.preload_act_table(ACT.Copy)
            n = norms["ffn1"]
            act.wait_ge(gains_loaded, 16)
            for d in range(D_TILES):
                if d == 0:
                    act.wait_ge(first_half["loaded"], 16)
                    copy(w_hi[0][:, 0:CHUNK // 2], raw[0][:, 0:CHUNK // 2]).then_inc(first_half["hi"], 1)
                if d == 4:
                    act.wait_ge(raw_loaded[0], 16)
                    copy(w_hi[0][:, CHUNK // 2:], raw[0][:, CHUNK // 2:]).then_inc(w_hi_made, 1)
                high(n, 0, d, (x_loaded[d // 2], 16))
            for d in range(D_TILES):
                if d == 0:
                    convert_hi(act, 1, 0, first=True)
                square(n, d, d % 2, (x_loaded[d // 2], 16))
            act.dma_start(head_gain[:, :], head_gains).then_inc(consts_loaded, 16)
            act.dma_start(ident[:, :], identity).then_inc(consts_loaded, 16)
            act.dma_start(ch_raw[:, :], channel_dft).then_inc(consts_loaded, 16)
            ffn("ffn1", "mix", C_FFN1, 1, False)

            def k_high(at_, g):
                k1, k2, v1, v2 = at_.buffers[g % len(at_.buffers)]
                source = at_.k_tiles[at_.half(g), g // 2, :]
                if g >= len(at_.buffers):
                    act.wait_ge(at_.s["st_full"], at_.pairs * at_.per_kv * (g - 1))
                copy(k1[LOW, :], source).then_inc(at_.s["k_hi"], 1)
                copy(k1[HIGH, :], source).then_inc(at_.s["k_hi"], 1)
                copy(k2[LOW, :], source).then_inc(at_.s["k_hi"], 1)

            def v_high(at_, g):
                k1, k2, v1, v2 = at_.buffers[g % len(at_.buffers)]
                values = at_.v_rows[:, :, HEAD_DIM * g:HEAD_DIM * (g + 1)]
                if g >= len(at_.buffers):
                    act.wait_ge(at_.s["pv"], at_.per_kv * (g - 1))
                copy(v1[:, :, LOW], values).then_inc(at_.s["v_hi"], 1)
                copy(v1[:, :, 2 * HEAD_DIM:], values).then_inc(at_.s["v_hi"], 1)

            def q_high(at_, i):
                source = at_.q_tiles[at_.half(i), i // 2, :]
                if i >= 4:
                    act.wait_ge(at_.s["st_full"], at_.pairs * (i - 3))
                copy(q1[i % 4][LOW, :], source).then_inc(at_.s["q_hi"], 1)

            def shift_in(at_, i):
                act.wait_ge(at_.s["shift"], i + 1)
                copy(q2[i % 4][HIGH, :], shift_bank[HIGH, :]).then_inc(at_.s["shift_in"], 1)

            def exponentials(at_, i):
                for j in range(at_.pairs):
                    act.wait_ge(at_.s["st_full"], at_.pairs * i + j + 1)
                    if i >= 1:
                        act.wait_ge(at_.s["p_lo"], at_.pairs * (i - 1) + j + 1)
                    if i >= 1 and at_ is cross:
                        act.wait_ge(at_.s["p_lo0"], i)
                    two = slice(2 * j, 2 * j + 2)
                    nc.scalar.activation(at_.p_raw[:, two, :], st_pair(at_, i, j)[:, :, :], ACT.Exp, scale=SCALE)\
                        .then_inc(at_.s["p"], 1)

            def second_high(at_, i):
                if at_.pairs == 2:
                    if i >= 2:
                        act.wait_ge(at_.s["pv"], i - 1)
                    act.wait_ge(at_.s["p"], 2 * i + 2)
                    copy(p_hi[i % 2][:, 2:4, :], at_.p_raw[:, 2:4, :]).then_inc(at_.s["p_hi1"], 1)

            def invert(at_, i):
                e = at_.half(i)
                act.wait_ge(at_.s["pv"], i + 1)
                nc.scalar.activation(denom[e, :], pv_bank[at_.half(i + 1), :], ACT.Ln).then_inc(at_.s["log_denom"], 1)
                act.wait_ge(at_.s["log_denom"], i + 1)
                nc.scalar.activation(denom[e, :], denom[e, :], ACT.Exp, scale=-1.0).then_inc(at_.s["inv_denom"], 1)

            act.wait_ge(chunk_used, C_IN)
            act.dma_start(rope_cos[:, :], rope[0]).then_inc(rope_loaded, 16)
            act.dma_start(rope_sin[:, :], rope[1]).then_inc(rope_loaded, 16)
            root(norms["mix"])

            def square_heads(s):
                act.wait_ge(pr["out"], s + 1 if s == 0 else s + 2)
                if s >= 1:
                    act.wait_ge(hd["stat"], s)
                nc.scalar.activation(hsq[:, :, :], kq[:, 2 * s:2 * s + 2, :], ACT.Square).then_inc(hd["sq"], 1)
                act.wait_ge(hd["sq"], s + 1)
                copy(hsq_hi[:, :, :], hsq[:, :, :]).then_inc(hd["sq_hi"], 1)

            def head_root(s):
                act.wait_ge(hd["stat"], s + 1)
                if s >= 1:
                    act.wait_ge(hd["t_mul"], s)
                nc.scalar.activation(hneg_half[:, :, :], ps_c[:, :, :], ACT.Copy, bias=-0.5 * EPS,
                                     scale=-0.5 / HEAD_DIM).then_inc(hd["neg_half"], 1)
                act.wait_ge(hd["neg_half"], s + 1 + FREE)
                if s >= 1:
                    act.wait_ge(hd["scaled"], s)
                inverse_root(hrsq[:, :, :], hneg_half[:, :, :]).then_inc(hd["root"], 1)
                act.wait_ge(hd["root"], s + 1)
                nc.scalar.activation(hnewton[:, :, :], hrsq[:, :, :], ACT.Square).then_inc(hd["y_sq"], 1)

            q0 = C_IN // 2
            act.wait_ge(consts_loaded, 48)
            copy(ch_hi[:, :], ch_raw[:, :]).then_inc(ch_hi_made, 1)
            convert_hi(act, 0, q0 + 1)
            square_heads(0)
            convert_hi(act, 1, q0 + 1)
            for u in range(2, 6):
                convert_hi(act, u % 2, q0 + u // 2 + 1)
                square_heads(u - 1)
                if u == 2:
                    act.wait_ge(pr["v_turned"], 1)
                    copy(v_tok[:, :, :].rearrange("p a b -> p (a b)"),
                         ps_d[:, :, :].rearrange("p a b -> p (a b)")).then_inc(pr["v_tok"], 1)
                head_root(u - 2)
            convert_hi(act, 0, q0 + 4)
            act.wait_ge(pr["out"], 7)
            copy(f_hi[:, 0:2, :], f_t[:, 0:2, :]).then_inc(pr["f_hi"], 1)
            head_root(4)
            act.wait_ge(hd["roped"], 2)
            k_high(main, 0)
            q_high(main, 0)
            q_high(main, 1)
            v_high(main, 0)
            act.wait_ge(pr["out"], 8)
            copy(f_hi[:, 2:4, :], f_t[:, 2:4, :]).then_inc(pr["f_hi"], 1)

            def attention(at_, before):
                for i in range(at_.heads):
                    if i >= 2:
                        invert(at_, i - 2)
                    if at_ is main and i + 3 < at_.heads:
                        q_high(at_, i + 3)
                    exponentials(at_, i)
                    if i + 1 < at_.heads:
                        shift_in(at_, i + 1)
                    second_high(at_, i)
                    if at_ is main and i // 4 + 1 < N_KV:
                        if i % 4 == 0:
                            k_high(at_, i // 4 + 1)
                        if i % 4 == 2:
                            v_high(at_, i // 4 + 1)
                for i in (at_.heads - 2, at_.heads - 1):
                    before[i]()
                    invert(at_, i)

            act.preload_act_table_set("natural_log_exp_and_others")
            for tt in range(4):
                act.wait_ge(pr["y_full"], tt + 1)
                copy(y_hi[:, tt, :], y_pipes[tt].rearrange("p a b -> p (a b)")).then_inc(pr["y_hi"], 1)
            convert_hi(act, 1, q0 + 4)
            shift_in(main, 0)
            act.wait_ge(hd["roped"], 5)
            q_high(main, 2)
            convert_hi(act, 0, C_BRANCH // 2, BRANCH_K[0] * COLS)
            for half in range(2):
                act.wait_ge(pr["a_full"], half + 1)
                copy(a_hi[:, 2 * half:2 * half + 2, :], dft_pipes[half][:, :, :]).then_inc(pr["a_hi"], 1)
            def split_x(tiles):
                act.wait_ge(main.s["pv"], N_HEADS - (tiles[0] == 0))
                for k in tiles:
                    copy(x_hi[:, k, :], h[:, k, :], gain[:, 1, k:k + 1]).then_inc(br["x_hi"], 1)

            attention(main, {N_HEADS - 2: lambda: convert_hi(act, 1, C_BRANCH // 2),
                             N_HEADS - 1: lambda: split_x(range(4))})

            split_x(range(4, D_TILES))
            convert_hi(act, 0, C_BRANCH // 2 + 1)
            act.preload_act_table(ACT.Sigmoid)
            act.wait_ge(main.s["o"], N_HEADS)
            for half in range(2):
                s = slice(4 * half, 4 * half + 4)
                copy(o_hi[:, s, :], main.out_tiles[:, s, :]).then_inc(br["o_hi"], 1)

            def branch(m, last):
                q = C_BRANCH // 2 + 2 * m
                act.wait_ge(br["gf_out"], m + 1 + FREE)
                nc.scalar.activation(gf_t[:, :, :], gf_t[:, :, :], ACT.Sigmoid).then_inc(br["sig_f"], 1)
                convert_hi(act, 1, q + 1)
                act.wait_ge(br["ga_out"], m + 1 + FREE)
                nc.scalar.activation(ga_t[:, :, :], ga_t[:, :, :], ACT.Sigmoid).then_inc(br["sig_a"], 1)
                convert_hi(act, 0, q + 2, CHUNK if last else BRANCH_K[0] * COLS)
                if last:
                    act.wait_ge(mem_loaded, 16)
                    nc.scalar.activation(mem_sq[:, :, :], mem[:, :, :], ACT.Square).then_inc(mm["squared"], 1)
                else:
                    convert_hi(act, 1, q + 2)
                wait_apart(act, br["merged"], m + 1)
                copy(m_hi[:, bass.ds(2 * m, 2), :], merged_t[:, :, :]).then_inc(br["m_hi"], 1)
                convert_hi(act, *((1, q + 2) if last else (0, q + 3)))

            with act.Fori(0, PAIRS - 1) as m:
                branch(m, False)
            branch(PAIRS - 1, True)

            n = norms["cross"]
            for p in range(PAIRS):
                for m in range(2):
                    high(n, 2, 2 * p + m, n.at(f"h_new{m}", p + 1))
                convert_hi(act, p % 2, C_OUT // 2 + p // 2 + 1)
                for m in range(2):
                    square(n, 2 * p + m, m, n.at(f"h_new{m}", p + 1))
                if p == 0:
                    act.wait_ge(mm["neg_half"], 1)
                    inverse_root(mrsq[:, :], mneg_half[:, :]).then_inc(mm["root"], 1)
                else:
                    act.wait_ge(mm["normed"], 1)
                    for k in range(*((0, 4), (4, 8), (8, 8))[p - 1]):
                        copy(mem_hi[:, k, :], mem[:, k, :], gain[:, 5, k:k + 1]).then_inc(mm["hi"], 1)

            convert_hi(act, 0, C_CK // 2 + 1)
            act.wait_ge(cr["k_out"], 1)
            for g in range(N_CROSS):
                k_high(cross, g)
            root(n)
            act.preload_act_table_set("natural_log_exp_and_others")
            for i in range(N_CROSS):
                act.wait_ge(cr["q_out"], i // 2 + 1)
                q_high(cross, i)
            convert_hi(act, 1, C_CK // 2 + 1)
            shift_in(cross, 0)
            act.wait_ge(cr["v_out"], 1)
            for g in range(N_CROSS):
                v_high(cross, g)

            def co_high(k):
                act.wait_ge(cross.s["o"], 2 * k + 2)
                copy(co_hi[:, k, :], cross_o[:, k, :]).then_inc(cr["co_hi"], 1)

            attention(cross, {N_CROSS - 2: lambda: co_high(0),
                              N_CROSS - 1: lambda: convert_hi(act, 0, C_CK // 2 + 2)})
            co_high(1)
            n = norms["ffn2"]
            for p in range(PAIRS):
                for m in range(2):
                    refresh(n, 3, 2 * p + m, m, n.at(f"h_new{m}", p + 1))
            convert_hi(act, 1, C_CK // 2 + 2)
            ffn("ffn2", "final", C_FFN2, 4, True)
            root(norms["final"])
            for d in range(DVE_TILES, D_TILES):
                copy(final_t[:, d, :], h[:, d, :], gain[:, 4, d:d + 1]).then_inc(gained, 1)

        @block.vector
        def _(dve):
            def tt(out, a, b, op):
                return nc.vector.tensor_tensor(out, a, b, op)

            def minus(out, a, hi):
                return tt(out, a, hi.bitcast(F32), ALU.subtract)

            def clear(n):
                nc.vector.memset(square_sum[:, :], 0.0).then_inc(n["summed"], 1)

            def low(n, gain_row, d):
                dve.wait_ge(*n.at("x_hi", d + 1))
                nc.vector.scalar_tensor_tensor(x_lo[:, d, :], h[:, d, :], gain[:, gain_row, bass.ds(d, 1)],
                                               x_hi[:, d, :].bitcast(F32), ALU.mult, ALU.subtract)\
                    .then_inc(n["x_lo"], 1)

            def add_squares(n, d, m):
                dve.wait_ge(*n.at("squared", d + 1))
                dve.wait_ge(*n.at("summed", d + 1))
                tt(square_sum[:, :], square_sum[:, :], squares[m][:, :], ALU.add).then_inc(n["summed"], 1)

            def refresh(n, gain_row, d, m, split=True):
                if split:
                    low(n, gain_row, d)
                add_squares(n, d, m)

            def residual(n, d, m, bank, factor):
                nc.vector.scalar_tensor_tensor(h[:, d, :], bank, factor, h[:, d, :], ALU.mult, ALU.add)\
                    .then_inc(n[f"h_new{m}"], 1)

            def half_mean(out, sums, count):
                return nc.vector.tensor_scalar(out, sums, -0.5 / count, -0.5 * EPS, ALU.mult, ALU.add)

            def refine(out, y, half, t, root, newton, factor, before=0):
                dve.wait_ge(root, before + 1)
                tt(t, y, y, ALU.mult).then_inc(newton, 1)
                dve.wait_ge(newton, 2 * before + 1)
                tt(t, t, half, ALU.mult).then_inc(newton, 1)
                dve.wait_ge(newton, 2 * before + 2)
                nc.vector.scalar_tensor_tensor(out, t, 1.5, y, ALU.add, ALU.mult).then_inc(factor, 1)
                dve.wait_ge(factor, before + 1)

            def factor(n):
                dve.wait_ge(*n.at("stat", 1))
                half_mean(neg_half[:, :], stat, D_MODEL).then_inc(n["neg_half"], 1)
                dve.wait_ge(*n.at("neg_half", 1))
                refine(row_factor[:, :], rsq[:, :], neg_half[:, :], newton[:, :], n["root"], n["newton"],
                       n["factor"], n.before["root"])

            rf = wide(row_factor[:, :])

            def feed_forward(tag, c0, j):
                f = ffns[tag]
                dve.wait_ge(chunk_used, c0 + 2 * j + 1)
                tt(gate_t[:, :, :], ps_a[:, :, :], rf, ALU.mult).then_inc(f["gate_out"], 1)
                convert_lo(dve, 0, c0 // 2 + j + 1)
                dve.wait_ge(chunk_used, c0 + 2 * j + 2)
                dve.wait_ge(f["ff_lo"], j)
                tt(up_t[:, :, :], ps_b[:, :, :], rf, ALU.mult).then_inc(f["up_out"], 1)
                dve.wait_ge(f["silu"], j + 1)
                dve.wait_ge(f["up_out"], j + 1)
                tt(up_t[:, :, :], up_t[:, :, :], silu_t[:, :, :], ALU.mult).then_inc(f["product"], 1)
                convert_lo(dve, 1, c0 // 2 + j + 1)
                dve.wait_ge(f["ff_hi"], j + 1)
                two = bass.ds(2 * j, 2)
                minus(ff_lo[:, two, :], up_t[:, :, :], ff_hi[:, two, :]).then_inc(f["ff_lo"], 1)

            def down(n, gain_row, c0, p, last, end):
                for i in range(3 if not (end and last) else 2):
                    cols = (DOWN_SPLIT[(i + 2) % 4] * COLS) if not (last and i >= 2) else CHUNK
                    convert_lo(dve, i % 2, c0 // 2 + 2 * p + i // 2 + 1, cols)
                dve.wait_ge(*n.at("tile0", p + 1))
                residual(n, 2 * p, 0, ps_c[:, 0, :], 0.5)
                dve.wait_ge(chunk_used, c0 + 4 * p + 4)
                residual(n, 2 * p + 1, 1, ps_c[:, 1, :], 0.5)
                for m in range(2):
                    if end and last and m == 1:
                        break
                    refresh(n, gain_row, 2 * p + m, m, split=not end)
                if not (end and last):
                    convert_lo(dve, 1, c0 // 2 + 2 * p + 2, CHUNK if last else DOWN_SPLIT[1] * COLS)

            def ffn(tag, nxt, c0, gain_row, end):
                factor(norms[tag])
                feed_forward(tag, c0, 0)
                with dve.Fori(1, FF_PAIRS) as j:
                    feed_forward(tag, c0, j)
                n = norms[nxt]
                clear(n)
                down0 = c0 + 2 * FF_PAIRS
                with dve.Fori(0, PAIRS - 1) as p:
                    down(n, gain_row, down0, p, False, end)
                down(n, gain_row, down0, PAIRS - 1, True, end)

            n = norms["ffn1"]
            clear(n)
            dve.wait_ge(gains_loaded, 16)
            half = CHUNK // 2
            for d in range(D_TILES):
                if d == 0:
                    dve.wait_ge(first_half["hi"], 1)
                    minus(w_lo[0][:, 0:half], raw[0][:, 0:half], w_hi[0][:, 0:half]).then_inc(first_half["lo"], 1)
                if d == 4:
                    dve.wait_ge(w_hi_made, 1)
                    minus(w_lo[0][:, half:], raw[0][:, half:], w_hi[0][:, half:]).then_inc(w_lo_made, 1)
                low(n, 0, d)
            for d in range(D_TILES):
                if d == 0:
                    convert_lo(dve, 1, 0)
                add_squares(n, d, d % 2)
            ffn("ffn1", "mix", C_FFN1, 1, False)

            def k_low(at_, g):
                k1, k2, v1, v2 = at_.buffers[g % len(at_.buffers)]
                e = at_.half(g)
                dve.wait_ge(at_.s["k_hi"], 3 * (g + 1))
                minus(k1[HIGH, :], at_.k_tiles[e, g // 2, :], k1[e, :]).then_inc(at_.s["k_all"], 1)

            def v_low(at_, g):
                k1, k2, v1, v2 = at_.buffers[g % len(at_.buffers)]
                dve.wait_ge(at_.s["v_hi"], 2 * (g + 1))
                values = at_.v_rows[:, :, HEAD_DIM * g:HEAD_DIM * (g + 1)]
                minus(v2[:, :, LOW], values, v1[:, :, LOW]).then_inc(at_.s["v_all"], 1)
                minus(v2[:, :, 2 * HEAD_DIM:], values, v1[:, :, LOW]).then_inc(at_.s["v_all"], 1)

            def q_high(at_, i):
                if i >= 4:
                    dve.wait_ge(at_.s["st_full"], at_.pairs * (i - 3))
                nc.vector.tensor_copy(q1[i % 4][HIGH, :], at_.q_tiles[at_.half(i), i // 2, :])\
                    .then_inc(at_.s["q_hi2"], 1)

            def q_low(at_, i):
                dve.wait_ge(at_.s["q_hi"], i + 1)
                dve.wait_ge(at_.s["q_hi2"], i + 1)
                e = at_.half(i)
                minus(q2[i % 4][LOW, :], at_.q_tiles[e, i // 2, :], q1[i % 4][e, :]).then_inc(at_.s["q_lo"], 1)

            def row_maxima(at_, i, j):
                tiles, bank = score_tiles(at_, j)
                dve.wait_ge(at_.s["s_full"], at_.steps * i + j + 1)
                nc.vector.tensor_reduce(row_max[:, i % 2, tiles[0]:tiles[-1] + 1], bank, AX.X, ALU.max)\
                    .then_inc(at_.s["row_max"], 1)

            def diagonal(at_, i):
                dve.wait_ge(at_.s["row_max"], at_.steps * (i + 1))
                if i >= 1:
                    dve.wait_ge(at_.s["shift"], i)
                nc.vector.scalar_tensor_tensor(diag[:, :, :], wide(ident[:, :], 4), -1.0,
                                               row_max[:, i % 2, :].unsqueeze(2).to_broadcast([P, 4, P]),
                                               ALU.mult, ALU.mult).then_inc(at_.s["diag"], 1)

            def probabilities(at_, i):
                if i >= 2:
                    dve.wait_ge(at_.s["pv"], i - 1)
                dve.wait_ge(at_.s["p"], at_.pairs * i + 1)
                nc.vector.tensor_copy(p_hi[i % 2][:, 0:2, :], at_.p_raw[:, 0:2, :]).then_inc(at_.s["p_hi0"], 1)
                if at_ is cross:
                    dve.wait_ge(at_.s["p_hi0"], i + 1)
                    minus(p_lo[i % 2][:, 0, :], at_.p_raw[:, 0, :], p_hi[i % 2][:, 0, :]).then_inc(at_.s["p_lo0"], 1)

            def normalize(at_, i):
                e = at_.half(i)
                dve.wait_ge(at_.s["inv_denom"], i + 1)
                tt(at_.out_tiles[e, i // 2, :], pv_bank[e, :], denom[e, :], ALU.mult).then_inc(at_.s["o"], 1)

            q0 = C_IN // 2
            dve.wait_ge(consts_loaded, 48)
            factor(norms["mix"])

            def project_out(u, b, out):
                dve.wait_ge(chunk_used, C_IN + u + 1)
                tt(out, pipes[b][:, :, :], rf, ALU.mult).then_inc(pr["out"], 1)

            def square_low(s):
                dve.wait_ge(hd["sq_hi"], s + 1)
                minus(hsq_lo[:, :, :], hsq[:, :, :], hsq_hi[:, :, :]).then_inc(hd["sq_lo"], 1)

            def y_low(tt_):
                dve.wait_ge(pr["y_hi"], tt_ + 1)
                minus(y_lo[:, tt_, :], y_pipes[tt_].rearrange("p a b -> p (a b)"), y_hi[:, tt_, :])\
                    .then_inc(pr["out"], 1)

            def f_low(half):
                s = slice(2 * half, 2 * half + 2)
                dve.wait_ge(pr["f_hi"], half + 1)
                minus(f_lo[:, s, :], f_t[:, s, :], f_hi[:, s, :]).then_inc(pr["f_lo"], 1)

            def norm_heads(s):
                if s == 4:
                    f_low(0)
                    project_out(7, 1, f_t[:, 2:4, :])
                    k_low(main, 0)
                    q_high(main, 0)
                if s == 4:
                    f_low(1)
                dve.wait_ge(hd["neg_half"], s + 1 + FREE)
                dve.wait_ge(hd["y_sq"], s + 1)
                tt(hnewton[:, :, :], hnewton[:, :, :], hneg_half[:, :, :], ALU.mult).then_inc(hd["t_mul"], 1)
                if s == 4:
                    q_low(main, 0)
                    for tt_ in range(4):
                        y_low(tt_)
                    q_high(main, 1)
                    row_maxima(main, 0, 0)
                dve.wait_ge(hd["t_mul"], s + 1)
                nc.vector.scalar_tensor_tensor(hrsq[:, :, :], hnewton[:, :, :], 1.5, hrsq[:, :, :],
                                               ALU.add, ALU.mult).then_inc(hd["factor"], 1)
                if s == 4:
                    row_maxima(main, 0, 1)
                    diagonal(main, 0)
                    convert_lo(dve, 1, q0 + 4)
                    q_low(main, 1)
                dve.wait_ge(hd["factor"], s + 1)
                if s >= 1:
                    dve.wait_ge(hd["mul"], 2 * s)
                nc.vector.scalar_tensor_tensor(normed[:, :, :], kq[:, 2 * s:2 * s + 2, :], head_gain[:, s:s + 1],
                                               hrsq[:, :, :], ALU.mult, ALU.mult).then_inc(hd["scaled"], 1)
                if s >= 1:
                    dve.wait_ge(hd["roped"], s)
                dve.wait_ge(hd["scaled"], s + 1)
                nc.vector.stream_shuffle(shuffled[:, :, :], normed[:, :, :], [(i + 16) % 32 for i in range(32)])\
                    .then_inc(hd["shuffled"], 1)

            project_out(0, 0, kq[:, 0:2, :])
            convert_lo(dve, 0, q0 + 1)
            square_low(0)
            dve.wait_ge(ch_hi_made, 1)
            minus(ch_lo[:, :], ch_raw[:, :], ch_hi[:, :]).then_inc(ch_lo_made, 1)
            project_out(1, 1, v_t[:, :, :])
            convert_lo(dve, 1, q0 + 1)
            for u in range(2, 6):
                project_out(u, u % 2, kq[:, 2 * u - 2:2 * u, :])
                convert_lo(dve, u % 2, q0 + u // 2 + 1)
                square_low(u - 1)
                norm_heads(u - 2)
            project_out(6, 0, f_t[:, 0:2, :])
            convert_lo(dve, 0, q0 + 4)
            norm_heads(4)

            def attention(at_, before):
                for i in range(at_.heads):
                    later = i + 2 < at_.heads
                    if later:
                        row_maxima(at_, i + 2, 0)
                    if i >= 2:
                        normalize(at_, i - 2)
                    if at_ is cross and i == 2:
                        convert_lo(dve, 1, C_CK // 2 + 1)
                    probabilities(at_, i)
                    if later and at_.steps == 2:
                        row_maxima(at_, i + 2, 1)
                    if at_ is main and i + 3 < at_.heads:
                        q_high(at_, i + 3)
                    if later:
                        diagonal(at_, i + 2)
                        q_low(at_, i + 2)
                for i in (at_.heads - 2, at_.heads - 1):
                    before[i]()
                    normalize(at_, i)

            row_maxima(main, 1, 0)
            v_low(main, 0)
            row_maxima(main, 1, 1)
            diagonal(main, 1)
            q_high(main, 2)
            convert_lo(dve, 0, C_BRANCH // 2, BRANCH_K[0] * COLS)
            for half in range(2):
                dve.wait_ge(pr["a_hi"], half + 1)
                s = slice(2 * half, 2 * half + 2)
                minus(a_lo[:, s, :], dft_pipes[half][:, :, :], a_hi[:, s, :]).then_inc(pr["a_lo"], 1)
            def split_x(tiles):
                for k in tiles:
                    dve.wait_ge(br["x_hi"], k + 1)
                    nc.vector.scalar_tensor_tensor(x_lo[:, k, :], h[:, k, :], gain[:, 1, k:k + 1],
                                                   x_hi[:, k, :].bitcast(F32), ALU.mult, ALU.subtract)\
                        .then_inc(br["x_lo"], 1)

            attention(main, {N_HEADS - 2: lambda: convert_lo(dve, 1, C_BRANCH // 2),
                             N_HEADS - 1: lambda: split_x(range(4))})

            split_x(range(4, D_TILES))
            convert_lo(dve, 0, C_BRANCH // 2 + 1)
            for half in range(2):
                s = slice(4 * half, 4 * half + 4)
                dve.wait_ge(br["o_hi"], half + 1)
                minus(o_lo[:, s, :], main.out_tiles[:, s, :], o_hi[:, s, :]).then_inc(br["o_lo"], 1)

            def branch(m, last):
                q = C_BRANCH // 2 + 2 * m
                dve.wait_ge(chunk_used, 2 * q + 2)
                tt(gf_t[:, :, :], ps_b[:, :, :], rf, ALU.mult).then_inc(br["gf_out"], 1)
                convert_lo(dve, 1, q + 1)
                dve.wait_ge(br["sig_f"], m + 1)
                tt(gf_t[:, :, :], ps_a[:, :, :], gf_t[:, :, :], ALU.mult).then_inc(br["yf"], 1)
                dve.wait_ge(chunk_used, 2 * q + 3)
                tt(ga_t[:, :, :], ps_d[:, :, :], rf, ALU.mult).then_inc(br["ga_out"], 1)
                convert_lo(dve, 0, q + 2, CHUNK if last else BRANCH_K[0] * COLS)
                if not last:
                    convert_lo(dve, 1, q + 2)
                dve.wait_ge(br["sig_a"], m + 1)
                dve.wait_ge(chunk_used, 2 * q + 4)
                tt(ga_t[:, :, :], ps_c[:, :, :], ga_t[:, :, :], ALU.mult).then_inc(br["ya"], 1)
                dve.wait_ge(br["yf"], m + 1 + FREE)
                dve.wait_ge(br["ya"], m + 1 + FREE)
                tt(merged_t[:, :, :], gf_t[:, :, :], ga_t[:, :, :], ALU.add).then_inc(br["merged"], 1)
                dve.wait_ge(br["m_hi"], m + 1)
                two = bass.ds(2 * m, 2)
                minus(m_lo[:, two, :], merged_t[:, :, :], m_hi[:, two, :]).then_inc(br["m_lo"], 1)
                convert_lo(dve, *((1, q + 2) if last else (0, q + 3)))

            with dve.Fori(0, PAIRS - 1) as m:
                branch(m, False)
            branch(PAIRS - 1, True)

            dve.wait_ge(mm["squared"], 1)
            nc.vector.tensor_reduce(msum[:, :], mem_sq[:, :, :].rearrange("p k t -> p t k"), AX.X, ALU.add)\
                .then_inc(mm["sum"], 1)
            n = norms["cross"]
            clear(n)
            for p in range(PAIRS):
                dve.wait_ge(*n.at("tile0", p + 1))
                residual(n, 2 * p, 0, out_pipes[p % 2][:, 0, :], 1.0)
                dve.wait_ge(chunk_used, C_OUT + p + 1)
                residual(n, 2 * p + 1, 1, out_pipes[p % 2][:, 1, :], 1.0)
                for m in range(2):
                    low(n, 2, 2 * p + m)
                convert_lo(dve, p % 2, C_OUT // 2 + p // 2 + 1)
                for m in range(2):
                    add_squares(n, 2 * p + m, m)
                if p == 0:
                    dve.wait_ge(mm["stat"], 1)
                    half_mean(mneg_half[:, :], ps_a[:, 0, 0:MEM_LEN], D_MODEL).then_inc(mm["neg_half"], 1)
                    dve.wait_ge(mm["neg_half"], 1)
                    refine(mrsq[:, :], mrsq[:, :], mneg_half[:, :], mnewton[:, :], mm["root"], mm["newton"],
                           mm["factor"])
                    tt(mem[:, :, :], mem[:, :, :], wide(mrsq[:, :], D_TILES), ALU.mult).then_inc(mm["normed"], 1)
                else:
                    for k in range(*((0, 4), (4, 8), (8, 8))[p - 1]):
                        dve.wait_ge(mm["hi"], k + 1)
                        nc.vector.scalar_tensor_tensor(mem_lo[:, k, :], mem[:, k, :], gain[:, 5, k:k + 1],
                                                       mem_hi[:, k, :].bitcast(F32), ALU.mult, ALU.subtract)\
                            .then_inc(mm["lo"], 1)

            dve.wait_ge(chunk_used, C_CK + 1)
            nc.vector.tensor_copy(cross_k[:, :, :], ps_a[:, :, 0:MEM_LEN]).then_inc(cr["k_out"], 1)
            convert_lo(dve, 0, C_CK // 2 + 1)
            for g in range(N_CROSS):
                k_low(cross, g)
            factor(n)
            dve.wait_ge(chunk_used, C_CQ + 1)
            for t in range(2):
                tt(cross_q[:, t, :], ps_b[:, t, :], row_factor[:, :], ALU.mult).then_inc(cr["q_out"], 1)
                dve.wait_ge(cr["q_out"], t + 1)
                q_high(cross, t)
            row_maxima(cross, 0, 0)
            diagonal(cross, 0)
            q_high(cross, 2)
            q_low(cross, 0)
            row_maxima(cross, 1, 0)
            diagonal(cross, 1)
            q_high(cross, 3)
            dve.wait_ge(chunk_used, C_CV + 1)
            nc.vector.tensor_copy(cross_v[:, :, :], ps_c[:, :, 0:MEM_LEN]).then_inc(cr["v_out"], 1)
            q_low(cross, 1)

            def co_low(k):
                dve.wait_ge(cr["co_hi"], k + 1)
                minus(co_lo[:, k, :], cross_o[:, k, :], co_hi[:, k, :]).then_inc(cr["co_lo"], 1)

            attention(cross, {N_CROSS - 2: lambda: co_low(0),
                              N_CROSS - 1: lambda: convert_lo(dve, 0, C_CK // 2 + 2)})
            co_low(1)
            n = norms["ffn2"]
            clear(n)
            for d in range(D_TILES + 1):
                if d < D_TILES:
                    dve.wait_ge(cr["co_tile"], d + 1)
                    residual(n, d, d % 2, co_banks[d], 1.0)
                if d > 0:
                    low(n, 3, d - 1)
            convert_lo(dve, 1, C_CK // 2 + 2)
            ffn("ffn2", "final", C_FFN2, 4, True)
            n = norms["final"]
            factor(n)
            for d in range(DVE_TILES):
                nc.vector.scalar_tensor_tensor(final_t[:, d, :], h[:, d, :], gain[:, 4, d:d + 1],
                                               row_factor[:, :], ALU.mult, ALU.mult).then_inc(out_ready, 1)

        @block.tensor
        def _(pe):
            def sum_rows(n):
                pe.wait_ge(*n.at("summed", D_TILES + 1))
                nc.tensor.matmul(stat, ones[:, :], square_sum[:, :], start=True, stop=True).then_inc(n["stat"], 1)

            def project(b, out, chunk, sums=None):
                pe.wait_ge(w_lo_made, chunk + 1)
                for m in range(2):
                    for k in range(D_TILES):
                        last = product(out[:, m, :], weight(b, k, m), part(x_parts, k), k == 0, k == D_TILES - 1)
                        if sums is not None and (m, k) == (0, 5):
                            sum_rows(sums)
                last.then_inc(chunk_used, 1)

            def project_new(b, out, chunk, n, halves=False, sums_after=D_TILES):
                pe.wait_ge(*((first_half["lo"], 1) if halves else (w_lo_made, chunk + 1)))
                for k in range(D_TILES):
                    pe.wait_ge(*n.at("x_lo", k + 1))
                    if halves and k == D_TILES // 2:
                        pe.wait_ge(w_lo_made, chunk + 1)
                    for m in range(2):
                        last = product(out[:, m, :], weight(b, k, m), part(x_parts, k), k == 0, k == D_TILES - 1)
                    if k == D_TILES - 1:
                        last.then_inc(chunk_used, 1)
                    if k == sums_after - 1:
                        sum_rows(n)

            def ffn(tag, nxt, c0):
                f, n = ffns[tag], norms[nxt]
                first = c0 == 0
                project_new(0, ps_a, c0, norms[tag], halves=first, sums_after=0 if first else D_TILES)
                project(1, ps_b, c0 + 1, sums=norms[tag] if first else None)
                with pe.Fori(1, FF_PAIRS) as j:
                    pe.wait_ge(f["gate_out"], j)
                    project(0, ps_a, c0 + 2 * j)
                    pe.wait_ge(f["up_out"], j)
                    project(1, ps_b, c0 + 2 * j + 1)
                down0 = c0 + 2 * FF_PAIRS
                with pe.Fori(0, PAIRS) as p:
                    for i in range(4):
                        pe.wait_ge(w_lo_made, down0 + 4 * p + i + 1)
                        pe.wait_ge(f["ff_lo"], FF_PAIRS - (i < 3))
                        for m in range(2):
                            if i == 0:
                                pe.wait_ge(*n.at(f"h_new{m}", p))
                            for k in range(DOWN_SPLIT[i]):
                                kt = DOWN_FIRST[i] + k
                                last = product(ps_c[:, m, :], weight(i % 2, k, m), part((ff_hi, ff_lo), kt),
                                               kt == 0, kt == FF_TILES - 1)
                            if i == 3 and m == 0:
                                last.then_inc(n["tile0"], 1)
                        last.then_inc(chunk_used, 1)

            for reader in (norm_sems["h_new0"], norm_sems["h_new1"], hd["neg_half"], br["yf"], br["ya"], br["gf_out"],
                           br["ga_out"]):
                pe.sem_inc(reader, FREE)
            pe.wait_ge(consts_set, 6)
            ffn("ffn1", "mix", C_FFN1)

            def head_sums(s):
                pe.wait_ge(hd["sq_lo"], s + 1)
                pe.wait_ge(hd["neg_half"], s + FREE)
                for m in range(2):
                    nc.tensor.matmul(ps_c[:, m, :], head_ones[:, :], hsq_hi[:, m, :], start=True, stop=False)
                    last = nc.tensor.matmul(ps_c[:, m, :], head_ones[:, :], hsq_lo[:, m, :], start=False, stop=True)
                last.then_inc(hd["stat"], 1)

            project_new(0, ps_a, C_IN, norms["mix"])
            project(1, ps_b, C_IN + 1)
            pe.wait_ge(pr["out"], 1)
            project(0, ps_a, C_IN + 2)
            pe.wait_ge(consts_loaded, 48)
            pe.wait_ge(pr["out"], 2)
            for kt in range(4):
                for m in range(2):
                    last = nc.tensor.transpose(ps_d[:, kt // 2, (kt % 2) * COLS + m * P:(kt % 2) * COLS + (m + 1) * P],
                                               v_t[:, m, kt * P:(kt + 1) * P], ident[:, :])
            last.then_inc(pr["v_turned"], 1)
            head_sums(0)
            with pe.Fori(0, 2) as t:
                for b in (1, 0):
                    s = 2 * t + 2 - b
                    pe.wait_ge(pr["out"], s + 1)
                    project(b, pipes[b], C_IN + 2 + s)
                    head_sums(s)
            pe.wait_ge(pr["out"], 6)
            project(1, ps_b, C_IN + 7)

            def scores(at_, i, j):
                k1, k2, v1, v2 = at_.kv(i)
                if j == 0:
                    pe.wait_ge(at_.s["k_all"], i // at_.per_kv + 1)
                    pe.wait_ge(at_.s["q_hi"], i + 1)
                    pe.wait_ge(at_.s["q_hi2"], i + 1)
                if at_.steps * i + j >= 1:
                    pe.wait_ge(at_.s["row_max"], at_.steps * i + j)
                tiles, bank = score_tiles(at_, j)
                for t, qt in enumerate(tiles):
                    last = nc.tensor.matmul(bank[:, t, :], q1[i % 4][:, qt * P:(qt + 1) * P], k1[:, :],
                                            start=True, stop=True)
                last.then_inc(at_.s["s_full"], 1)

            def shift(at_, i):
                pe.wait_ge(at_.s["diag"], i + 1)
                if i >= 1:
                    pe.wait_ge(at_.s["shift_in"], i)
                nc.tensor.matmul(shift_bank, pick[:, :], diag[:, :, :], start=True, stop=True)\
                    .then_inc(at_.s["shift"], 1)

            def turned_scores(at_, i):
                k1, k2, v1, v2 = at_.kv(i)
                pe.wait_ge(at_.s["shift_in"], i + 1)
                pe.wait_ge(at_.s["q_lo"], i + 1)
                if at_ is cross and i == 1:
                    pe.wait_ge(cr["v_out"], 1)
                for j in range(at_.pairs):
                    if at_ is main and i == 0:
                        pe.wait_ge(pr["a_lo"], j + 1)
                    if at_.pairs * i + j >= 2:
                        pe.wait_ge(at_.s["p"], at_.pairs * i + j - 1)
                    for t in range(2):
                        s = slice((2 * j + t) * P, (2 * j + t + 1) * P)
                        bank = st_pair(at_, i, j)[:, t, :]
                        nc.tensor.matmul(bank, k1[:, s], q1[i % 4][:, :], start=True, stop=False)
                        last = nc.tensor.matmul(bank, k2[:, s], q2[i % 4][:, :], start=False, stop=True)
                    last.then_inc(at_.s["st_full"], 1)

            def values(at_, i, j):
                k1, k2, v1, v2 = at_.kv(i)
                e = slice(HEAD_DIM * (i % 2), HEAD_DIM * (i % 2) + P)
                if j == 0:
                    pe.wait_ge(at_.s["v_all"], 2 * (i // at_.per_kv) + 2)
                    if i >= 1:
                        pe.wait_ge(at_.s["o"], i)
                pe.wait_ge(at_.s["p_lo"], at_.pairs * i + j + 1)
                if at_ is cross:
                    pe.wait_ge(at_.s["p_lo0"], i + 1)
                for kt in (2 * j, 2 * j + 1):
                    last = product(pv_bank, (v1[:, kt, e], v2[:, kt, e]), part((p_hi[i % 2], p_lo[i % 2]), kt),
                                   kt == 0, kt == 2 * at_.pairs - 1)
                if j == at_.pairs - 1:
                    last.then_inc(at_.s["pv"], 1)

            def attention(at_, before):
                pe.wait_ge(at_.s["consts"], 4 * len(at_.buffers))
                for i in range(at_.heads):
                    later = i + 2 < at_.heads
                    if later:
                        scores(at_, i + 2, 0)
                    turned_scores(at_, i)
                    if later and at_.steps == 2:
                        scores(at_, i + 2, 1)
                    if i + 1 < at_.heads:
                        shift(at_, i + 1)
                    if i >= 1:
                        if i - 1 in before:
                            before[i - 1]()
                        for j in range(at_.pairs):
                            values(at_, i - 1, j)
                if at_.heads - 1 in before:
                    before[at_.heads - 1]()
                for j in range(at_.pairs):
                    values(at_, at_.heads - 1, j)

            pe.wait_ge(ch_lo_made, 1)
            pe.wait_ge(hd["neg_half"], 5 + FREE)
            for g0 in (0, 2):
                pe.wait_ge(pr["f_lo"], g0 // 2 + 1)
                for tt_ in range(4):
                    if y_pipes[tt_] is ps_b:
                        pe.wait_ge(pr["out"], 8)
                    for g in (g0, g0 + 1):
                        last = product(y_pipes[tt_][:, g // 2, (g % 2) * COLS:(g % 2 + 1) * COLS],
                                       part((f_hi, f_lo), g, slice(tt_ * P, (tt_ + 1) * P)), (ch_hi[:, :], ch_lo[:, :]),
                                       True, True)
                    if g0 == 2:
                        last.then_inc(pr["y_full"], 1)
            between = {(0, 0): lambda: scores(main, 0, 0),
                       (0, 1): lambda: scores(main, 0, 1),
                       (0, 3): lambda: shift(main, 0),
                       (1, 0): lambda: scores(main, 1, 0),
                       (1, 2): lambda: scores(main, 1, 1)}
            for i in range(2):
                pe.wait_ge(w_lo_made, C_DFT + i + 1)
                for g in range(GROUPS):
                    for tt_ in range(4):
                        if i == 0:
                            pe.wait_ge(pr["out"], 9 + tt_ if g < 2 else 12)
                        s = slice(tt_ * TOKENS, (tt_ + 1) * TOKENS)
                        last = product(dft_pipes[g // 2][:, g % 2, :],
                                       part((y_hi, y_lo), tt_, slice(g * COLS + i * P, g * COLS + (i + 1) * P)),
                                       (w_hi[i][:, s], w_lo[i][:, s]), i == 0 and tt_ == 0, i == 1 and tt_ == 3)
                    if g == GROUPS - 1 and i == 0:
                        last.then_inc(chunk_used, 1)
                    if i == 1 and g % 2 == 1:
                        last.then_inc(pr["a_full"], 1)
                    if (i, g) in between:
                        between[i, g]()
            pe.drain().then_inc(chunk_used, 1)

            def fourier_branch(c, tiles=range(2)):
                pe.wait_ge(w_lo_made, c + 1)
                for t in tiles:
                    for k in range(GROUPS):
                        last = product(ps_a[:, t, :], weight(0, k, t), part((a_hi, a_lo), k), k == 0, k == GROUPS - 1)
                if tiles[-1] == 1:
                    last.then_inc(chunk_used, 1)

            def first_fourier_branch(t):
                pe.wait_ge(main.s["row_max"], 2 * N_HEADS)
                fourier_branch(C_BRANCH, range(t, t + 1))

            attention(main, {N_HEADS - 2 + t: functools.partial(first_fourier_branch, t) for t in range(2)})

            def branch(m, last_turn):
                c = C_BRANCH + 4 * m
                pe.wait_ge(w_lo_made, c + 2)
                pe.wait_ge(br["gf_out"], m + FREE)
                for t in range(2):
                    for k in range(D_TILES):
                        pe.wait_ge(br["x_lo"], k + 1)
                        last = product(ps_b[:, t, :], weight(1, k, t), part(x_parts, k), k == 0, k == D_TILES - 1)
                last.then_inc(chunk_used, 1)
                pe.wait_ge(br["ga_out"], m + FREE)
                project(0, ps_d, c + 2)
                pe.wait_ge(w_lo_made, c + 4)
                pe.wait_ge(br["ya"], m + FREE)
                for t in range(2):
                    for k in range(D_TILES):
                        pe.wait_ge(br["o_lo"], k // 4 + 1)
                        last = product(ps_c[:, t, :], weight(1, k, t), part((o_hi, o_lo), k), k == 0, k == D_TILES - 1)
                last.then_inc(chunk_used, 1)
                if not last_turn:
                    pe.wait_ge(br["yf"], m + 1 + FREE)
                    fourier_branch(c + 4)

            pe.wait_ge(main.s["p"], 2 * N_HEADS)
            with pe.Fori(0, PAIRS - 1) as m:
                branch(m, False)
            branch(PAIRS - 1, True)

            n = norms["cross"]
            pe.wait_ge(br["ga_out"], PAIRS + FREE)

            def out_pair(p, b):
                pe.wait_ge(w_lo_made, C_OUT + p + 1)
                for ks in (range(D_TILES - 2), range(D_TILES - 2, D_TILES)):
                    for m in range(2):
                        if ks[0] == 0 and p >= 2:
                            pe.wait_ge(*n.at(f"h_new{m}", p - 1))
                        if m == 0:
                            pe.wait_ge(br["m_lo"], PAIRS - (ks[0] == 0))
                        for k in ks:
                            last = product(out_pipes[b][:, m, :], weight(b, k, m), part((m_hi, m_lo), k),
                                           k == 0, k == D_TILES - 1)
                        if m == 0 and ks[0] > 0:
                            last.then_inc(n["tile0"], 1)
                last.then_inc(chunk_used, 1)

            out_pair(0, 0)
            pe.wait_ge(mm["sum"], 1)
            pe.wait_ge(br["yf"], PAIRS + FREE)
            nc.tensor.matmul(ps_a[:, 0, 0:MEM_LEN], ones[:, :], msum[:, :], start=True, stop=True)\
                .then_inc(mm["stat"], 1)
            for p in range(1, PAIRS):
                out_pair(p, p % 2)

            pe.wait_ge(mm["lo"], D_TILES)
            pe.wait_ge(w_lo_made, C_CK + 1)
            pe.wait_ge(mm["factor"], 1)
            for m in range(2):
                for k in range(D_TILES):
                    last = product(ps_a[:, m, 0:MEM_LEN], weight(0, k, m), part((mem_hi, mem_lo), k),
                                   k == 0, k == D_TILES - 1)
            last.then_inc(chunk_used, 1)
            pe.wait_ge(br["gf_out"], PAIRS + FREE)
            project_new(1, ps_b, C_CQ, n, sums_after=4)
            pe.wait_ge(w_lo_made, C_CV + 1)
            pe.wait_ge(br["ya"], PAIRS + FREE)

            def memory_values(mt):
                for k in range(D_TILES):
                    s = slice(k * COLS, (k + 1) * COLS)
                    last = product(ps_c[:, mt, 0:COLS], part((mem_hi, mem_lo), k, slice(mt * P, (mt + 1) * P)),
                                   (w_hi[0][:, s], w_lo[0][:, s]), k == 0, k == D_TILES - 1)
                return last

            memory_values(0)
            pe.wait_ge(cr["k_out"], 1)
            scores(cross, 0, 0)
            memory_values(1).then_inc(chunk_used, 1)
            shift(cross, 0)
            scores(cross, 1, 0)
            pe.wait_ge(cr["q_out"], 2)
            n = norms["ffn2"]

            def co(k, tiles):
                pe.wait_ge(cr["co_lo"], k + 1)
                for d in tiles:
                    last = product(co_banks[d], weight(1, k, d, D_MODEL), part((co_hi, co_lo), k), k == 0, k == 1)
                    if k == 1:
                        last.then_inc(cr["co_tile"], 1)

            def co_early():
                pe.wait_ge(w_lo_made, C_CO + 1)
                pe.wait_ge(cross.s["row_max"], N_CROSS)
                pe.wait_ge(cross.s["p"], N_CROSS - 1)
                co(0, range(4))

            attention(cross, {N_CROSS - 1: co_early})
            pe.wait_ge(cross.s["p"], N_CROSS)
            co(0, range(4, 6))
            pe.wait_ge(cross.s["o"], N_CROSS)
            co(0, range(6, D_TILES))
            co(1, range(D_TILES))
            pe.drain().then_inc(chunk_used, 1)
            pe.wait_ge(*n.at("h_new1", 1))
            ffn("ffn2", "final", C_FFN2)
            n = norms["final"]
            pe.wait_ge(*n.at("summed", D_TILES))
            nc.tensor.matmul(stat, ones[:, :], square_sum[:, :], start=True, stop=False)
            pe.wait_ge(*n.at("squared", D_TILES))
            nc.tensor.matmul(stat, ones[:, :], squares[1][:, :], start=False, stop=True).then_inc(n["stat"], 1)


def column_chunks(w):
    K, N = w.shape
    return w.reshape(K // P, P, N // COLS, COLS).transpose(2, 1, 0, 3).reshape(N // COLS, P, K // P * COLS)


def down_chunks(w):
    return [c[:, f * COLS:(f + k) * COLS] for c in column_chunks(w) for f, k in zip(DOWN_FIRST, DOWN_SPLIT)]


def weight_stream(a):
    def gate_up(gate, up):
        return [c for pair in zip(column_chunks(gate), column_chunks(up)) for c in pair]

    q_w, kv_w, f_w = N_HEADS * HEAD_DIM, N_KV * HEAD_DIM, GROUPS * P
    w_in = a["w_in"][0]
    edges = np.cumsum([0, q_w, kv_w, kv_w, f_w, D_MODEL, D_MODEL])
    q, k, v, f, gate_f, gate_a = (column_chunks(w_in[:, s:e]) for s, e in zip(edges[:-1], edges[1:]))
    t = np.arange(TOKENS)
    angle = 2 * np.pi * (np.outer(t, t) % TOKENS) / TOKENS
    dft = [np.cos(angle), -np.sin(angle)]
    dft = [m.astype(np.float32).reshape(4, P, TOKENS).transpose(1, 0, 2).reshape(P, CHUNK) for m in dft]
    branches = zip(column_chunks(a["w_fourier_branch"][0]), gate_f, gate_a, column_chunks(a["w_attn_branch"][0]))
    w_co = a["w_co"][0].reshape(2, P, D_MODEL).transpose(1, 0, 2).reshape(P, CHUNK)
    chunks = [*gate_up(a["w1_gate"][0], a["w1_up"][0]), *down_chunks(a["w1_down"][0]),
              *k, *v, *q, *f, *dft,
              *(c for four in branches for c in four), *column_chunks(a["w_out"][0]),
              *column_chunks(a["w_ck"][0]), *column_chunks(a["w_cq"][0]), *column_chunks(a["w_cv"][0]), w_co,
              *gate_up(a["w2_gate"][0], a["w2_up"][0]), *down_chunks(a["w2_down"][0])]
    out = np.zeros((N_CHUNKS, P, CHUNK), np.float32)
    assert len(chunks) == N_CHUNKS
    for n, c in enumerate(chunks):
        out[n, :, :c.shape[1]] = c
    return out


def feature_tiles(x):
    return np.ascontiguousarray(x.reshape(x.shape[0], -1, P).transpose(2, 1, 0))


def rope_tables():
    f32 = np.float32
    t = np.arange(TOKENS)
    inv = f32(1.0) / (f32(10000.0) ** (np.arange(0, 32, 2, dtype=f32) / f32(32)))
    d = np.arange(P) % HEAD_DIM
    position = np.where((d < 32)[:, None], (t // 64)[None, :], (t % 64)[None, :]).astype(f32)
    angle = position * inv[d % 16][:, None]
    sign = np.where(d % 32 < 16, -1.0, 1.0)[:, None]
    return np.stack([np.cos(angle), sign * np.sin(angle)]).astype(f32)


def kernel(**inputs):
    import concourse.bacc as _bacc
    from concourse.bass_utils import run_bass_kernel_spmd as _run

    a = {name: np.asarray(value) for name, value in inputs.items()}
    gains = np.stack([a["g_ffn1"][0], a["g_mix"][0], a["g_cross"][0], a["g_ffn2"][0], a["g_final"], a["g_mem"][0]])
    heads = np.stack([a["k_gain"][0]] + [a["q_gain"][0]] * 7, axis=1)
    c = np.arange(P)
    angle = 2 * np.pi * (np.outer(c, c) % P) / P
    channel = np.concatenate([np.cos(angle), np.sin(angle)], axis=1) / np.sqrt(TOKENS * P)
    arrays = {
        "xT": feature_tiles(a["x"][0]),
        "memT": feature_tiles(a["mem"][0]),
        "stream": weight_stream(a),
        "gains": np.ascontiguousarray(gains.reshape(6, D_TILES, P).transpose(2, 0, 1)),
        "head_gains": np.ascontiguousarray(np.concatenate([heads, heads])),
        "rope": rope_tables(),
        "channel_dft": channel.astype(np.float32),
        "identity": np.eye(P, dtype=np.float32),
    }
    nc = _bacc.Bacc("TRN2", target_bir_lowering=False, num_devices=1)
    args = [nc.dram_tensor(name, x.shape, F32, kind="ExternalInput").ap() for name, x in arrays.items()]
    out = nc.dram_tensor("outT", (P, D_TILES, TOKENS), F32, kind="ExternalOutput").ap()
    encoder_block(nc, *args, out)
    r = _run(nc, [arrays], core_ids=[0])
    outT = r.results[0]["outT"]
    return outT.transpose(2, 1, 0).reshape(1, TOKENS, D_MODEL)
```
